# Optimizing a Trainium2 kernel written in Bass

```python
import jax, jax.numpy as jnp
from jax import lax
import numpy as np

D_MODEL = 2048
BATCH = 1
SEQ = 256
DEPTH = 1

CHUNK = 64
HEAD_DIM = 128
N_HEADS_SB = 8
N_HEADS_CA = 8
W_SB = N_HEADS_SB * HEAD_DIM
W_CA = N_HEADS_CA * HEAD_DIM
LEFT_CHUNKS = 8
BAND = (LEFT_CHUNKS + 1) * CHUNK
REL_CLIP = 128
N_REL = REL_CLIP + CHUNK
Q_BLOCK = 128
D_FF = -(-8 * D_MODEL // (3 * 256)) * 256
D_PLE = 256
EPS = 1e-6
NEG = -1e30
IN_COLS = 3 * W_SB + 3 * W_CA + 2 * D_MODEL


def rmsnorm(x, g):
    xf = x.astype(jnp.float32)
    y = xf * lax.rsqrt(jnp.mean(xf * xf, axis=-1, keepdims=True) + EPS)
    return (y * g.astype(jnp.float32)).astype(x.dtype)

def stick_breaking_attention(q, k, v):
    B, S, H, Dh = q.shape
    scale = Dh ** -0.5
    outs = []
    for qb in range(S // Q_BLOCK):
        t0 = qb * Q_BLOCK
        t1 = t0 + Q_BLOCK
        kb = k[:, :t1]
        vb = v[:, :t1]
        z = jnp.einsum('bqhd,bkhd->bhqk', q[:, t0:t1], kb).astype(jnp.float32) * scale
        past = jnp.arange(t1)[None, :] < jnp.arange(t0, t1)[:, None]
        log_keep = jnp.where(past, jax.nn.log_sigmoid(-z), 0.0)
        between = lax.cumsum(log_keep, axis=3, reverse=True) - log_keep
        a = jnp.where(past, jnp.exp(jax.nn.log_sigmoid(z) + between), 0.0)
        outs.append(jnp.einsum('bhqk,bkhd->bqhd', a.astype(v.dtype), vb))
    return jnp.concatenate(outs, axis=1)

def chunked_relpos_attention(q, k, v, rel_bias):
    B, S, H, Dh = q.shape
    nc = S // CHUNK
    pad = LEFT_CHUNKS * CHUNK
    scale = Dh ** -0.5
    kp = jnp.pad(k, ((0, 0), (pad, 0), (0, 0), (0, 0)))
    vp = jnp.pad(v, ((0, 0), (pad, 0), (0, 0), (0, 0)))
    qc = jnp.moveaxis(q.reshape(B, nc, CHUNK, H, Dh), 1, 0)
    s_loc = jnp.arange(BAND)[None, :]
    rel = s_loc - (jnp.arange(CHUNK)[:, None] + pad)
    rel_idx = jnp.clip(rel, -REL_CLIP, CHUNK - 1) + REL_CLIP
    bias = rel_bias.astype(jnp.float32)[:, rel_idx]

    def one_chunk(args):
        c, qblk = args
        start = c * CHUNK
        kb = lax.dynamic_slice_in_dim(kp, start, BAND, axis=1)
        vb = lax.dynamic_slice_in_dim(vp, start, BAND, axis=1)
        valid = (start + s_loc) >= pad
        z = jnp.einsum('bqhd,bkhd->bhqk', qblk, kb).astype(jnp.float32) * scale + bias
        w = jax.nn.softmax(jnp.where(valid, z, NEG), axis=-1)
        return jnp.einsum('bhqk,bkhd->bqhd', w.astype(v.dtype), vb)

    out = lax.map(one_chunk, (jnp.arange(nc), qc))
    return jnp.moveaxis(out, 0, 1).reshape(B, S, H, Dh)

def first_inputs(seed: int = 0) -> dict:
    key = jax.random.key(seed)
    ks = jax.random.split(key, 16)
    f32 = jnp.float32

    def w(k, shape, fan_in):
        return jax.random.normal(k, shape, f32) * fan_in ** -0.5

    def gain(k, shape):
        return 1.0 + 0.05 * jax.random.normal(k, shape, f32)

    return {
        "x": jax.random.normal(ks[0], (BATCH, SEQ, D_MODEL), f32),
        "p": jax.random.normal(ks[1], (DEPTH, BATCH, SEQ, D_PLE), f32),
        "w_in": w(ks[2], (DEPTH, D_MODEL, IN_COLS), D_MODEL),
        "w_sb_out": w(ks[3], (DEPTH, W_SB, D_MODEL), W_SB),
        "w_ca_out": w(ks[4], (DEPTH, W_CA, D_MODEL), W_CA),
        "w_mix_out": w(ks[5], (DEPTH, D_MODEL, D_MODEL), D_MODEL),
        "rel_bias": 0.3 * jax.random.normal(ks[6], (DEPTH, N_HEADS_CA, N_REL), f32),
        "g_mix": gain(ks[7], (DEPTH, D_MODEL)),
        "g_ffn": gain(ks[8], (DEPTH, D_MODEL)),
        "g_ple": gain(ks[9], (DEPTH, D_MODEL)),
        "g_final": gain(ks[10], (D_MODEL,)),
        "w_ffn_in": w(ks[11], (DEPTH, D_MODEL, 2 * D_FF), D_MODEL),
        "w_ffn_out": w(ks[12], (DEPTH, D_FF, D_MODEL), D_FF),
        "w_ple_in": w(ks[13], (DEPTH, D_PLE, D_MODEL), D_PLE),
        "w_ple_gate": w(ks[14], (DEPTH, D_MODEL, D_MODEL), D_MODEL),
    }

def first_block(x, p, w_in, w_sb_out, w_ca_out, w_mix_out, rel_bias, g_mix, g_ffn, g_ple, g_final,
              w_ffn_in, w_ffn_out, w_ple_in, w_ple_gate):
    B, S, _ = x.shape
    splits = [W_SB, 2 * W_SB, 3 * W_SB, 3 * W_SB + W_CA, 3 * W_SB + 2 * W_CA, 3 * W_SB + 3 * W_CA,
              3 * W_SB + 3 * W_CA + D_MODEL]
    for i in range(DEPTH):
        h = rmsnorm(x, g_mix[i])
        proj = h @ w_in[i]
        q_sb, k_sb, v_sb, q_ca, k_ca, v_ca, gate_sb, gate_ca = jnp.split(proj, splits, axis=-1)
        y_sb = stick_breaking_attention(q_sb.reshape(B, S, N_HEADS_SB, HEAD_DIM),
                                        k_sb.reshape(B, S, N_HEADS_SB, HEAD_DIM),
                                        v_sb.reshape(B, S, N_HEADS_SB, HEAD_DIM)).reshape(B, S, W_SB)
        y_ca = chunked_relpos_attention(q_ca.reshape(B, S, N_HEADS_CA, HEAD_DIM),
                                        k_ca.reshape(B, S, N_HEADS_CA, HEAD_DIM),
                                        v_ca.reshape(B, S, N_HEADS_CA, HEAD_DIM),
                                        rel_bias[i]).reshape(B, S, W_CA)
        merged = (jax.nn.sigmoid(gate_sb) * (y_sb @ w_sb_out[i])
                  + jax.nn.sigmoid(gate_ca) * (y_ca @ w_ca_out[i]))
        x = x + merged @ w_mix_out[i]
        h = rmsnorm(x, g_ffn[i])
        g_ff, u_ff = jnp.split(h @ w_ffn_in[i], 2, axis=-1)
        x = x + (jax.nn.silu(g_ff) * u_ff) @ w_ffn_out[i]
        h = rmsnorm(x, g_ple[i])
        x = x + jax.nn.sigmoid(h @ w_ple_gate[i]) * (p[i] @ w_ple_in[i])
    return rmsnorm(x, g_final)


DEPTH_2 = 2

N_MEM = 256

SC_WIDTH = 1024
SC_KERNEL = 3

SSD_HEADS = 32
SSD_HEAD_DIM = 64
SSD_WIDTH = SSD_HEADS * SSD_HEAD_DIM
SSD_STATE = 128
SSD_GROUPS = 4
SSD_CONV = 4
SSD_CHUNK = 128
SSD_CONV_DIM = SSD_WIDTH + 2 * SSD_GROUPS * SSD_STATE
DT_MIN = 0.001
DT_MAX = 0.1

MLA_HEADS = 16
MLA_Q_RANK = 768
MLA_KV_RANK = 512
MLA_NOPE = 128
MLA_ROPE = 64
MLA_V = 128
MLA_WIDTH = MLA_HEADS * MLA_V
ROPE_THETA = 10000.0

MEM_HEADS = 4
MEM_HEAD_DIM = 128
MEM_WIDTH = MEM_HEADS * MEM_HEAD_DIM

EVEN_SPLITS = (SC_WIDTH, SC_WIDTH, SC_WIDTH, SC_WIDTH,
               SSD_WIDTH, SSD_CONV_DIM, SSD_HEADS, MEM_WIDTH, MEM_WIDTH)
EVEN_IN = sum(EVEN_SPLITS)
EVEN_OUT = SC_WIDTH + SSD_WIDTH + MEM_WIDTH
ODD_SPLITS = (MLA_Q_RANK, MLA_KV_RANK, MLA_ROPE, MLA_WIDTH, MEM_WIDTH, MEM_WIDTH)
ODD_IN = sum(ODD_SPLITS)
ODD_OUT = MLA_WIDTH + MEM_WIDTH


def _split(t, sizes):
    idx = [int(i) for i in np.cumsum(sizes)[:-1]]
    return jnp.split(t, idx, axis=-1)

def rms_norm(x, w):
    xf = x.astype(jnp.float32)
    y = xf * lax.rsqrt(jnp.mean(xf * xf, axis=-1, keepdims=True) + EPS)
    return (y * w.astype(jnp.float32)).astype(x.dtype)

def causal_depthwise_conv(u, w):
    k_w, c = w.shape
    return lax.conv_general_dilated(
        u, w.reshape(k_w, 1, c).astype(u.dtype), window_strides=(1,),
        padding=[(k_w - 1, 0)], dimension_numbers=("NWC", "WIO", "NWC"),
        feature_group_count=c)

def rope(t, pos):
    half = MLA_ROPE // 2
    inv = ROPE_THETA ** (-jnp.arange(half, dtype=jnp.float32) / half)
    ang = pos.astype(jnp.float32)[..., None] * inv
    cos = jnp.cos(ang)[:, :, None, :]
    sin = jnp.sin(ang)[:, :, None, :]
    t1 = t[..., :half].astype(jnp.float32)
    t2 = t[..., half:].astype(jnp.float32)
    return jnp.concatenate([t1 * cos - t2 * sin, t1 * sin + t2 * cos], axis=-1).astype(t.dtype)

def memory_attention(q, mem_n, w_mk, w_mv):
    b_, l_, _ = q.shape
    qh = q.reshape(b_, l_, MEM_HEADS, MEM_HEAD_DIM)
    k = (mem_n @ w_mk).reshape(b_, -1, MEM_HEADS, MEM_HEAD_DIM)
    v = (mem_n @ w_mv).reshape(b_, -1, MEM_HEADS, MEM_HEAD_DIM)
    s = jnp.einsum('bqhd,bkhd->bhqk', qh, k).astype(jnp.float32) * (MEM_HEAD_DIM ** -0.5)
    p = jax.nn.softmax(s, axis=-1).astype(v.dtype)
    o = jnp.einsum('bhqk,bkhd->bqhd', p, v)
    return o.reshape(b_, l_, MEM_WIDTH)

def ssd_chunked(xs, dt, a, bm, cm):
    b_, l_, h_, p_ = xs.shape
    nc = l_ // SSD_CHUNK
    hpg = h_ // SSD_GROUPS
    xdt = (xs * dt[..., None]).reshape(b_, nc, SSD_CHUNK, SSD_GROUPS, hpg, p_)
    bm = bm.reshape(b_, nc, SSD_CHUNK, SSD_GROUPS, SSD_STATE)
    cm = cm.reshape(b_, nc, SSD_CHUNK, SSD_GROUPS, SSD_STATE)
    a_cum = jnp.cumsum((dt * a).reshape(b_, nc, SSD_CHUNK, SSD_GROUPS, hpg), axis=2)
    seg = a_cum[:, :, :, None] - a_cum[:, :, None, :]
    causal = (jnp.arange(SSD_CHUNK)[:, None] >= jnp.arange(SSD_CHUNK)[None, :])[:, :, None, None]
    decay = jnp.exp(jnp.where(causal, seg, -jnp.inf))
    cb = jnp.einsum('bcqgn,bckgn->bcqkg', cm, bm)
    y_diag = jnp.einsum('bcqkg,bcqkgh,bckghp->bcqghp', cb, decay, xdt)
    decay_to_end = jnp.exp(a_cum[:, :, -1:] - a_cum)
    states = jnp.einsum('bckgn,bckgh,bckghp->bcghpn', bm, decay_to_end, xdt)
    chunk_decay = jnp.exp(a_cum[:, :, -1])

    def step(s, inp):
        st, dec = inp
        return s * dec[..., None, None] + st, s

    init = jnp.zeros((b_, SSD_GROUPS, hpg, p_, SSD_STATE), jnp.float32)
    _, s_enter = lax.scan(step, init, (jnp.moveaxis(states, 1, 0), jnp.moveaxis(chunk_decay, 1, 0)))
    s_enter = jnp.moveaxis(s_enter, 0, 1)
    y_off = jnp.einsum('bcqgn,bcghpn,bcqgh->bcqghp', cm, s_enter, jnp.exp(a_cum))
    return (y_diag + y_off).reshape(b_, l_, h_, p_)

def causal_block_attention(q, k, v):
    b_, l_, h_, dk = q.shape
    nb = l_ // Q_BLOCK
    scale = dk ** -0.5
    qb = jnp.moveaxis(q.reshape(b_, nb, Q_BLOCK, h_, dk), 1, 0)
    k_pos = jnp.arange(l_)

    def one_block(args):
        q_blk, i = args
        s = jnp.einsum('bqhd,bkhd->bhqk', q_blk, k).astype(jnp.float32) * scale
        q_pos = i * Q_BLOCK + jnp.arange(Q_BLOCK)
        s = jnp.where(k_pos[None, :] <= q_pos[:, None], s, -jnp.inf)
        p = jax.nn.softmax(s, axis=-1).astype(v.dtype)
        return jnp.einsum('bhqk,bkhv->bqhv', p, v)

    o = lax.map(one_block, (qb, jnp.arange(nb)))
    return jnp.moveaxis(o, 0, 1).reshape(b_, l_, h_ * v.shape[-1])

def even_layer(x, mem_n, norm_w, w_in, sc_conv_w, ssd_conv_w, ssd_conv_b, ssd_dt_bias,
               ssd_a_log, ssd_d, ssd_norm_w, w_mk, w_mv, w_out):
    b_, l_, _ = x.shape
    h = rms_norm(x, norm_w)
    proj = h @ w_in
    sc_b, sc_c, sc_v, sc_z, ssd_z, ssd_xbc, ssd_dt, mq, mz = _split(proj, EVEN_SPLITS)
    y_a = sc_b * causal_depthwise_conv(sc_c * sc_v, sc_conv_w)
    y_a = y_a * jax.nn.silu(sc_z)
    xbc = jax.nn.silu(causal_depthwise_conv(ssd_xbc, ssd_conv_w) + ssd_conv_b)
    xs, bm, cm = _split(xbc, (SSD_WIDTH, SSD_GROUPS * SSD_STATE, SSD_GROUPS * SSD_STATE))
    xs = xs.reshape(b_, l_, SSD_HEADS, SSD_HEAD_DIM).astype(jnp.float32)
    bm = bm.reshape(b_, l_, SSD_GROUPS, SSD_STATE).astype(jnp.float32)
    cm = cm.reshape(b_, l_, SSD_GROUPS, SSD_STATE).astype(jnp.float32)
    dt = jax.nn.softplus(ssd_dt.astype(jnp.float32) + ssd_dt_bias.astype(jnp.float32))
    a = -jnp.exp(ssd_a_log.astype(jnp.float32))
    y_b = ssd_chunked(xs, dt, a, bm, cm) + xs * ssd_d.astype(jnp.float32)[:, None]
    y_b = y_b.reshape(b_, l_, SSD_WIDTH) * jax.nn.silu(ssd_z.astype(jnp.float32))
    y_b = y_b.reshape(b_, l_, SSD_GROUPS, SSD_WIDTH // SSD_GROUPS)
    y_b = y_b * lax.rsqrt(jnp.mean(y_b * y_b, axis=-1, keepdims=True) + EPS)
    y_b = (y_b.reshape(b_, l_, SSD_WIDTH) * ssd_norm_w.astype(jnp.float32)).astype(x.dtype)
    y_m = memory_attention(mq, mem_n, w_mk, w_mv) * jax.nn.silu(mz)
    return x + jnp.concatenate([y_a, y_b, y_m], axis=-1) @ w_out

def odd_layer(x, mem_n, positions, norm_w, w_in, mla_q_norm_w, mla_kv_norm_w, mla_w_uq,
              mla_w_ukv, w_mk, w_mv, w_out):
    b_, l_, _ = x.shape
    h = rms_norm(x, norm_w)
    proj = h @ w_in
    c_q, c_kv, k_r, z_c, mq, mz = _split(proj, ODD_SPLITS)
    q = (rms_norm(c_q, mla_q_norm_w) @ mla_w_uq).reshape(b_, l_, MLA_HEADS, MLA_NOPE + MLA_ROPE)
    kv = (rms_norm(c_kv, mla_kv_norm_w) @ mla_w_ukv).reshape(b_, l_, MLA_HEADS, MLA_NOPE + MLA_V)
    q_nope, q_rope = q[..., :MLA_NOPE], rope(q[..., MLA_NOPE:], positions)
    k_nope, v = kv[..., :MLA_NOPE], kv[..., MLA_NOPE:]
    k_rope = jnp.broadcast_to(rope(k_r[:, :, None, :], positions), (b_, l_, MLA_HEADS, MLA_ROPE))
    q_full = jnp.concatenate([q_nope, q_rope], axis=-1)
    k_full = jnp.concatenate([k_nope, k_rope], axis=-1)
    y_c = causal_block_attention(q_full, k_full, v) * jax.nn.silu(z_c)
    y_m = memory_attention(mq, mem_n, w_mk, w_mv) * jax.nn.silu(mz)
    return x + jnp.concatenate([y_c, y_m], axis=-1) @ w_out

def second_inputs(seed: int = 0) -> dict:
    key = jax.random.key(seed)
    ks = jax.random.split(key, 32)
    f32 = jnp.float32

    def dense(k, fan_in, fan_out):
        return jax.random.normal(k, (fan_in, fan_out), f32) * fan_in ** -0.5

    def gain(k, n):
        return 1.0 + 0.05 * jax.random.normal(k, (n,), f32)

    x = jax.random.normal(ks[0], (BATCH, SEQ, D_MODEL), f32)
    mem = jax.random.normal(ks[1], (BATCH, N_MEM, D_MODEL), f32)
    offsets = jax.random.randint(ks[2], (BATCH, 1), 0, 4096, dtype=jnp.int32)
    positions = offsets + jnp.arange(SEQ, dtype=jnp.int32)[None, :]
    dt0 = jnp.exp(jax.random.uniform(ks[3], (SSD_HEADS,), f32) * (np.log(DT_MAX) - np.log(DT_MIN)) + np.log(DT_MIN))
    return {
        "x": x,
        "mem": mem,
        "positions": positions,
        "mem_norm_w": gain(ks[4], D_MODEL),
        "norm0_w": gain(ks[5], D_MODEL),
        "w_in0": dense(ks[6], D_MODEL, EVEN_IN),
        "sc_conv_w": jax.random.normal(ks[7], (SC_KERNEL, SC_WIDTH), f32) * SC_KERNEL ** -0.5,
        "ssd_conv_w": jax.random.normal(ks[8], (SSD_CONV, SSD_CONV_DIM), f32) * SSD_CONV ** -0.5,
        "ssd_conv_b": 0.01 * jax.random.normal(ks[9], (SSD_CONV_DIM,), f32),
        "ssd_dt_bias": dt0 + jnp.log(-jnp.expm1(-dt0)),
        "ssd_a_log": jnp.log(jax.random.uniform(ks[10], (SSD_HEADS,), f32, 1.0, 16.0)),
        "ssd_d": 1.0 + 0.1 * jax.random.normal(ks[11], (SSD_HEADS,), f32),
        "ssd_norm_w": gain(ks[12], SSD_WIDTH),
        "mem_k0": dense(ks[13], D_MODEL, MEM_WIDTH),
        "mem_v0": dense(ks[14], D_MODEL, MEM_WIDTH),
        "w_out0": dense(ks[15], EVEN_OUT, D_MODEL),
        "norm1_w": gain(ks[16], D_MODEL),
        "w_in1": dense(ks[17], D_MODEL, ODD_IN),
        "mla_q_norm_w": gain(ks[18], MLA_Q_RANK),
        "mla_kv_norm_w": gain(ks[19], MLA_KV_RANK),
        "mla_w_uq": dense(ks[20], MLA_Q_RANK, MLA_HEADS * (MLA_NOPE + MLA_ROPE)),
        "mla_w_ukv": dense(ks[21], MLA_KV_RANK, MLA_HEADS * (MLA_NOPE + MLA_V)),
        "mem_k1": dense(ks[22], D_MODEL, MEM_WIDTH),
        "mem_v1": dense(ks[23], D_MODEL, MEM_WIDTH),
        "w_out1": dense(ks[24], ODD_OUT, D_MODEL),
        "final_norm_w": gain(ks[25], D_MODEL),
    }

def second_block(x, mem, positions, mem_norm_w, norm0_w, w_in0, sc_conv_w, ssd_conv_w, ssd_conv_b,
              ssd_dt_bias, ssd_a_log, ssd_d, ssd_norm_w, mem_k0, mem_v0, w_out0, norm1_w, w_in1,
              mla_q_norm_w, mla_kv_norm_w, mla_w_uq, mla_w_ukv, mem_k1, mem_v1, w_out1, final_norm_w):
    mem_n = rms_norm(mem, mem_norm_w)
    even_params = (norm0_w, w_in0, sc_conv_w, ssd_conv_w, ssd_conv_b, ssd_dt_bias, ssd_a_log,
                   ssd_d, ssd_norm_w, mem_k0, mem_v0, w_out0)
    odd_params = (norm1_w, w_in1, mla_q_norm_w, mla_kv_norm_w, mla_w_uq, mla_w_ukv,
                  mem_k1, mem_v1, w_out1)
    layer_params = [even_params, odd_params]
    for layer in range(DEPTH_2):
        if layer % 2 == 0:
            x = even_layer(x, mem_n, *layer_params[layer])
        else:
            x = odd_layer(x, mem_n, positions, *layer_params[layer])
    return rms_norm(x, final_norm_w)


def setup_inputs(seed=0):
    out = dict(first_inputs(seed))
    for name, value in second_inputs(seed + 1).items():
        if name != "x":
            out[name + "_2"] = value
    return out


def reference(
    x, p, w_in, w_sb_out, w_ca_out, w_mix_out, rel_bias, g_mix, g_ffn, g_ple, g_final, w_ffn_in,
    w_ffn_out, w_ple_in, w_ple_gate, mem_2, positions_2, mem_norm_w_2, norm0_w_2, w_in0_2,
    sc_conv_w_2, ssd_conv_w_2, ssd_conv_b_2, ssd_dt_bias_2, ssd_a_log_2, ssd_d_2, ssd_norm_w_2,
    mem_k0_2, mem_v0_2, w_out0_2, norm1_w_2, w_in1_2, mla_q_norm_w_2, mla_kv_norm_w_2,
    mla_w_uq_2, mla_w_ukv_2, mem_k1_2, mem_v1_2, w_out1_2, final_norm_w_2,
):
    x = first_block(
        x, p, w_in, w_sb_out, w_ca_out, w_mix_out, rel_bias, g_mix, g_ffn, g_ple, g_final,
        w_ffn_in, w_ffn_out, w_ple_in, w_ple_gate,
    )
    return second_block(
        x, mem_2, positions_2, mem_norm_w_2, norm0_w_2, w_in0_2, sc_conv_w_2, ssd_conv_w_2,
        ssd_conv_b_2, ssd_dt_bias_2, ssd_a_log_2, ssd_d_2, ssd_norm_w_2, mem_k0_2, mem_v0_2,
        w_out0_2, norm1_w_2, w_in1_2, mla_q_norm_w_2, mla_kv_norm_w_2, mla_w_uq_2, mla_w_ukv_2,
        mem_k1_2, mem_v1_2, w_out1_2, final_norm_w_2,
    )


_drawn_inputs = setup_inputs


def setup_inputs(seed=0):
    import zlib

    import numpy as np

    out = dict(_drawn_inputs(seed))
    spreads = {}
    factors = {'g_ple': 5.52,
     'mem_norm_w_2': 8.0,
     'ssd_conv_b_2': 6.653,
     'mem_k0_2': 3.869,
     'mem_v0_2': 3.078,
     'norm1_w_2': 6.241,
     'mla_q_norm_w_2': 8.0,
     'mla_kv_norm_w_2': 8.0,
     'mem_k1_2': 3.312}
    for name, (base, spread) in spreads.items():
        noise = np.random.default_rng([zlib.crc32(name.encode()), seed]).standard_normal(out[name].shape)
        drawn = base * np.exp(spread * noise) if base else spread * noise
        out[name] = __import__('jax').numpy.asarray(drawn.astype(out[name].dtype))
    for name, factor in factors.items():
        out[name] = (out[name] * factor).astype(out[name].dtype)
    return out
```

```python
from contextlib import ExitStack

import numpy as np
import concourse.bass as bass
from concourse import mybir

F32 = mybir.dt.float32
F32R = mybir.dt.float32r
I32 = mybir.dt.int32
ALU = mybir.AluOpType
ACT = mybir.ActivationFunctionType
AX = mybir.AxisListType

P = 128
TOK = 256
TH = TOK // P
D = 2048
NBW = 512
UCH = 2
UW = UCH * NBW
RING = 4
LEAD = 3
D_FF = 5632
HD = 128
NEG = -1e30
EPS = 1e-6
SCALE = float(HD) ** -0.5
W_IN1 = 10240
EVW = 10272
REL_CLIP, CHUNK = 128, 64
N_REL = REL_CLIP + CHUNK
OLW = 448
L_SCALE = 192 ** -0.5
GATED = 13
PI = float(np.pi)
PI_IN = 3.1415925
TWO_PI = (6.28125, 0.0019350051879882812, 3.019916050561733e-07)
ROUND = 12582912.0

STAGES = [
    ("mem", 4, 8), ("win", 20, 8), ("out", 8, 4), ("mix", 4, 8), ("ffn", 22, 8),
    ("ffo", 4, 22), ("ple", 4, 1), ("gate", 4, 8),
    ("ein", 12, 8), ("dt", 0, 1), ("sc", 8, 8), ("eout", 4, 14),
    ("olow", 3, 8), ("omem", 2, 8), ("uq", 6, 3), ("ukv", 8, 2), ("zc", 4, 8), ("oout", 4, 10),
]
U0, B0 = {}, {}
_u = _b = 0
for _n, _nb, _ub in STAGES:
    U0[_n], B0[_n] = _u, _b
    _u += (_nb or 1) * _ub
    _b += _nb
N_UNITS = _u + LEAD


class At:

    def __init__(self, k, i=0, per=0):
        self.k, self.i, self.per = k, i, per

    def __add__(self, n):
        return At(self.k + n, self.i, self.per)

    def times(self, n, plus=0):
        if isinstance(self.i, int):
            return n * (self.k + self.i * self.per) + plus
        return self.i * (n * self.per) + (n * self.k + plus)

    @property
    def slot(self):
        return self.k % RING

    def landed(self):
        if isinstance(self.i, int):
            return 16 * ((self.k + self.i * self.per) // RING + 1)
        return self.i * (16 * self.per // RING) + 16 * (self.k // RING + 1)


def build(nc, io):
    ctx = ExitStack()
    with ctx:
        program(nc, io, ctx)


def program(nc, io, ctx):
    stream = io["stream"]
    base = (nc.sbuf_base + 63) // 64 * 64

    def place(name, shape, dt, at):
        return nc.alloc_sbuf_tensor_at(name, shape, dt, offset=base + at)

    def sem(name):
        return ctx.enter_context(nc.semaphore(name))

    def dram(name, shape):
        return nc.dram_tensor(name, shape, F32, kind="Internal").ap()

    K = 1024
    raw = place("raw", [P, RING, UW], F32, 0)
    w_hi = place("w_hi", [P, RING, UW], F32R, 16 * K)
    w_lo = place("w_lo", [P, RING, UW], F32R, 32 * K)
    AT, WD = 48 * K, 80 * K

    def pair(name, chunks, at):
        size = chunks * TOK * 4
        return (place(name + "_hi", [P, chunks, TOK], F32R, at),
                place(name + "_lo", [P, chunks, TOK], F32R, at + size))

    x_t = pair("x_t", 16, AT)
    mem_t = pair("mem_t", 16, WD)
    y_t = pair("y_t", 16, WD)
    m_t = pair("m_t", 16, WD + 32 * K)
    ff_t = pair("ff_t", 44, WD)
    ple_t = pair("ple_t", 2, WD + 32 * K)
    x3_t = pair("x3_t", 16, WD)
    END = WD + 88 * K
    tile = [place(f"tile{s}", [P, TH, NBW], F32, END + 4 * K * s) for s in range(2)]
    xin = [place(f"xin{s}", [P, TH, NBW], F32, END + 8 * K + 4 * K * s) for s in range(2)]
    junk = place("junk", [P, TH * NBW], F32, END + 16 * K)
    ident = place("ident", [P, P], F32, END + 20 * K)
    gain = place("gain", [P, P], F32, END + 20 * K + 512)
    past = place("past", [P, 3 * P], F32, END + 21 * K)
    stat = place("stat", [P, 64], F32, END + 23 * K)
    rstd = place("rstd", [P, 64], F32, END + 23 * K + 256)
    expo = place("expo", [P, 2], F32, END + 23 * K + 512)
    total = place("total", [P, 32], F32, END + 23 * K + 576)
    mean = place("mean", [P, 32], F32, END + 23 * K + 704)
    T0 = WD + 32 * K
    qkv = [place(f"qkv{s}", [P, TH, 3, HD], F32, T0 + 3 * K * s if s < 2 else WD + 76 * K + 3 * K * (s - 2))
           for s in range(4)]
    qk_t = [place(f"qk_t{s}", [P, 2 * TOK], F32, T0 + 6 * K + 2 * K * s) for s in range(2)]
    H3 = 3 * P
    kinds = ("sb", "ca")
    z = {k: place(f"z_{k}", [P, H3], F32, T0 + 10 * K + 1536 * n) for n, k in enumerate(kinds)}
    prob = {k: place(f"prob_{k}", [P, H3], F32, T0 + 13 * K + 1536 * n) for n, k in enumerate(kinds)}
    keep = place("keep", [P, H3], F32, T0 + 16 * K)
    drop = place("drop", [P, H3], F32, T0 + 18 * K)
    left = place("left", [P, H3], F32, T0 + 20 * K)
    p_t = [place(f"p_t{s}", [P, H3], F32, T0 + 22 * K + 1536 * s) for s in range(2)]
    sm = place("sm", [P, 8], F32, T0 + 29 * K)
    e_rows = place("e_rows", [8, H3], F32, T0 + 30 * K)
    bias = place("bias", [P, 8, H3], F32, T0 + 32 * K)
    gates = [place(f"gates{s}", [P, 2, TH, NBW], F32, WD + 64 * K + 8 * K * s) for s in range(2)]
    part = place("part", [P, 2, TH, NBW], F32, WD + 80 * K)
    g_half = place("g_half", [P, TH, NBW], F32, END + 8 * K)
    g_sig = place("g_sig", [P, TH, NBW], F32, END + 12 * K)
    pl_row = place("pl_row", [P, TH, TOK], F32, WD + 37 * K)
    pl_out = place("pl_out", [P, 4, TH, NBW], F32, WD + 40 * K)
    gf_row = place("gf_row", [P, D], F32, WD + 56 * K)
    pl_sig = place("pl_sig", [P, TH, NBW], F32, WD + 64 * K)
    x_raw = place("x_raw", [P, TH, NBW], F32, WD + 68 * K)

    z_t = pair("z_t", 28, WD + 32 * K)
    lat_t = pair("lat_t", 10, WD)
    o_t = pair("o_t", 20, WD + 20 * K)

    def row_of(at, *items):
        out = []
        for name, shape, dt in items:
            out.append(place(name, shape, dt, at))
            at += (int(np.prod(shape[1:])) * 4 + 31) // 32 * 32
        return out

    XT = END + 24 * K
    (col2, rowb, inv, posi, ones, tri, scal, posf, a_exp, dtz, dts, d_a, acum, e_ac, d_end, g_ss, g_ms, g_r,
     bm_t, cbm, zt, yb) = row_of(
        XT, ("col2", [P, 144], F32), ("rowb", [P, 96], F32), ("inv", [P, 32], F32), ("posi", [P, 2], I32),
        ("ones", [P, TOK], F32), ("tri", [P, P], F32), ("scal", [P, 2], F32), ("posf", [P, 2], F32), ("a_exp", [P, 32], F32),
        ("dtz", [P, 64], F32), ("dts", [P, 64], F32), ("d_a", [P, 64], F32), ("acum", [P, 64], F32),
        ("e_ac", [P, 32], F32), ("d_end", [P, 32], F32), ("g_ss", [P, 2], F32), ("g_ms", [P, 2], F32),
        ("g_r", [P, 2], F32), ("bm_t", [P, P], F32), ("cbm", [P, TH, P], F32),
        ("zt", [P, TH, NBW], F32), ("yb", [P, TH, NBW], F32))
    HG = 8
    SP_ = 64
    dec, u_in, cv, xs, xdt, xde, st = row_of(
        AT, ("dec", [P, TH, HG * P], F32), ("u_in", [P, TH, 768], F32), ("cv", [P, 6, TOK], F32),
        ("xs", [P, TH, NBW], F32), ("xdt", [P, TH, NBW], F32), ("xde", [P, NBW], F32), ("st", [P, NBW], F32))
    th = place("th", [P, 6 * TOK], F32, AT + 8 * K)
    zth = place("zth", [P, TH, NBW], F32, END + 16 * K)
    ac_t = place("ac_t", [64, P], F32, AT + 30 * K)
    mbuf = []
    for n, at in enumerate((AT, WD + 60 * K)):
        mbuf.append(row_of(at, *[(f"m{n}_{name}", shape, F32) for name, shape in (
            ("qkv", [P, 4, TH, HD]), ("qk_t", [P, 2 * TOK]), ("prob", [P, 2 * TOK]), ("p_t", [P, 2 * TOK]),
            ("y", [P, TH, HD]), ("th", [P, TH, HD]), ("sm", [P, 8]))]))
    mqkv = [[mbuf[0][0]], [mbuf[1][0], place("m1_qkv_b", [P, 4, TH, HD], F32, XT + 10 * K)]]
    sc_in, sc_cv, sc_y = row_of(AT, ("sc_in", [P, TH, 4, NBW], F32), ("sc_cv", [P, 4, TOK], F32),
                                ("sc_y", [P, 4 * TOK], F32))
    lat, = row_of(WD + 20 * K, ("lat", [P, TH, 1344], F32))
    ybuf, = row_of(WD, ("ybuf", [P, TH, D], F32))
    (kr, cosn, sinn, ang, ang2, ang3, lz0, lz1, lp0, lp1, lpt0, lpt1, kr_t) = row_of(
        WD + 73 * K, ("kr", [P, TH, 64], F32), ("cosn", [P, TH, 64], F32), ("sinn", [P, TH, 64], F32),
        ("ang", [P, TH, 64], F32), ("ang2", [P, TH, 64], F32), ("ang3", [P, TH, 64], F32),
        ("lz0", [P, H3], F32), ("lz1", [P, H3], F32), ("lp0", [P, H3], F32), ("lp1", [P, H3], F32),
        ("lpt0", [P, H3], F32), ("lpt1", [P, H3], F32), ("kr_t", [64, TOK], F32))
    lz, lp, lpt = (lz0, lz1), (lp0, lp1), (lpt0, lpt1)
    lq0, lq1, lkv0, lkv1, lqk0, lqk1 = row_of(
        XT + 3 * K, ("lq0", [P, TH, 192], F32), ("lq1", [P, TH, 192], F32),
        ("lkv0", [P, TH, 256], F32), ("lkv1", [P, TH, 256], F32),
        ("lqk0", [P, 2 * TOK], F32), ("lqk1", [P, 2 * TOK], F32))
    lq2 = place("lq2", [P, TH, 192], F32, XT + 14 * K)
    lkv2 = place("lkv2", [P, TH, 256], F32, WD + 86 * K)
    lq, lkv, lqk = (lq0, lq1, lq2), (lkv0, lkv1, lkv2), (lqk0, lqk1)
    lr0, lr1, lsm, rswap = row_of(
        WD + 60 * K, ("lr0", [64, TOK], F32), ("lr1", [64, TOK], F32),
        ("lsm", [P, 16], F32), ("rswap", [P, TH, 64], F32))
    lr = (lr0, lr1)
    causal = place("causal", [P, H3], F32, END + 21 * K)
    lat_junk = place("lat_junk", [P, 2560], F32, XT + 3 * K)
    zgt = place("zgt", [P, TH, NBW], F32, WD + 64 * K)
    res, fin = row_of(WD + 60 * K, ("res", [P, 4, TH, NBW], F32), ("fin", [P, D], F32))

    acc = [ctx.enter_context(nc.psum_tensor(f"acc{n}", [P, NBW], F32)) for n in range(4)]
    turn = [ctx.enter_context(nc.psum_tensor(f"turn{n}", [P, NBW], F32)) for n in range(2)]
    ps_s = ctx.enter_context(nc.psum_tensor("ps_s", [P, NBW], F32))
    ps_y = ctx.enter_context(nc.psum_tensor("ps_y", [P, NBW], F32))

    d_mem = dram("d_mem", (TOK, 4 * NBW))
    d_in = dram("d_in", (TOK, W_IN1))
    d_x = [dram(f"d_x{n}", (TOK, D)) for n in range(3)]
    d_e = dram("d_e", (8, 4 * P))
    d_skew = dram("d_skew", (P, 8, 4 * P))

    d_ev = dram("d_ev", (TOK, 10240))
    d_ac = dram("d_ac", (TH, 32 * P))
    d_x4 = dram("d_x4", (TOK, D))
    d_om = dram("d_om", (TOK, 2 * NBW))
    d_q = dram("d_q", (TOK, 3072))
    d_kv = dram("d_kv", (TOK, 4096))

    def halves(a):
        return a.rearrange("(t p) n -> p t n", p=P)

    raw_landed = [sem(f"raw_landed{s}") for s in range(RING)]
    hi_ready = sem("hi_ready")
    lo_ready = sem("lo_ready")
    unit_used = sem("unit_used")
    sums_out = sem("sums_out")
    tile_ready = sem("tile_ready")
    tile_moved = [sem(f"tile_moved{s}") for s in range(2)]
    xin_landed = [sem(f"xin_landed{s}") for s in range(2)]
    turned = sem("turned")
    turn_hi = sem("turn_hi")
    turn_lo = sem("turn_lo")
    squared = sem("squared")
    sum_ready = sem("sum_ready")
    mean_ready = sem("mean_ready")
    rstd_ready = sem("rstd_ready")
    zeroed = sem("zeroed")
    const_ready = sem("const_ready")
    mask_ready = sem("mask_ready")
    pe_once = sem("pe_once")
    act_once = sem("act_once")
    ones_ready = sem("ones_ready")
    e_built, e_out = sem("e_built"), sem("e_out")
    skewed = sem("skewed")
    bias_in, bias_ready = sem("bias_in"), sem("bias_ready")
    at_loaded = [sem(f"at_loaded{s}") for s in range(4)]
    AT_LOADS = 4 * 32
    at_qk_ps, at_qk = sem("at_qk_ps"), sem("at_qk")
    at_scores, at_z = sem("at_scores"), sem("at_z")
    at_abs, at_exp0, at_keep = sem("at_abs"), sem("at_exp0"), sem("at_keep")
    at_drop, at_scan, at_left = sem("at_drop"), sem("at_scan"), sem("at_left")
    at_max, at_exp, at_inv = sem("at_max"), sem("at_exp"), sem("at_inv")
    at_prob = {k: sem(f"at_prob_{k}") for k in ("sb", "ca")}
    at_pt_ps, at_pt = sem("at_pt_ps"), sem("at_pt")
    at_y_ps, at_y_hi, at_y_lo = sem("at_y_ps"), sem("at_y_hi"), sem("at_y_lo")
    gates_in = [sem(f"gates_in{s}") for s in range(2)]
    gates_sig = sem("gates_sig")
    ff_mul = sem("ff_mul")
    ff_half = sem("ff_half")
    ple_lo = sem("ple_lo")
    late_in = sem("late_in")
    pl_mul, pl_sum = sem("pl_mul"), sem("pl_sum")

    small_in = sem("small_in")
    cc = sem("cc")
    dt_v, dt_out = sem("dt_v"), sem("dt_out")
    m_loaded = [sem(f"m_loaded{s}") for s in range(2)]
    m_qk_ps, m_qk, m_scores, m_max, m_max2, m_exp, m_inv, m_pt_ps, m_pt = (
        sem(f"m_{n}") for n in ("qk_ps", "qk", "scores", "max", "max2", "exp", "inv", "pt_ps", "pt"))
    m_y_ps, m_zs, m_y, m_yt_ps, m_hi, m_lo = (
        sem(f"m_{n}") for n in ("y_ps", "zs", "y", "yt_ps", "hi", "lo"))
    s_u, s_ac, s_z = sem("s_u"), sem("s_ac"), sem("s_z")
    s_ut, s_conv, s_th, s_silu, s_xt, s_cb = (sem(f"s_{n}") for n in ("ut", "conv", "th", "silu", "xt", "cb"))
    s_xs, s_cbm, s_xdt, s_xde, s_min = (sem(f"s_{n}") for n in ("xs", "cbm", "xdt", "xde", "min"))
    s_dec, s_st, s_state, s_m, s_xd, s_y = (sem(f"s_{n}") for n in ("dec", "st", "state", "m", "xd", "y"))
    s_ya, s_yb, s_zth, s_zs, s_yg, s_sq = (sem(f"s_{n}") for n in ("ya", "yb", "zth", "zs", "yg", "sq"))
    s_gm, s_gr, s_tile = (sem(f"s_{n}") for n in ("gm", "gr", "tile"))
    c_in, c_u, c_th, c_zs, c_w, c_ut, c_wt, c_conv, c_y, c_hi, c_lo = (
        sem(f"c_{n}") for n in ("in", "u", "th", "zs", "w", "ut", "wt", "conv", "y", "hi", "lo"))
    lat_ms, lat_r, lat_ps, lat_hi, lat_lo = (sem(f"lat_{n}") for n in ("ms", "r", "ps", "hi", "lo"))
    r_step, r_kr = sem("r_step"), sem("r_kr")
    l_rot, l_qk_ps, l_qr_ps, l_qk, l_qr, l_scores, l_z, l_max, l_exp, l_inv, l_pt_ps, l_pt, l_y_ps, l_y = (
        sem(f"l_{n}") for n in ("rot", "qk_ps", "qr_ps", "qk", "qr", "scores", "z", "max", "exp", "inv",
                                "pt_ps", "pt", "y_ps", "y"))
    l_rp = sem("l_rp")
    l_zs, l_tile = sem("l_zs"), sem("l_tile")
    fin_ready, fin_out = sem("fin_ready"), sem("fin_out")

    TURN = {"mem": 0, "x": 4, "mix": 8, "ffn": 12, "ffo": 16, "ple": 27, "x3": 31,
            "sy": 35, "x4": 39, "oy": 43}
    STORED = {"mem": 0, "win": 2, "mix": 12, "ffo": 14, "gate": 16, "l2": 18,
              "sc": 24, "eout": 28, "omem": 30, "uq": 31, "ukv": 34, "oout": 38}
    LOADED = {"mem": 0, "x": 2, "mix": 4, "ffo": 6, "gate": 8, "eout": 10, "oout": 12}

    def blk(stage, b, i=0, nb=2):
        return At(B0[stage] + b, i, nb)

    def written(b):
        return b.times(1, 3)

    block = ctx.enter_context(nc.Block())

    @block.sync
    def _(sp):
        def load(u):
            sp.wait_ge(lo_ready, u.times(1, 1))
            sp.dma_start(raw[:, u.slot, :], stream[bass.ds(u.times(1), 1), :, :].rearrange("a p n -> p (a n)"))\
              .then_inc(raw_landed[u.slot], 16)

        with sp.Fori(0, N_UNITS // RING) as i:
            for s in range(RING):
                load(At(s, i, RING))
        for u in range(N_UNITS // RING * RING, N_UNITS):
            load(At(u))

    @block.gpsimd
    def _(pool):
        def load_tile(src, b, slot, value):
            for s_, v_ in value:
                pool.wait_ge(s_, v_)
            pool.dma_start(xin[slot][:, :, :], src[:, :, bass.ds(b.times(NBW), NBW)])\
                .then_inc(xin_landed[slot], 16)

        def store_tile(dst, b, slot, s_, v_):
            pool.wait_ge(s_, v_)
            pool.dma_start(dst[:, :, bass.ds(b.times(NBW), NBW)], tile[slot][:, :, :])\
                .then_inc(tile_moved[slot], 16)

        def all_stored(count):
            for s in range(2):
                pool.wait_ge(tile_moved[s], 16 * (count + 1))

        pool.dma_start(tile[0][0:122, 0, 0:P], io["gain_rows"]).then_inc(tile_moved[0], 16)
        pool.dma_start(tile[1][0:8, 0, 0:N_REL], io["rel_bias"]).then_inc(tile_moved[1], 16)
        pool.dma_start(junk[0:120, 0:P], io["rows2"]).then_inc(small_in, 16)
        pool.dma_start(junk[0:24, P:2 * P], io["rows3"]).then_inc(small_in, 16)
        pool.dma_start(rowb[:, :], io["rowb"].partition_broadcast(P)).then_inc(small_in, 16)
        pool.dma_start(inv[:, :], io["inv"].partition_broadcast(P)).then_inc(small_in, 16)
        pool.dma_start(posi[:, :], io["positions"]).then_inc(small_in, 16)
        pool.memset(ident[:, :], 0.0).then_inc(zeroed, 1)
        pool.memset(past[:, :], 0.0).then_inc(zeroed, 1)
        pool.memset(expo[:, :], -0.5).then_inc(zeroed, 1)
        pool.wait_ge(zeroed, 1)
        pool.affine_select(out=ident[:, :], in_=ident[:, :], compare_op=ALU.not_equal, fill=1.0, base=0,
                           pattern=[[-1, P]], channel_multiplier=1).then_inc(const_ready, 1)
        mem_v, x_v, dx_v = halves(io["mem"]), halves(io["x"]), [halves(a) for a in d_x]
        for b in range(4):
            free = [(turned, 2 * b - 2), (squared, b - 1)] if b >= 2 else []
            load_tile(mem_v, At(b), b % 2, free)
        pool.memset(tri[:, :], 1.0).then_inc(mask_ready, 1)
        pool.wait_ge(mask_ready, 1)
        pool.affine_select(out=tri[:, :], in_=tri[:, :], compare_op=ALU.is_ge, fill=0.0, base=0,
                           pattern=[[1, P]], channel_multiplier=-1).then_inc(mask_ready, 1)
        pool.wait_ge(zeroed, 3)
        for at in (0, TOK):
            m = past[:, at:at + P]
            pool.affine_select(out=m, in_=m, compare_op=ALU.is_ge, fill=NEG, base=-1,
                               pattern=[[-1, P]], channel_multiplier=1).then_inc(mask_ready, 1)

        def norm(r):
            pool.wait_ge(mean_ready, r + 1)
            pool.tensor_tensor(rstd[:, 2 * r:2 * r + 2], mean[:, 2 * r:2 * r + 2], expo[:, :], ALU.pow)\
                .then_inc(rstd_ready, 1)

        norm(0)
        for b in range(2):
            load_tile(x_v, At(b), b, [(turned, 2 * b + 6), (squared, b + 3)])
        pool.wait_ge(e_built, 3)
        pool.dma_start(d_e[:, 0:H3], e_rows[:, :]).then_inc(e_out, 16)
        pool.wait_ge(e_out, 16)
        pool.dma_start(bass.AP(d_skew.tensor, 0, [[8 * 4 * P + 1, P], [4 * P, 8], [1, H3]]),
                       bass.AP(d_e.tensor, 0, [[0, P], [4 * P, 8], [1, H3]])).then_inc(skewed, 16)
        pool.wait_ge(skewed, 16)
        pool.dma_start(bias[:, :, 0:P], d_skew[:, :, TOK - 1:H3 - 1]).then_inc(bias_in, 16)
        pool.dma_start(bias[:, :, P:H3], d_skew[:, :, P - 1:H3 - 1]).then_inc(bias_in, 16)
        pool.wait_ge(bias_in, 32)
        pool.memset(bias[0:CHUNK, :, CHUNK:P], NEG).then_inc(bias_ready, 1)
        pool.memset(bias[0:CHUNK, :, H3 - CHUNK:H3], NEG).then_inc(bias_ready, 1)
        for b in range(4):
            store_tile(halves(d_mem), At(b), b % 2, sums_out, B0["mem"] + b + 3)
            if b < 2:
                load_tile(x_v, At(b + 2), b, [(turned, 2 * b + 10), (squared, b + 5)])
        norm(1)
        din_v = halves(d_in)
        with pool.Fori(0, 5) as i:
            for b in range(2):
                store_tile(din_v, At(b, i, 2), b, sums_out, written(blk("win", b, i)))
        heads = [halves(d_in[:, 3072 * k:3072 * (k + 1)]).rearrange("p t (m h d) -> p t m h d", m=3, h=8)
                 for k in range(2)]

        def load_head(j, J, m):
            if J is not None:
                pool.wait_ge(at_y_ps, J)
            for t in range(TH):
                src = heads[j % 2][:, t, :, bass.ds(m, 1), :].rearrange("p m h d -> p m (h d)")
                pool.dma_start(qkv[j][:, t, :, :], src).then_inc(at_loaded[j], 16)

        store_tile(din_v, At(10), 0, sums_out, written(blk("win", 10)))
        pool.wait_ge(tile_moved[1], 16 * (STORED["win"] + 5 + 1))
        pool.wait_ge(tile_moved[0], 16 * (STORED["win"] + 6 + 1))
        for j in range(4):
            load_head(j, None, j // 2)
        store_tile(din_v, At(11), 1, sums_out, written(blk("win", 11)))
        pool.wait_ge(tile_moved[1], 16 * (STORED["win"] + 6 + 1))

        def gate_pair(i, last):
            for j in range(4):
                if not last:
                    load_head(j, At(j, i, 4).times(1, 3), At(2 + j // 2, i, 2).times(1))
                if j == 0:
                    store_tile(din_v, At(12, i, 2), 0, sums_out, written(blk("win", 12, i)))
            if last:
                pool.wait_ge(at_z, 17)
                pool.wait_ge(tile_moved[0], 16 * (STORED["win"] + 9 + 1))
                load_gates(0, 0, None)
            store_tile(din_v, At(13, i, 2), 1, sums_out, written(blk("win", 13, i)))

        gate_v = d_in[:, 6144:].rearrange("(t p) (g n) -> p t g n", p=P, g=2)

        def load_gates(s, b, n):
            if n is not None:
                pool.wait_ge(tile_ready, n)
            for g in range(2):
                pool.dma_start(gates[s][:, g, :, :], gate_v[:, :, g, bass.ds(b, NBW)])\
                    .then_inc(gates_in[s], 16)

        with pool.Fori(0, 3) as i:
            gate_pair(i, False)
        gate_pair(3, True)
        pool.wait_ge(at_y_lo, 17)
        pool.wait_ge(tile_moved[1], 16 * (STORED["win"] + 9 + 1))
        load_gates(1, NBW, None)
        all_stored(STORED["mix"])
        for n in (2, 3):
            load_gates(n % 2, n * NBW, n + 1)

        def residual(stage, old, new, ready, base):
            for b in range(2):
                load_tile(old, At(b), b, [])
            for b in range(4):
                s_, v_ = ready(b)
                store_tile(new, At(b), b % 2, s_, v_)
                if b < 2:
                    load_tile(old, At(b + 2), b % 2, [])

        residual("mix", x_v, dx_v[0], lambda b: (sums_out, B0["mix"] + b + 3), 0)
        norm(2)
        all_stored(STORED["ffo"])
        pool.wait_ge(unit_used, U0["ffo"] + RING + 1)
        residual("ffo", dx_v[0], dx_v[1], lambda b: (sums_out, B0["ffo"] + b + 3), 0)
        norm(3)
        all_stored(STORED["gate"])
        pool.wait_ge(sums_out, B0["ffo"] + 3 + 3)
        pool.dma_start(pl_row[:, :, :], halves(io["p"])).then_inc(late_in, 16)
        pool.dma_start(gf_row[:, :], io["g_final"].partition_broadcast(P)).then_inc(late_in, 16)
        residual("gate", dx_v[1], dx_v[2], lambda b: (tile_ready, 4 + b + 1 + 2), 0)
        norm(4)
        all_stored(STORED["l2"])
        norm(5)
        ev_v = halves(d_ev)
        mem_heads = [d_mem[:, 1024 * n:1024 * (n + 1)].rearrange("(t p) (m h d) -> p m t h d", p=P, m=2, h=4)
                     for n in range(2)]

        def load_mem(n, h, J, src):
            buf, landed = mqkv[n][J % len(mqkv[n])], m_loaded[J % len(mqkv[n])]
            for m in range(2):
                q = src[:, m * NBW:(m + 1) * NBW].rearrange("(t p) (h d) -> p t h d", p=P, h=4)
                pool.dma_start(buf[:, 3 * m, :, :], q[:, :, bass.ds(h, 1), :].rearrange("p t h d -> p t (h d)"))\
                    .then_inc(landed, 16)
                kv = mem_heads[n][:, m, :, bass.ds(h, 1), :].rearrange("p t h d -> p t (h d)")
                pool.dma_start(buf[:, 1 + m, :, :], kv).then_inc(landed, 16)

        def store_block(dst, stage, b, i, col, slot):
            store_tile(dst, col, slot, sums_out, written(blk(stage, b, i)))

        for b in range(2):
            store_block(ev_v, "ein", b, 0, At(b), b)
        all_stored(STORED["l2"] + 1)
        load_mem(0, 0, 0, d_ev)

        def ein_pair(i, last):
            store_block(ev_v, "ein", 2, i, At(2, i, 2), 0)
            if not last:
                pool.wait_ge(m_yt_ps, At(1, i, 1).times(1))
                load_mem(0, At(1, i, 1).times(1), 0, d_ev)
            store_block(ev_v, "ein", 3, i, At(3, i, 2), 1)

        with pool.Fori(0, 3) as i:
            ein_pair(i, False)
        ein_pair(3, True)
        for b in range(2):
            store_block(ev_v, "ein", 10 + b, 0, At(10 + b), b)
        all_stored(STORED["l2"] + 6)
        pool.wait_ge(m_lo, 5)
        pool.wait_ge(dt_v, 6)
        pool.dma_start(d_ac.rearrange("t (h q) -> (t h) q", q=P), ac_t[:, :]).then_inc(dt_out, 16)
        pool.wait_ge(dt_out, 16)

        def load_u(g):
            pool.dma_start(u_in[:, :, 0:512], ev_v[:, :, bass.ds(g.times(512, 1024), 512)]).then_inc(s_u, 16)
            for m in range(2):
                pool.dma_start(u_in[:, :, 512 + m * P:640 + m * P],
                               ev_v[:, :, bass.ds(g.times(P, 3072 + 512 * m), P)]).then_inc(s_u, 16)

        def load_ac(g):
            pool.dma_start(dec[:, :, :], d_ac[:, bass.ds(g.times(HG * P), HG * P)].partition_broadcast(P))\
                .then_inc(s_ac, 16)

        def load_z(g):
            pool.dma_start(zt[:, :, :], ev_v[:, :, bass.ds(g.times(512, 4096), 512)]).then_inc(s_z, 16)

        load_u(At(0))
        load_ac(At(0))
        load_z(At(0))

        def sc_pair(i, last):
            g = At(1, i, 1)
            if not last:
                pool.wait_ge(s_silu, g.times(1))
                load_u(g)
            store_block(ev_v, "sc", 0, i, At(12, i, 2), 0)
            if not last:
                pool.wait_ge(s_y, g.times(1))
                load_ac(g)
                pool.wait_ge(s_yg, g.times(1))
                load_z(g)
            pool.wait_ge(s_gm, g.times(1))
            pool.tensor_tensor(g_r[:, :], g_ms[:, :], expo[:, :], ALU.pow).then_inc(s_gr, 1)
            store_block(ev_v, "sc", 1, i, At(13, i, 2), 1)

        with pool.Fori(0, 3) as i:
            sc_pair(i, False)
        sc_pair(3, True)
        all_stored(STORED["eout"])
        for j in range(2):
            if j:
                pool.wait_ge(c_ut, 2 * j)
                pool.wait_ge(c_wt, 2 * j)
            else:
                pool.wait_ge(turn_lo, 2 * TURN["x4"] + 2)
            for t in range(TH):
                pool.dma_start(sc_in[:, t, :, :].rearrange("p a n -> p (a n)"),
                               ev_v[:, t, 6144 + 2048 * j:6144 + 2048 * (j + 1)]).then_inc(c_in, 16)
        residual("eout", dx_v[2], halves(d_x4), lambda b: (sums_out, B0["eout"] + b + 3), 0)
        pool.memset(causal[:, :], 0.0).then_inc(mask_ready, 1)
        pool.wait_ge(mask_ready, 5)
        for at in (0, TOK):
            pool.affine_select(out=causal[:, at:at + P], in_=causal[:, at:at + P], compare_op=ALU.is_ge, fill=NEG,
                               base=0, pattern=[[-1, P]], channel_multiplier=1).then_inc(mask_ready, 1)
        norm(6)
        om_v = halves(d_om)
        for b in range(2):
            store_block(om_v, "omem", b, 0, At(b), b)
        pool.wait_ge(lat_ms, 2)
        for m in range(2):
            pool.tensor_tensor(rstd[:, 16 + 2 * m:18 + 2 * m], mean[:, 16 + 2 * m:18 + 2 * m], expo[:, :],
                               ALU.pow).then_inc(lat_r, 1)
        all_stored(STORED["uq"])
        load_mem(1, 0, 4, d_om)
        load_mem(1, 1, 5, d_om)
        q_v, kv_v = halves(d_q), halves(d_kv)

        def load_latent(J):
            s = J % 3
            if J >= 3:
                pool.wait_ge(l_y_ps, J)
            pool.dma_start(lq[s][:, :, :], q_v[:, :, 192 * J:192 * (J + 1)]).then_inc(at_loaded[s], 16)
            pool.dma_start(lkv[s][:, :, :], kv_v[:, :, 256 * J:256 * (J + 1)]).then_inc(at_loaded[s], 16)

        for b in range(6):
            if b == 4:
                pool.wait_ge(m_yt_ps, 5)
                load_mem(1, 2, 6, d_om)
            store_block(q_v, "uq", b, 0, At(b), b % 2)
        for b in range(8):
            if b == 1:
                pool.wait_ge(m_yt_ps, 6)
                load_mem(1, 3, 7, d_om)
            store_block(kv_v, "ukv", b, 0, At(b), b % 2)
            if b == 3:
                for s in range(2):
                    pool.wait_ge(tile_moved[s], 16 * (STORED["ukv"] + 1 + 1))
                for J in range(3):
                    load_latent(J)
        all_stored(STORED["oout"])
        for J in range(3, 16):
            load_latent(J)

        pool.wait_ge(l_tile, 4)
        pool.dma_start(fin[:, :], io["final_norm"].partition_broadcast(P)).then_inc(late_in, 16)
        for b in range(4):
            free = [] if b < 2 else [(sums_out, B0["oout"] + b + 1)]
            load_tile(halves(d_x4), At(b), b % 2, free)
        norm(7)
        out_v = halves(io["out"])
        for b in range(4):
            pool.wait_ge(fin_ready, b + 1)
            pool.dma_start(out_v[:, :, b * NBW:(b + 1) * NBW], res[:, b, :, :]).then_inc(fin_out, 16)
        pool.wait_ge(fin_out, 64)

    @block.tensor
    def _(pe):
        def unit(u, src, chunk, bank, first, last, width=NBW):
            pe.wait_ge(lo_ready, u.times(1, 1 + RING))
            s = u.slot
            for c in range(UCH):
                w = slice(c * width, (c + 1) * width)
                for t in range(TH):
                    a_hi = src[0][:, chunk + c, t * P:(t + 1) * P]
                    a_lo = src[1][:, chunk + c, t * P:(t + 1) * P]
                    out = acc[2 * bank + t][:, 0:width]
                    nc.tensor.matmul(out, a_hi, w_hi[:, s, w], start=first and c == 0, stop=False)
                    nc.tensor.matmul(out, a_hi, w_lo[:, s, w], start=False, stop=False)
                    mm = nc.tensor.matmul(out, a_lo, w_hi[:, s, w], start=False,
                                          stop=last and c == UCH - 1)
            mm.then_inc(unit_used, 1)

        def turn_tile(n, src, ready, value):
            pe.wait_ge(ready, value)
            for h in range(2):
                pe.wait_ge(turn_lo, n.times(2, h + 1))
                for c in range(2):
                    for t in range(TH):
                        at = (2 * h + c) * P
                        mm = nc.tensor.transpose(turn[h][:, (c * TH + t) * P:(c * TH + t + 1) * P],
                                                 src[:, t, at:at + P], ident[:, :])
                mm.then_inc(turned, 1)

        def source(turns, k):
            if k % 2 == 0:
                pe.wait_ge(turn_lo, 2 * (turns + k // 2) + 4)

        pe.sem_inc(unit_used, RING)
        pe.sem_inc(at_scores, 2)
        pe.sem_inc(at_y_ps, 2)
        pe.sem_inc(l_y_ps, 2)
        pe.wait_ge(const_ready, 1)
        pe.wait_ge(tile_moved[0], 16)
        nc.tensor.transpose(ps_s[:, 0:122], tile[0][0:122, 0, 0:P], ident[0:122, 0:122]).then_inc(pe_once, 1)
        pe.wait_ge(small_in, 80)
        nc.tensor.transpose(ps_y[:, 0:120], junk[0:120, 0:P], ident[0:120, 0:120])
        nc.tensor.transpose(ps_y[:, 120:144], junk[0:24, P:2 * P], ident[0:24, 0:24]).then_inc(pe_once, 1)
        for b in range(4):
            turn_tile(At(TURN["mem"] + b), xin[b % 2], xin_landed[b % 2], 16 * (b // 2 + 1))

        with pe.Fori(0, 2) as i:
            for b in range(2):
                pe.wait_ge(sums_out, blk("mem", b, i).times(1, 1))
                for k in range(8):
                    source(TURN["mem"], k)
                    unit(At(U0["mem"] + 8 * b + k, i, 16), mem_t, UCH * k, b, k == 0, k == 7)
                turn_tile(At(TURN["x"] + b, i, 2), xin[b], xin_landed[b], At(LOADED["x"], i, 1).times(16, 16))

        with pe.Fori(0, 6) as i:
            for b in range(2):
                pe.wait_ge(sums_out, blk("win", b, i).times(1, 1))
                for k in range(8):
                    source(TURN["x"], k)
                    unit(At(U0["win"] + 8 * b + k, i, 16), x_t, UCH * k, b, k == 0, k == 7)

        def attend(p, i):
            for j in range(4):
                J, m, s, kind = At(j, i, 4), At(j // 2, i, 2), j % 2, ("sb", "ca")[j % 2]
                if p == 3 * j:
                    pe.wait_ge(at_loaded[j], At(0, i, 1).times(32, 32))
                    pe.wait_ge(at_qk, J.times(1, 1))
                    for x in range(2):
                        for t in range(TH):
                            mm = nc.tensor.transpose(turn[0][:, (2 * x + t) * P:(2 * x + t + 1) * P],
                                                     qkv[j][:, t, x, :], ident[:, :])
                    mm.then_inc(at_qk_ps, 1)
                if p == 3 * j + 1:
                    pe.wait_ge(at_qk, J.times(1, 2))
                    pe.wait_ge(at_z, J.times(1, 1))
                    q, k = qk_t[s][:, 0:TOK], qk_t[s][:, TOK:2 * TOK]
                    nc.tensor.matmul(ps_s[:, 0:P], q[:, 0:P], k[:, 0:P], start=True, stop=True)
                    nc.tensor.matmul(ps_s[:, P:H3], q[:, P:TOK], k, start=True, stop=True)\
                        .then_inc(at_scores, 1)
                if p == 3 * j + 5:
                    pe.wait_ge(at_prob[kind], m.times(1, 1))
                    pe.wait_ge(at_pt, J.times(1, 1))
                    for c in range(3):
                        mm = nc.tensor.transpose(turn[1][:, c * P:(c + 1) * P],
                                                 prob[kind][:, c * P:(c + 1) * P], ident[:, :])
                    mm.then_inc(at_pt_ps, 1)
                if p == 3 * j + 6:
                    pe.wait_ge(at_pt, J.times(1, 2))
                    pe.wait_ge(at_y_lo, J.times(1, 1))
                    nc.tensor.matmul(ps_y[:, 0:TOK], qkv[j][:, 0, 2, :], p_t[s][:, 0:TOK],
                                     start=True, stop=False)
                    nc.tensor.matmul(ps_y[:, P:TOK], qkv[j][:, 1, 2, :], p_t[s][:, TOK:H3],
                                     start=False, stop=True).then_inc(at_y_ps, 1)

        with pe.Fori(0, 4) as i:
            for b in range(2):
                pe.wait_ge(sums_out, blk("win", 12 + b, i).times(1, 1))
                for k in range(8):
                    attend(8 * b + k, i)
                    unit(At(U0["win"] + 96 + 8 * b + k, i, 16), x_t, UCH * k, b, k == 0, k == 7)

        pe.wait_ge(at_y_lo, 17)
        with pe.Fori(0, 4) as i:
            for b in range(2):
                pe.wait_ge(sums_out, blk("out", b, i).times(1, 1))
                for k in range(4):
                    unit(At(U0["out"] + 4 * b + k, i, 8), y_t, 8 * b + UCH * k, b, k == 0, k == 3)
            turn_tile(At(TURN["mix"], i, 1), tile[0], tile_ready, At(0, i, 1).times(1, 3))

        def residual(stage, src, units, src_turns, turns, ready):
            with pe.Fori(0, 2) as i:
                for b in range(2):
                    pe.wait_ge(sums_out, blk(stage, b, i).times(1, 1))
                    for k in range(units):
                        source(src_turns, k)
                        if b == 1 and k == 3:
                            turn_tile(At(turns, i, 2), tile[0], *ready(0, i))
                        unit(At(U0[stage] + b * units + k, i, 2 * units), src, UCH * k, b,
                             k == 0, k == units - 1)
                turn_tile(At(turns + 1, i, 2), tile[1], *ready(1, i))

        def from_sums(stage):
            return lambda b, i: (sums_out, written(blk(stage, b, i)))

        residual("mix", m_t, 8, TURN["mix"], TURN["ffn"], from_sums("mix"))
        with pe.Fori(0, 11) as i:
            for b in range(2):
                pe.wait_ge(sums_out, blk("ffn", b, i).times(1, 1))
                for k in range(8):
                    source(TURN["ffn"], k)
                    unit(At(U0["ffn"] + 8 * b + k, i, 16), x_t, UCH * k, b, k == 0, k == 7)
            turn_tile(At(TURN["ffo"], i, 1), tile[0], sums_out, written(blk("ffn", 1, i)))
        residual("ffo", ff_t, 22, TURN["ffo"], TURN["ple"], from_sums("ffo"))

        pe.wait_ge(late_in, 32)
        for c in range(2):
            for t in range(TH):
                mm = nc.tensor.transpose(ps_s[:, (2 * c + t) * P:(2 * c + t + 1) * P],
                                         pl_row[:, t, c * P:(c + 1) * P], ident[:, :])
        mm.then_inc(pe_once, 1)
        pe.wait_ge(ple_lo, 1)
        for b in range(4):
            pe.wait_ge(sums_out, B0["ple"] + b + 1)
            unit(At(U0["ple"] + b), ple_t, 0, b % 2, True, True)
        residual("gate", x_t, 8, TURN["ple"], TURN["x3"],
                 lambda b, i: (tile_ready, At(4 + b, i, 2).times(1, 3)))

        def mem_job(n, J, p):
            _, qk_, pr_, pt_, y_, th_, sm_ = mbuf[n]
            qkv_ = mqkv[n][J.k % len(mqkv[n])]
            if p == 0:
                if n == 0:
                    pe.wait_ge(m_loaded[0], J.times(64, 64))
                else:
                    pe.wait_ge(m_loaded[J.k % 2], 64 * ((4 if J.k % 2 == 0 else 0) + (J.k - 4) // 2 + 1))
                pe.wait_ge(m_qk, J.times(1, 1))
                for x in range(2):
                    for t in range(TH):
                        mm = nc.tensor.transpose(turn[0][:, (2 * x + t) * P:(2 * x + t + 1) * P],
                                                 qkv_[:, x, t, :], ident[:, :])
                mm.then_inc(m_qk_ps, 1)
            if p == 1:
                pe.wait_ge(m_qk, J.times(1, 2))
                for t in range(TH):
                    mm = nc.tensor.matmul(ps_s[:, t * TOK:(t + 1) * TOK], qk_[:, t * P:(t + 1) * P],
                                          qk_[:, TOK:2 * TOK], start=True, stop=True)
                mm.then_inc(m_scores, 1)
            if p == 4:
                pe.wait_ge(m_exp, J.times(1, 1))
                for k in range(2):
                    for t in range(TH):
                        mm = nc.tensor.transpose(turn[1][:, (2 * k + t) * P:(2 * k + t + 1) * P],
                                                 pr_[:, t * TOK + k * P:t * TOK + (k + 1) * P], ident[:, :])
                mm.then_inc(m_pt_ps, 1)
            if p == 5:
                pe.wait_ge(m_pt, J.times(1, 1))
                pe.wait_ge(m_lo, J.times(1, 1))
                for t in range(TH):
                    for k in range(2):
                        mm = nc.tensor.matmul(ps_y[:, t * P:(t + 1) * P], pt_[:, (2 * k + t) * P:(2 * k + t + 1) * P],
                                              qkv_[:, 2, k, :], start=k == 0, stop=k == 1)
                mm.then_inc(m_y_ps, 1)
            if p == 7:
                pe.wait_ge(m_y, J.times(1, 1))
                for t in range(TH):
                    mm = nc.tensor.transpose(ps_y[:, TOK + t * P:TOK + (t + 1) * P], y_[:, t, :], ident[:, :])
                mm.then_inc(m_yt_ps, 1)

        def pair_of(stage, b0, i, per, units, src, chunk, beside=None, turns=None):
            for b in range(2):
                n = blk(stage, b0 + b, i)
                pe.wait_ge(sums_out, n.times(1, 1))
                for k in range(units):
                    if turns is not None:
                        source(turns, k)
                    if beside:
                        beside(units * b + k)
                    unit(At(U0[stage] + units * (b0 + b) + k, i, 2 * units), src, chunk + UCH * k, n.k % 2,
                         k == 0, k == units - 1)

        pair_of("ein", 0, 0, 0, 8, x3_t, 0, None, TURN["x3"])
        with pe.Fori(0, 4) as i:
            pair_of("ein", 2, i, 1, 8, x3_t, 0, lambda p: mem_job(0, At(0, i, 1), p - 4))
        pair_of("ein", 10, 0, 0, 8, x3_t, 0)
        u = At(U0["dt"])
        pe.wait_ge(lo_ready, u.times(1, 1 + RING))
        pe.wait_ge(m_lo, 5)
        for t in range(TH):
            for c in range(16):
                w = slice(32 * c, 32 * c + 32)
                a_hi, a_lo = (x3_t[x][:, c, t * P:(t + 1) * P] for x in range(2))
                out = ps_y[:, 32 * t:32 * t + 32]
                nc.tensor.matmul(out, a_hi, w_hi[:, u.slot, w], start=c == 0, stop=False)
                nc.tensor.matmul(out, a_hi, w_lo[:, u.slot, w], start=False, stop=False)
                mm = nc.tensor.matmul(out, a_lo, w_hi[:, u.slot, w], start=False, stop=c == 15)
        mm.then_inc(unit_used, 1)
        pe.wait_ge(dt_v, 3)
        pe.wait_ge(mask_ready, 2)
        nc.tensor.matmul(ps_y[:, 64:128], tri[:, :], d_a[:, :], start=True, stop=True)
        nc.tensor.matmul(ps_y[:, 128:192], ones[:, 0:P], d_a[:, :], start=True, stop=True).then_inc(pe_once, 1)
        pe.wait_ge(dt_v, 4)
        nc.tensor.transpose(ps_s[0:64, 0:P], acum[:, :], ident[:, :]).then_inc(pe_once, 1)

        def ssd(p, i):
            n = At(0, i, 1)
            if p == 0:
                pe.wait_ge(s_u, n.times(48, 48))
                pe.wait_ge(dt_v, 6)
                pe.wait_ge(turn_lo, At(TURN["sy"], i, 1).times(2, 2))
                for c in range(6):
                    bank = (turn[0], turn[1], ps_s)[c // 2]
                    for t in range(TH):
                        mm = nc.tensor.transpose(bank[:, (c % 2 * TH + t) * P:(c % 2 * TH + t + 1) * P],
                                                 u_in[:, t, c * P:(c + 1) * P], ident[:, :])
                mm.then_inc(s_ut, 1)
            if p == 7:
                pe.wait_ge(s_silu, n.times(1, 1))
                for t in range(TH):
                    for c in range(4):
                        mm = nc.tensor.transpose(turn[t][:, c * P:(c + 1) * P], cv[:, c, t * P:(t + 1) * P],
                                                 ident[:, :])
                mm.then_inc(s_xt, 1)
                nc.tensor.transpose(ps_s[:, 0:P], cv[:, 4, 0:P], ident[:, :])
                for t in range(TH):
                    w = slice(t * P, (t + 1) * P)
                    mm = nc.tensor.matmul(ps_s[:, (1 + t) * P:(2 + t) * P], cv[:, 4, w], cv[:, 5, w],
                                          start=True, stop=True)
                mm.then_inc(s_cb, 1)
            if p == 9:
                pe.wait_ge(s_xde, n.times(1, 1))
                nc.tensor.matmul(ps_s[:, :], bm_t[:, :], xde[:, :], start=True, stop=True).then_inc(s_st, 1)
            if p == 11:
                pe.wait_ge(s_m, n.times(1, 1))
                pe.wait_ge(s_xd, n.times(1, 1))
                pe.wait_ge(s_state, n.times(1, 1))
                for t in range(TH):
                    for h in range(HG):
                        w = slice(h * SP_, (h + 1) * SP_)
                        nc.tensor.matmul(turn[t][:, w], dec[:, t, h * P:(h + 1) * P], xdt[:, t, w],
                                         start=True, stop=True)
                nc.tensor.matmul(ps_y[:, :], cv[:, 5, P:TOK], st[:, :], start=True, stop=True).then_inc(s_y, 1)
            if p == 15:
                turn_tile(At(TURN["sy"], i, 1), yb, s_tile, n.times(1, 1))

        with pe.Fori(0, 4) as i:
            pair_of("sc", 0, i, 1, 8, x3_t, 0, lambda p: ssd(p, i))

        def short(p, j):
            if p == 3 + 5 * j:
                if j:
                    pe.wait_ge(c_y, j)
                pe.wait_ge(c_u, j + 1)
                pe.wait_ge(c_w, j + 1)
                for src, banks, s_ in ((sc_in[:, :, 1, :], turn, c_ut), (sc_in[:, :, 0, :], (ps_s, ps_y), c_wt)):
                    for h in range(2):
                        for c in range(2):
                            for t in range(TH):
                                mm = nc.tensor.transpose(
                                    banks[h][:, (c * TH + t) * P:(c * TH + t + 1) * P],
                                    src[:, t, (2 * h + c) * P:(2 * h + c + 1) * P], ident[:, :])
                        mm.then_inc(s_, 1)

        def eout_body(i, first):
            for b in range(2):
                n = blk("eout", b, i)
                pe.wait_ge(sums_out, n.times(1, 1))
                for k in range(14):
                    if b == 1 and k == 3:
                        turn_tile(At(TURN["x4"], i, 2), tile[0], sums_out, written(blk("eout", 0, i)))
                    if first and b == 0:
                        for j in range(2):
                            short(k, j)
                            if k == 10 + 2 * j:
                                pe.wait_ge(c_lo, j + 1)
                        if k == 0:
                            pe.wait_ge(turn_lo, 2 * TURN["x4"] + 2)
                            pe.wait_ge(m_lo, 5)
                    unit(At(U0["eout"] + 14 * b + k, i, 28), z_t, UCH * k, n.k % 2, k == 0, k == 13)
            turn_tile(At(TURN["x4"] + 1, i, 2), tile[1], sums_out, written(blk("eout", 1, i)))

        eout_body(0, True)
        eout_body(1, False)

        for b in range(3):
            n = B0["olow"] + b
            pe.wait_ge(sums_out, n + 1)
            for k in range(8):
                source(TURN["x4"], k)
                unit(At(U0["olow"] + 8 * b + k), x_t, UCH * k, n % 2, k == 0, k == 7, 448)

        def latents(h):
            if h == 0:
                pe.wait_ge(sums_out, B0["olow"] + 2 + 3)
            pe.wait_ge(lat_lo, h + 1)
            for c in range(2):
                for t in range(TH):
                    at = (2 * h + c) * P
                    mm = nc.tensor.transpose(turn[h % 2][:, (c * TH + t) * P:(c * TH + t + 1) * P],
                                             lat[:, t, at:at + P], ident[:, :])
            mm.then_inc(lat_ps, 1)

        def omem_beside(p):
            if p in (2, 4, 6, 8, 10):
                latents(p // 2 - 1)
            if p == 14:
                pe.wait_ge(r_kr, 1)
                for t in range(TH):
                    mm = nc.tensor.transpose(ps_s[0:64, t * P:(t + 1) * P], kr[:, t, :], ident[:, :])
                mm.then_inc(pe_once, 1)

        pair_of("omem", 0, 0, 0, 8, x_t, 0, omem_beside)
        pe.wait_ge(lat_lo, 7)
        pe.wait_ge(act_once, 12)
        for b in range(6):
            n = B0["uq"] + b
            pe.wait_ge(sums_out, n + 1)
            for k in range(3):
                p = 3 * b + k
                for j in range(4):
                    mem_job(1, At(4 + j), p - 7 * j - 5)
                unit(At(U0["uq"] + p), lat_t, UCH * k, n % 2, k == 0, k == 2)
        for b in range(8):
            n = B0["ukv"] + b
            pe.wait_ge(sums_out, n + 1)
            for k in range(2):
                p = 2 * b + k
                for j in range(4):
                    mem_job(1, At(4 + j), 18 + p - 7 * j - 5)
                unit(At(U0["ukv"] + p), lat_t, 6 + UCH * k, n % 2, k == 0, k == 1)

        def latent_heads(p):
            for J in range(16):
                s, q = J % 2, p - 2 * J
                if q == 0:
                    pe.wait_ge(at_loaded[J % 3], AT_LOADS + 32 * (J // 3 + 1))
                    pe.wait_ge(l_rot, J + 1)
                    pe.wait_ge(l_pt, J + 1)
                    pe.wait_ge(turn_lo, 2 * TURN["oy"] + sum(p > GATED + 8 * n + 2 * h for n in range(4)
                                                             for h in range(2)) + 2)
                    for x, src in enumerate((lq[J % 3], lkv[J % 3])):
                        for t in range(TH):
                            mm = nc.tensor.transpose(turn[0][:, (2 * x + t) * P:(2 * x + t + 1) * P],
                                                     src[:, t, 0:P], ident[:, :])
                    mm.then_inc(l_qk_ps, 1)
                    for t in range(TH):
                        mm = nc.tensor.transpose(turn[1][0:64, t * P:(t + 1) * P], lq[J % 3][:, t, P:192],
                                                 ident[:, :])
                    mm.then_inc(l_qr_ps, 1)
                if q == 1:
                    pe.wait_ge(l_qk, J + 1)
                    pe.wait_ge(l_qr, J + 1)
                    pe.wait_ge(l_z, J + 1)
                    q_n, k_n, q_r = lqk[s][:, 0:TOK], lqk[s][:, TOK:2 * TOK], lr[s]
                    for out, qw, kw in ((ps_s[:, 0:P], slice(0, P), slice(0, P)),
                                        (ps_s[:, P:H3], slice(P, TOK), slice(0, TOK))):
                        nc.tensor.matmul(out, q_n[:, qw], k_n[:, kw], start=True, stop=False)
                        mm = nc.tensor.matmul(out, q_r[:, qw], kr_t[:, kw], start=False, stop=True)
                    mm.then_inc(l_scores, 1)
                if q == 3:
                    pe.wait_ge(l_exp, J + 1)
                    pe.wait_ge(l_qr, min(J + 2, 16))
                    for c in range(3):
                        mm = nc.tensor.transpose(turn[1][:, c * P:(c + 1) * P], lp[s][:, c * P:(c + 1) * P],
                                                 ident[:, :])
                    mm.then_inc(l_pt_ps, 1)
                if q == 4:
                    pe.wait_ge(l_pt, J + 3)
                    pe.wait_ge(l_y, J + 1)
                    v = lkv[J % 3]
                    nc.tensor.matmul(ps_y[:, 0:P], lpt[s][:, 0:P], v[:, 0, P:TOK], start=True, stop=True)
                    nc.tensor.matmul(ps_y[:, P:TOK], lpt[s][:, P:TOK], v[:, 0, P:TOK],
                                     start=True, stop=False)
                    nc.tensor.matmul(ps_y[:, P:TOK], lpt[s][:, TOK:H3], v[:, 1, P:TOK],
                                     start=False, stop=True).then_inc(l_y_ps, 1)
            for n in range(4):
                for h in range(2):
                    if p == GATED + 8 * n + 2 * h:
                        pe.wait_ge(l_tile, n + 1)
                        pe.wait_ge(turn_lo, 2 * (TURN["oy"] + n) + h + 2)
                        pe.wait_ge(l_qk, min(p // 2 + 1, 16))
                        for c in range(2):
                            for t in range(TH):
                                at = n * NBW + (2 * h + c) * P
                                mm = nc.tensor.transpose(turn[0][:, (c * TH + t) * P:(c * TH + t + 1) * P],
                                                         ybuf[:, t, at:at + P], ident[:, :])
                        mm.then_inc(turned, 1)

        for b in range(4):
            n = B0["zc"] + b
            pe.wait_ge(sums_out, n + 1)
            for k in range(8):
                latent_heads(8 * b + k)
                unit(At(U0["zc"] + 8 * b + k), x_t, UCH * k, n % 2, k == 0, k == 7)
        pe.wait_ge(m_lo, 9)
        for b in range(4):
            n = B0["oout"] + b
            pe.wait_ge(sums_out, n + 1)
            for k in range(10):
                if b == 0:
                    latent_heads(32 + k)
                    if k >= 2:
                        pe.wait_ge(turn_lo, 2 * TURN["oy"] + k - 1 + 2)
                unit(At(U0["oout"] + 10 * b + k), o_t, (16 + UCH * k) % 20, n % 2, k == 0, k == 9)

    @block.scalar
    def _(act):
        def split(u):
            act.wait_ge(raw_landed[u.slot], u.landed())
            act.wait_ge(unit_used, u.times(1, 1))
            nc.scalar.activation(w_hi[:, u.slot, :], raw[:, u.slot, :], ACT.Copy).then_inc(hi_ready, 1)

        def splits(stage, units, first, i, per, hook=None):
            for k in range(units):
                if hook:
                    hook(k)
                split(At(U0[stage] + first + k + LEAD, i, per))

        def summed(u):
            act.wait_ge(unit_used, u.times(1, 1 + RING))

        def high(n, dst, b, g=None):
            for h in range(2):
                act.wait_ge(turned, n.times(2, h + 1))
                if g is None:
                    at = dst[0][:, bass.ds(b.times(4, 2 * h), 2), :].rearrange("p c t -> p (c t)")
                    last = nc.scalar.activation(at, turn[h][:, :], ACT.Copy)
                else:
                    for c in range(2):
                        at = dst[0][:, bass.ds(b.times(4, 2 * h + c), 1), :].rearrange("p c t -> p (c t)")
                        last = nc.scalar.activation(at, turn[h][:, c * TOK:(c + 1) * TOK], ACT.Copy,
                                                    scale=gain[:, bass.ds(b.times(4, 2 * h + c + g), 1)])
                last.then_inc(turn_hi, 1)

        def square(src, col, b, count):
            if count is not None:
                act.wait_ge(squared, count)
            for t in range(TH):
                last = nc.scalar.activation(junk[:, t * NBW:(t + 1) * NBW], src[:, t, :], ACT.Square,
                                            accum_out=stat[:, bass.ds(b.times(1, col + 4 * t), 1)])
            last.then_inc(squared, 1)

        def scale_out(u, s, stored, r):
            summed(u)
            act.wait_ge(tile_moved[s], stored)
            for t in range(TH):
                last = nc.scalar.activation(tile[s][:, t, :], acc[2 * s + t][:, :], ACT.Copy,
                                            scale=rstd[:, 2 * r + t:2 * r + t + 1])
            last.then_inc(sums_out, 1)

        act.sem_inc(at_qk, 1)
        act.sem_inc(m_qk, 1)
        act.wait_ge(pe_once, 1)
        nc.scalar.activation(gain[:, 0:122], ps_s[:, 0:122], ACT.Copy).then_inc(act_once, 1)
        act.wait_ge(pe_once, 2)
        nc.scalar.activation(col2[:, 0:24], ps_y[:, 0:24], ACT.Copy)
        nc.scalar.activation(col2[:, 24:144], ps_y[:, 24:144], ACT.Copy, scale=0.5).then_inc(act_once, 1)
        act.wait_ge(act_once, 2)
        for u in range(LEAD):
            split(At(u))
        for b in range(4):
            act.wait_ge(xin_landed[b % 2], 16 * (b // 2 + 1))
            square(xin[b % 2], 0, At(b), b or None)
            high(At(TURN["mem"] + b), mem_t, At(b), 0)
        with act.Fori(0, 2) as i:
            for b in range(2):
                splits("mem", 8, 8 * b, i, 16)
                act.wait_ge(rstd_ready, 1)
                act.wait_ge(e_built, 3)
                scale_out(At(8 * b + 7, i, 16), b, At(STORED["mem"], i, 1).times(16, 16), 0)
                act.wait_ge(xin_landed[b], At(LOADED["x"], i, 1).times(16, 16))
                square(xin[b], 8, At(b, i, 2), At(4 + b, i, 2).times(1))
                high(At(TURN["x"] + b, i, 2), x_t, At(b, i, 2), 16)
        act.wait_ge(rstd_ready, 2)
        with act.Fori(0, 6) as i:
            for b in range(2):
                splits("win", 8, 8 * b, i, 16)
                scale_out(At(U0["win"] + 8 * b + 7, i, 16), b, At(STORED["win"], i, 1).times(16, 16), 1)

        def attend(p, i):
            for j in range(4):
                J, m, s, kind = At(j, i, 4), At(j // 2, i, 2), j % 2, ("sb", "ca")[j % 2]
                if p == 3 * j:
                    act.wait_ge(at_qk_ps, J.times(1, 1))
                    act.wait_ge(at_scores, J.times(1, 1))
                    nc.scalar.activation(qk_t[s][:, :], turn[0][:, :], ACT.Copy).then_inc(at_qk, 1)
                if p == 3 * j + 1 and kind == "sb":
                    act.wait_ge(at_z, J.times(1, 2))
                    nc.scalar.activation(keep[:, :], z["sb"][:, :], ACT.Abs).then_inc(at_abs, 1)
                    act.wait_ge(at_abs, m.times(1, 1))
                    nc.scalar.activation(keep[:, :], keep[:, :], ACT.Exp, scale=-1.0).then_inc(at_exp0, 1)
                    act.wait_ge(at_exp0, m.times(1, 1))
                    nc.scalar.activation(keep[:, :], keep[:, :], ACT.Ln, bias=1.0).then_inc(at_keep, 1)
                if p == 3 * j + 2 and kind == "ca":
                    act.wait_ge(at_max, m.times(1, 1))
                    for x, w in enumerate((slice(0, P), slice(P, H3))):
                        last = nc.scalar.activation(prob["ca"][:, w], z["ca"][:, w], ACT.Exp,
                                                    bias=sm[:, x:x + 1], accum_out=sm[:, 2 + x:3 + x])
                    last.then_inc(at_exp, 1)
                if p == 3 * j + 3 and kind == "sb":
                    act.wait_ge(at_left, m.times(1, 1))
                    nc.scalar.activation(prob["sb"][:, :], left[:, :], ACT.Exp).then_inc(at_prob["sb"], 1)
                if p == 3 * j + 6:
                    act.wait_ge(at_y_ps, J.times(1, 3))
                    head = At(j // 2 + 8 * s, i, 2)
                    nc.scalar.activation(y_t[0][:, bass.ds(head.times(1), 1), :].rearrange("p c t -> p (c t)"),
                                         ps_y[:, 0:TOK], ACT.Copy).then_inc(at_y_hi, 1)

        with act.Fori(0, 4) as i:
            for b in range(2):
                splits("win", 8, 96 + 8 * b, i, 16, lambda k: attend(8 * b + k, i))
                scale_out(At(U0["win"] + 96 + 8 * b + 7, i, 16), b,
                          At(STORED["win"] + 6, i, 1).times(16, 16), 1)

        def open_gates(s, i):
            act.wait_ge(gates_in[s], At(0, i, 1).times(32, 32))
            g = gates[s][:, :, :, :].rearrange("p g t n -> p (g t n)")
            nc.scalar.activation(g, g, ACT.Sigmoid).then_inc(gates_sig, 1)

        with act.Fori(0, 2) as i:
            for b in range(2):
                splits("out", 8, 8 * b, i, 16, lambda k: open_gates(b, i) if k == 1 else None)
                high(At(TURN["mix"] + b, i, 2), m_t, At(b, i, 2))

        def residual(stage, units, turns, dst, g, col, count, ready, gate=None):
            with act.Fori(0, 2) as i:
                def tile_out(b):
                    act.wait_ge(*ready(b, i))
                    n = At(b, i, 2)
                    square(tile[b], col, n, n.times(1, count) if gate is None else n.times(2, count + 1))
                    high(At(turns + b, i, 2), dst, At(b, i, 2), g)
                for b in range(2):
                    splits(stage, units, b * units, i, 2 * units,
                           lambda k: tile_out(0) if (b, k) == (1, 3) else None)
                    if gate:
                        gate(b, At(U0[stage] + b * units + units - 1, i, 2 * units), At(b, i, 2))
                tile_out(1)

        def from_sums(stage):
            return lambda b, i: (sums_out, written(blk(stage, b, i)))

        residual("mix", 8, TURN["ffn"], x_t, 32, 16, 8, from_sums("mix"))
        act.wait_ge(rstd_ready, 3)
        with act.Fori(0, 11) as i:
            for b in range(2):
                splits("ffn", 8, 8 * b, i, 16)
                if b == 0:
                    summed(At(U0["ffn"] + 7, i, 16))
                    act.wait_ge(ff_half, At(0, i, 1).times(1, 1))
                    for t in range(TH):
                        r = rstd[:, 4 + t:5 + t]
                        nc.scalar.activation(g_half[:, t, :], acc[t][:, :], ACT.Copy, scale=r)
                        last = nc.scalar.activation(g_sig[:, t, :], acc[t][:, :], ACT.Sigmoid, scale=r)
                    last.then_inc(sums_out, 1)
            high(At(TURN["ffo"], i, 1), ff_t, At(0, i, 1))
        residual("ffo", 22, TURN["ple"], x_t, 48, 24, 12, from_sums("ffo"))

        act.wait_ge(pe_once, 3)
        nc.scalar.activation(ple_t[0][:, :, :].rearrange("p c t -> p (c t)"), ps_s[:, :], ACT.Copy)\
            .then_inc(act_once, 1)
        for b in range(4):
            split(At(U0["ple"] + b + LEAD))
            summed(At(U0["ple"] + b))
            for t in range(TH):
                last = nc.scalar.activation(pl_out[:, b, t, :], acc[2 * (b % 2) + t][:, :], ACT.Copy)
            last.then_inc(sums_out, 1)
        act.wait_ge(rstd_ready, 4)

        def ple_gate(b, u, n):
            summed(u)
            act.wait_ge(pl_mul, n.times(1, 1))
            for t in range(TH):
                last = nc.scalar.activation(pl_sig[:, t, :], acc[2 * b + t][:, :], ACT.Sigmoid,
                                            scale=rstd[:, 6 + t:7 + t])
            last.then_inc(sums_out, 1)
            act.wait_ge(pl_sum, n.times(1, 1))
            square(x_raw, 32, n, n.times(2, 16))

        residual("gate", 8, TURN["x3"], x3_t, 64, 40, 16,
                 lambda b, i: (tile_ready, At(4 + b, i, 2).times(1, 3)), ple_gate)

        def scaled(u, bank, slot, stored, scale):
            summed(u)
            act.wait_ge(tile_moved[slot], stored)
            for t in range(TH):
                last = nc.scalar.activation(tile[slot][:, t, :], acc[2 * bank + t][:, :], ACT.Copy,
                                            scale=scale[:, t:t + 1])
            last.then_inc(sums_out, 1)

        def mem_job(n, J, p, dst, chunk):
            _, qk_, pr_, pt_, y_, th_, sm_ = mbuf[n]
            qkv_ = mqkv[n][J.k % len(mqkv[n])]
            if p == 0:
                act.wait_ge(m_qk_ps, J.times(1, 1))
                nc.scalar.activation(qk_[:, :], turn[0][:, :], ACT.Copy).then_inc(m_qk, 1)
                nc.scalar.activation(th_[:, :, :], qkv_[:, 3, :, :], ACT.Tanh, scale=0.5)
            if p == 2:
                act.wait_ge(m_max2, J.times(1, 1))
                for t in range(TH):
                    last = nc.scalar.activation(pr_[:, t * TOK:(t + 1) * TOK], ps_s[:, t * TOK:(t + 1) * TOK],
                                                ACT.Exp, scale=SCALE, bias=sm_[:, t:t + 1],
                                                accum_out=sm_[:, 2 + t:3 + t])
                last.then_inc(m_exp, 1)
            if p == 7:
                act.wait_ge(m_yt_ps, J.times(1, 1))
                nc.scalar.activation(dst[0][:, bass.ds(chunk, 1), :].rearrange("p c t -> p (c t)"),
                                     ps_y[:, TOK:2 * TOK], ACT.Copy, scale=0.5).then_inc(m_hi, 1)

        act.wait_ge(small_in, 80)
        nc.scalar.activation(a_exp[:, :], rowb[:, 32:64], ACT.Exp).then_inc(act_once, 1)
        for b in range(2):
            splits("ein", 8, 8 * b, 0, 0)
            act.wait_ge(cc, 3)
            scaled(At(U0["ein"] + 8 * b + 7), b, b, 16 * (STORED["l2"] + 1), scal)
        with act.Fori(0, 4) as i:
            for b in range(2):
                splits("ein", 8, 16 + 8 * b, i, 16,
                       lambda k: mem_job(0, At(0, i, 1), 8 * b + k - 4, z_t, At(16, i, 1).times(1)))
                scaled(At(U0["ein"] + 16 + 8 * b + 7, i, 16), b, b, At(STORED["l2"] + 1, i, 1).times(16, 16), scal)
        for b in range(2):
            splits("ein", 8, 80 + 8 * b, 0, 0)
            scaled(At(U0["ein"] + 80 + 8 * b + 7), b, b, 16 * (STORED["l2"] + 6), scal)
        split(At(U0["dt"] + LEAD))
        act.wait_ge(dt_v, 1)
        nc.scalar.activation(dts[:, :], dtz[:, :], ACT.Abs).then_inc(act_once, 1)
        act.wait_ge(act_once, 5)
        nc.scalar.activation(dts[:, :], dts[:, :], ACT.Exp, scale=-1.0).then_inc(act_once, 1)
        act.wait_ge(act_once, 6)
        nc.scalar.activation(dts[:, :], dts[:, :], ACT.Ln, bias=1.0).then_inc(act_once, 1)
        act.wait_ge(dt_v, 5)
        nc.scalar.activation(d_end[:, :], d_end[:, :], ACT.Exp).then_inc(act_once, 1)
        nc.scalar.activation(e_ac[:, :], acum[:, 32:64], ACT.Exp).then_inc(act_once, 1)

        def ssd(p, i):
            n = At(0, i, 1)
            if p == 3:
                act.wait_ge(s_conv, n.times(4, 4))
                nc.scalar.activation(th[:, :], cv[:, :, :].rearrange("p c t -> p (c t)"), ACT.Tanh)\
                    .then_inc(s_th, 1)
            if p == 5:
                act.wait_ge(s_z, n.times(16, 16))
                nc.scalar.activation(zth[:, :, :], zt[:, :, :], ACT.Tanh, scale=0.5).then_inc(s_zth, 1)
                act.wait_ge(s_min, n.times(1, 1))
                nc.scalar.activation(dec[:, :, :], dec[:, :, :], ACT.Exp).then_inc(s_dec, 1)
            if p == 7:
                act.wait_ge(s_xt, n.times(1, 1))
                for t in range(TH):
                    last = nc.scalar.activation(xs[:, t, :], turn[t][:, :], ACT.Copy)
                last.then_inc(s_xs, 1)
            if p == 9:
                act.wait_ge(s_st, n.times(1, 1))
                nc.scalar.activation(st[:, :], ps_s[:, :], ACT.Copy).then_inc(s_state, 1)
            if p == 12:
                act.wait_ge(s_yg, n.times(1, 1))
                for t in range(TH):
                    last = nc.scalar.activation(zth[:, t, :], yb[:, t, :], ACT.Square,
                                                accum_out=g_ss[:, t:t + 1])
                last.then_inc(s_sq, 1)

        with act.Fori(0, 4) as i:
            for b in range(2):
                splits("sc", 8, 8 * b, i, 16, lambda k: ssd(8 * b + k, i))
                if b == 1:
                    high(At(TURN["sy"], i, 1), z_t, At(0, i, 1), 96)
                scaled(At(U0["sc"] + 8 * b + 7, i, 16), b, b, At(STORED["sc"], i, 1).times(16, 16), scal)

        def short(k, j):
            if k == 5 * j + 1:
                act.wait_ge(c_u, j + 1)
                nc.scalar.activation(sc_in[:, :, 2, :], sc_in[:, :, 3, :], ACT.Tanh, scale=0.5).then_inc(c_th, 1)
            if k == 5 * j + 5:
                act.wait_ge(c_y, j + 1)
                nc.scalar.activation(z_t[0][:, 20 + 4 * j:24 + 4 * j, :].rearrange("p c t -> p (c t)"),
                                     sc_y[:, :], ACT.Copy).then_inc(c_hi, 1)

        def eout_tile(b, i):
            act.wait_ge(sums_out, written(blk("eout", b, i)))
            n = At(b, i, 2)
            square(tile[b], 48, n, n.times(1, 24))
            high(At(TURN["x4"] + b, i, 2), x_t, n, 80)

        for i in range(2):
            for b in range(2):
                for k in range(14):
                    if i == 0 and b == 0:
                        for j in range(2):
                            short(k, j)
                    if (b, k) == (1, 3):
                        eout_tile(0, i)
                    split(At(U0["eout"] + 28 * i + 14 * b + k + LEAD))
            eout_tile(1, i)

        c4 = rstd[:, 12:14]
        for b in range(3):
            splits("olow", 8, 8 * b, 0, 0)
            act.wait_ge(rstd_ready, 7)
            summed(At(U0["olow"] + 8 * b + 7))
            bank = (B0["olow"] + b) % 2
            for t in range(TH):
                last = nc.scalar.activation(lat[:, t, 448 * b:448 * (b + 1)], acc[2 * bank + t][:, 0:448],
                                            ACT.Copy, scale=c4[:, t:t + 1])
            last.then_inc(sums_out, 1)
            if b == 1:
                act.wait_ge(r_step, 8)
                nc.scalar.activation(sinn[:, :, 0:32], ang[:, :, 0:32], ACT.Sin, scale=-1.0)
                nc.scalar.activation(sinn[:, :, 32:64], ang[:, :, 32:64], ACT.Sin)
                act.wait_ge(r_step, 12)
                nc.scalar.activation(cosn[:, :, :], ang3[:, :, :], ACT.Sin).then_inc(act_once, 1)
        act.wait_ge(sums_out, B0["olow"] + 2 + 3)
        for m, w in enumerate((slice(0, 768), slice(768, 1280))):
            for t in range(TH):
                at = (0, 768, 1536, 2048)[2 * m + t]
                last = nc.scalar.activation(lat_junk[:, at:at + w.stop - w.start], lat[:, t, w], ACT.Square,
                                            accum_out=stat[:, 56 + 2 * m + t:57 + 2 * m + t])
        last.then_inc(act_once, 1)

        def omem_beside(p):
            if p in (2, 4, 6, 8, 10):
                h = p // 2 - 1
                act.wait_ge(lat_ps, h + 1)
                for c in range(2):
                    last = nc.scalar.activation(lat_t[0][:, 2 * h + c, :], turn[h % 2][:, c * TOK:(c + 1) * TOK],
                                                ACT.Copy, scale=gain[:, 112 + 2 * h + c:113 + 2 * h + c])
                last.then_inc(lat_hi, 1)
            if p == 14:
                act.wait_ge(pe_once, 6)
                nc.scalar.activation(kr_t[:, :], ps_s[0:64, 0:TOK], ACT.Copy).then_inc(act_once, 1)

        for b in range(2):
            splits("omem", 8, 8 * b, 0, 0, lambda k: omem_beside(8 * b + k))
            scaled(At(U0["omem"] + 8 * b + 7), (B0["omem"] + b) % 2, b, 16 * (STORED["omem"] + 1), c4)
        act.wait_ge(lat_r, 2)
        for b in range(6):
            for k in range(3):
                p = 3 * b + k
                for j in range(4):
                    mem_job(1, At(4 + j), p - 7 * j - 5, o_t, 16 + j)
                split(At(U0["uq"] + p + LEAD))
            scaled(At(U0["uq"] + 3 * b + 2), (B0["uq"] + b) % 2, b % 2, 16 * (STORED["uq"] + b // 2 + 1),
                   rstd[:, 16:18])
        for b in range(8):
            for k in range(2):
                p = 2 * b + k
                for j in range(4):
                    mem_job(1, At(4 + j), 18 + p - 7 * j - 5, o_t, 16 + j)
                split(At(U0["ukv"] + p + LEAD))
            scaled(At(U0["ukv"] + 2 * b + 1), (B0["ukv"] + b) % 2, b % 2, 16 * (STORED["ukv"] + b // 2 + 1),
                   rstd[:, 18:20])

        def latent_heads(p):
            for J in range(16):
                s, q = J % 2, p - 2 * J
                if q == 0:
                    act.wait_ge(l_qk_ps, J + 1)
                    nc.scalar.activation(lqk[s][:, :], turn[0][:, :], ACT.Copy).then_inc(l_qk, 1)
                    act.wait_ge(l_qr_ps, J + 1)
                    nc.scalar.activation(lr[s][:, :], turn[1][0:64, 0:TOK], ACT.Copy).then_inc(l_qr, 1)
                if q == 1:
                    act.wait_ge(l_max, J + 1)
                    for x, w in enumerate((slice(0, P), slice(P, H3))):
                        last = nc.scalar.activation(lp[s][:, w], lz[s][:, w], ACT.Exp,
                                                    bias=lsm[:, 8 * s + x:8 * s + x + 1],
                                                    accum_out=lsm[:, 8 * s + 2 + x:8 * s + 3 + x])
                    last.then_inc(l_exp, 1)
            for n in range(4):
                for h in range(2):
                    if p == GATED + 8 * n + 2 * h:
                        act.wait_ge(turned, 2 * (TURN["oy"] + n) + h + 1)
                        w = slice(4 * n + 2 * h, 4 * n + 2 * h + 2)
                        nc.scalar.activation(o_t[0][:, w, :].rearrange("p c t -> p (c t)"), turn[0][:, :],
                                             ACT.Copy).then_inc(turn_hi, 1)

        act.wait_ge(cc, 4)
        for n in range(4):
            b = n % 2
            splits("zc", 8, 8 * n, 0, 0, lambda k: latent_heads(8 * n + k))
            summed(At(U0["zc"] + 8 * n + 7))
            act.wait_ge(tile_moved[b], 16 * (STORED["oout"] + 1))
            if n:
                act.wait_ge(l_zs, n)
            if n >= 2:
                act.wait_ge(l_tile, n - 1)
            bank = (B0["zc"] + n) % 2
            for t in range(TH):
                nc.scalar.activation(tile[b][:, t, :], acc[2 * bank + t][:, :], ACT.Copy, scale=c4[:, t:t + 1])
                last = nc.scalar.activation(zgt[:, t, :], acc[2 * bank + t][:, :], ACT.Tanh,
                                            scale=scal[:, t:t + 1])
            last.then_inc(sums_out, 1)
        for b in range(4):
            splits("oout", 10, 10 * b, 0, 0, lambda k: latent_heads(32 + k) if b == 0 else None)
            act.wait_ge(sums_out, B0["oout"] + b + 3)
            square(res[:, b, :, :], 0, At(b), 28 + b)

    @block.vector
    def _(dve):
        def split(u):
            dve.wait_ge(hi_ready, u.times(1, 1))
            s = u.slot
            nc.vector.tensor_tensor(w_lo[:, s, :], raw[:, s, :], w_hi[:, s, :].bitcast(F32),
                                    ALU.subtract).then_inc(lo_ready, 1)

        def splits(stage, units, first, i, per, hook=None):
            for k in range(units):
                if hook:
                    hook(k)
                split(At(U0[stage] + first + k + LEAD, i, per))

        def summed(u):
            dve.wait_ge(unit_used, u.times(1, 1 + RING))

        def low(n, dst, b, g=None):
            for h in range(2):
                dve.wait_ge(turn_hi, n.times(2, h + 1))
                if g is None:
                    w = bass.ds(b.times(4, 2 * h), 2)
                    last = nc.vector.tensor_tensor(
                        dst[1][:, w, :].rearrange("p c t -> p (c t)"), turn[h][:, :],
                        dst[0][:, w, :].rearrange("p c t -> p (c t)").bitcast(F32), ALU.subtract)
                else:
                    for c in range(2):
                        w = bass.ds(b.times(4, 2 * h + c), 1)
                        last = nc.vector.scalar_tensor_tensor(
                            out=dst[1][:, w, :].rearrange("p c t -> p (c t)"),
                            in0=turn[h][:, c * TOK:(c + 1) * TOK],
                            scalar=gain[:, bass.ds(b.times(4, 2 * h + c + g), 1)],
                            in1=dst[0][:, w, :].rearrange("p c t -> p (c t)").bitcast(F32),
                            op0=ALU.mult, op1=ALU.subtract)
                last.then_inc(turn_lo, 1)

        def mean_squares(r, col, count):
            dve.wait_ge(squared, count)
            nc.vector.tensor_reduce(total[:, 2 * r:2 * r + 2],
                                    stat[:, col:col + 8].rearrange("p (t b) -> p t b", t=TH),
                                    AX.X, ALU.add).then_inc(sum_ready, 1)
            dve.wait_ge(sum_ready, r + 1)

        def norm(r, col, count):
            mean_squares(r, col, count)
            nc.vector.tensor_scalar(mean[:, 2 * r:2 * r + 2], total[:, 2 * r:2 * r + 2], 1.0 / D, EPS,
                                    ALU.mult, ALU.add).then_inc(mean_ready, 1)

        dve.sem_inc(lo_ready, RING)
        dve.sem_inc(sums_out, 2)
        dve.sem_inc(tile_ready, 2)
        dve.sem_inc(turn_lo, 2)
        dve.sem_inc(at_z, 1)
        dve.sem_inc(at_pt, 1)
        dve.sem_inc(at_y_lo, 1)
        dve.sem_inc(ff_half, 1)
        dve.sem_inc(pl_mul, 1)
        dve.sem_inc(m_lo, 1)
        dve.sem_inc(lat_lo, 2)
        dve.sem_inc(l_z, 1)
        dve.sem_inc(l_pt, 2)
        dve.sem_inc(l_y, 1)
        nc.vector.memset(ones[:, :], 1.0).then_inc(ones_ready, 1)
        dve.wait_ge(act_once, 2)
        for u in range(LEAD):
            split(At(u))
        for b in range(4):
            low(At(TURN["mem"] + b), mem_t, At(b), 0)
        norm(0, 0, 4)
        dve.wait_ge(ones_ready, 1)
        rel = tile[1][0:8, 0, 0:N_REL]
        dve.wait_ge(tile_moved[1], 16)
        nc.vector.tensor_copy(e_rows[:, P - 1:P - 1 + N_REL], rel).then_inc(e_built, 1)
        nc.vector.tensor_scalar(e_rows[:, 0:P - 1], ones[0:8, 0:P - 1], rel[:, 0:1], None, ALU.mult)\
            .then_inc(e_built, 1)
        nc.vector.tensor_scalar(e_rows[:, P - 1 + N_REL:H3], ones[0:8, 0:H3 - N_REL - P + 1],
                                rel[:, N_REL - 1:N_REL], None, ALU.mult).then_inc(e_built, 1)
        with dve.Fori(0, 2) as i:
            for b in range(2):
                splits("mem", 8, 8 * b, i, 16)
                low(At(TURN["x"] + b, i, 2), x_t, At(b, i, 2), 16)
        norm(1, 8, 8)
        with dve.Fori(0, 6) as i:
            for b in range(2):
                splits("win", 8, 8 * b, i, 16)

        def attend(p, i):
            for j in range(4):
                J, m, s, kind = At(j, i, 4), At(j // 2, i, 2), j % 2, ("sb", "ca")[j % 2]
                if p == 3 * j + 1:
                    dve.wait_ge(at_scores, J.times(1, 3))
                    if kind == "sb":
                        more = past[:, :]
                    else:
                        more = bias[:, bass.ds(m.times(1), 1), :].rearrange("p h n -> p (h n)")
                    nc.vector.scalar_tensor_tensor(out=z[kind][:, :], in0=ps_s[:, 0:H3], scalar=SCALE,
                                                   in1=more, op0=ALU.mult, op1=ALU.add).then_inc(at_z, 1)
                    if kind == "ca":
                        dve.wait_ge(at_z, J.times(1, 2))
                        for x, w in enumerate((slice(0, P), slice(P, H3))):
                            last = nc.vector.tensor_reduce(sm[:, x:x + 1], z["ca"][:, w], AX.X, ALU.max,
                                                           negate=True)
                        last.then_inc(at_max, 1)
                if p == 3 * j + 2 and kind == "sb":
                    dve.wait_ge(at_keep, m.times(1, 1))
                    nc.vector.scalar_tensor_tensor(out=drop[:, :], in0=z["sb"][:, :], scalar=0.0,
                                                   in1=keep[:, :], op0=ALU.max, op1=ALU.add)\
                        .then_inc(at_drop, 1)
                    dve.wait_ge(at_drop, m.times(1, 1))
                    nc.vector.tensor_tensor_scan(left[:, P - 1::-1], ones[:, 0:P], drop[:, P - 1::-1], 0.0,
                                                 ALU.mult, ALU.add)
                    nc.vector.tensor_tensor_scan(left[:, H3 - 1:P - 1:-1], ones[:, :],
                                                 drop[:, H3 - 1:P - 1:-1], 0.0,
                                                 ALU.mult, ALU.add).then_inc(at_scan, 1)
                    dve.wait_ge(at_scan, m.times(1, 1))
                    nc.vector.tensor_tensor(left[:, :], z["sb"][:, :], left[:, :], ALU.subtract)\
                        .then_inc(at_left, 1)
                if p == 3 * j + 3 and kind == "ca":
                    dve.wait_ge(at_exp, m.times(1, 1))
                    nc.vector.reciprocal(sm[:, 4:6], sm[:, 2:4]).then_inc(at_inv, 1)
                    dve.wait_ge(at_inv, m.times(1, 1))
                    for x, w in enumerate((slice(0, P), slice(P, H3))):
                        last = nc.vector.tensor_scalar(prob["ca"][:, w], prob["ca"][:, w],
                                                       sm[:, 4 + x:5 + x], None, ALU.mult)
                    last.then_inc(at_prob["ca"], 1)
                if p == 3 * j + 5:
                    dve.wait_ge(at_pt_ps, J.times(1, 1))
                    nc.vector.tensor_copy(p_t[s][:, :], turn[1][:, 0:H3]).then_inc(at_pt, 1)
                if p == 3 * j + 6:
                    dve.wait_ge(at_y_hi, J.times(1, 1))
                    w = bass.ds(At(j // 2 + 8 * s, i, 2).times(1), 1)
                    nc.vector.tensor_tensor(
                        y_t[1][:, w, :].rearrange("p c t -> p (c t)"), ps_y[:, 0:TOK],
                        y_t[0][:, w, :].rearrange("p c t -> p (c t)").bitcast(F32),
                        ALU.subtract).then_inc(at_y_lo, 1)

        dve.wait_ge(mask_ready, 4)
        dve.wait_ge(bias_ready, 2)
        with dve.Fori(0, 4) as i:
            for b in range(2):
                splits("win", 8, 96 + 8 * b, i, 16, lambda k: attend(8 * b + k, i))

        for s in range(2):
            dve.wait_ge(tile_moved[s], 16 * (STORED["mix"] + 1))
        with dve.Fori(0, 2) as i:
            for n in range(2):
                for b in range(2):
                    splits("out", 4, 8 * n + 4 * b, i, 16)
                    if b == 0:
                        dve.wait_ge(gates_sig, At(n, i, 2).times(1, 1))
                    summed(At(U0["out"] + 8 * n + 4 * b + 3, i, 16))
                    for t in range(TH):
                        last = nc.vector.tensor_tensor(part[:, b, t, :], acc[2 * b + t][:, :],
                                                       gates[n][:, b, t, :], ALU.mult)
                    last.then_inc(sums_out, 1)
                dve.wait_ge(sums_out, written(blk("out", 2 * n + 1, i, 4)))
                dve.wait_ge(turned, At(TURN["mix"] + n, i, 2).times(2))
                nc.vector.tensor_tensor(tile[0][:, :, :], part[:, 0, :, :], part[:, 1, :, :], ALU.add)\
                    .then_inc(tile_ready, 1)
                low(At(TURN["mix"] + n, i, 2), m_t, At(n, i, 2))

        def residual(stage, units, turns, dst, g, body):
            with dve.Fori(0, 2) as i:
                for b in range(2):
                    splits(stage, units, b * units, i, 2 * units,
                           lambda k: low(At(turns, i, 2), dst, At(0, i, 2), g) if (b, k) == (1, 3) else None)
                    body(b, i, At(U0[stage] + b * units + units - 1, i, 2 * units))
                low(At(turns + 1, i, 2), dst, At(1, i, 2), g)

        def add_to(stage):
            def body(b, i, u):
                summed(u)
                dve.wait_ge(xin_landed[b], At(LOADED[stage], i, 1).times(16, 16))
                dve.wait_ge(tile_moved[b], At(STORED[stage], i, 1).times(16, 16))
                for t in range(TH):
                    last = nc.vector.tensor_tensor(tile[b][:, t, :], acc[2 * b + t][:, :],
                                                   xin[b][:, t, :], ALU.add)
                last.then_inc(sums_out, 1)
            return body

        residual("mix", 8, TURN["ffn"], x_t, 32, add_to("mix"))
        norm(2, 16, 12)
        dve.wait_ge(tile_moved[0], 16 * (STORED["ffo"] + 1))
        with dve.Fori(0, 11) as i:
            for b in range(2):
                splits("ffn", 8, 8 * b, i, 16)
                if b == 0:
                    dve.wait_ge(sums_out, written(blk("ffn", 0, i)))
                    nc.vector.tensor_tensor(g_half[:, :, :], g_half[:, :, :], g_sig[:, :, :], ALU.mult)\
                        .then_inc(ff_mul, 1)
            summed(At(U0["ffn"] + 15, i, 16))
            dve.wait_ge(ff_mul, At(0, i, 1).times(1, 1))
            dve.wait_ge(turned, At(TURN["ffo"], i, 1).times(2))
            for t in range(TH):
                last = nc.vector.scalar_tensor_tensor(out=tile[0][:, t, :], in0=acc[2 + t][:, :],
                                                      scalar=rstd[:, 4 + t:5 + t], in1=g_half[:, t, :],
                                                      op0=ALU.mult, op1=ALU.mult)
            last.then_inc(sums_out, 1)
            low(At(TURN["ffo"], i, 1), ff_t, At(0, i, 1))
            nc.vector.sem_inc(ff_half, 1)
        residual("ffo", 22, TURN["ple"], x_t, 48, add_to("ffo"))
        norm(3, 24, 16)

        dve.wait_ge(act_once, 3)
        nc.vector.tensor_tensor(ple_t[1][:, :, :].rearrange("p c t -> p (c t)"), ps_s[:, :],
                                ple_t[0][:, :, :].rearrange("p c t -> p (c t)").bitcast(F32),
                                ALU.subtract).then_inc(ple_lo, 1)
        for b in range(4):
            split(At(U0["ple"] + b + LEAD))
        dve.wait_ge(late_in, 32)

        def ple_add(b, i, u):
            n = At(b, i, 2)
            dve.wait_ge(sums_out, written(blk("gate", b, i)))
            dve.wait_ge(squared, n.times(2, 16))
            nc.vector.tensor_tensor(x_raw[:, :, :], pl_sig[:, :, :],
                                    pl_out[:, bass.ds(n.times(1), 1), :, :].rearrange("p a t n -> p (a t) n"),
                                    ALU.mult).then_inc(pl_mul, 1)
            dve.wait_ge(pl_mul, n.times(1, 2))
            dve.wait_ge(xin_landed[b], At(LOADED["gate"], i, 1).times(16, 16))
            nc.vector.tensor_tensor(x_raw[:, :, :], x_raw[:, :, :], xin[b][:, :, :], ALU.add)\
                .then_inc(pl_sum, 1)
            dve.wait_ge(pl_sum, n.times(1, 1))
            dve.wait_ge(tile_moved[b], At(STORED["gate"], i, 1).times(16, 16))
            for t in range(TH):
                last = nc.vector.tensor_tensor(tile[b][:, t, :], x_raw[:, t, :],
                                               gf_row[:, bass.ds(n.times(NBW), NBW)], ALU.mult)
            last.then_inc(tile_ready, 1)

        residual("gate", 8, TURN["x3"], x3_t, 64, ple_add)
        norm(4, 32, 24)

        def mem_job(n, J, p, dst, chunk):
            _, qk_, pr_, pt_, y_, th_, sm_ = mbuf[n]
            qkv_ = mqkv[n][J.k % len(mqkv[n])]
            if p == 1:
                dve.wait_ge(m_scores, J.times(1, 1))
                nc.vector.tensor_reduce(sm_[:, 0:2], ps_s[:, :].rearrange("p (t n) -> p t n", t=TH), AX.X,
                                        ALU.max, negate=True).then_inc(m_max, 1)
                dve.wait_ge(m_max, J.times(1, 1))
                nc.vector.tensor_scalar(sm_[:, 0:2], sm_[:, 0:2], SCALE, None, ALU.mult).then_inc(m_max2, 1)
            if p == 3:
                dve.wait_ge(m_exp, J.times(1, 1))
                nc.vector.reciprocal(sm_[:, 4:6], sm_[:, 2:4]).then_inc(m_inv, 1)
                nc.vector.scalar_tensor_tensor(out=qkv_[:, 3, :, :], in0=th_[:, :, :], scalar=1.0,
                                               in1=qkv_[:, 3, :, :], op0=ALU.add, op1=ALU.mult)\
                    .then_inc(m_zs, 1)
            if p == 4:
                dve.wait_ge(m_pt_ps, J.times(1, 1))
                nc.vector.tensor_copy(pt_[:, :], turn[1][:, :]).then_inc(m_pt, 1)
            if p == 5:
                dve.wait_ge(m_y_ps, J.times(1, 1))
                dve.wait_ge(m_inv, J.times(1, 1))
                dve.wait_ge(m_zs, J.times(1, 1))
                for t in range(TH):
                    last = nc.vector.scalar_tensor_tensor(out=y_[:, t, :], in0=ps_y[:, t * P:(t + 1) * P],
                                                          scalar=sm_[:, 4 + t:5 + t], in1=qkv_[:, 3, t, :],
                                                          op0=ALU.mult, op1=ALU.mult)
                last.then_inc(m_y, 1)
            if p == 7:
                dve.wait_ge(m_hi, J.times(1, 1))
                nc.vector.scalar_tensor_tensor(
                    out=dst[1][:, bass.ds(chunk, 1), :].rearrange("p c t -> p (c t)"),
                    in0=ps_y[:, TOK:2 * TOK], scalar=0.5,
                    in1=dst[0][:, bass.ds(chunk, 1), :].rearrange("p c t -> p (c t)").bitcast(F32),
                    op0=ALU.mult, op1=ALU.subtract).then_inc(m_lo, 1)

        dve.wait_ge(small_in, 80)
        mean_squares(5, 40, 24)
        dve.wait_ge(rstd_ready, 5)
        r3 = rstd[:, 8:10]
        nc.vector.tensor_tensor(mean[:, 10:12], total[:, 10:12], r3, ALU.mult).then_inc(cc, 1)
        dve.wait_ge(cc, 1)
        nc.vector.tensor_tensor(mean[:, 10:12], mean[:, 10:12], r3, ALU.mult).then_inc(cc, 1)
        dve.wait_ge(cc, 2)
        nc.vector.tensor_scalar(mean[:, 10:12], mean[:, 10:12], 1.0 / D, EPS, ALU.mult, ALU.add)\
            .then_inc(mean_ready, 1)
        dve.wait_ge(rstd_ready, 6)
        nc.vector.tensor_tensor(scal[:, :], rstd[:, 10:12], r3, ALU.mult).then_inc(cc, 1)
        splits("ein", 16, 0, 0, 0)
        with dve.Fori(0, 4) as i:
            splits("ein", 16, 16, i, 16, lambda k: mem_job(0, At(0, i, 1), k - 4, z_t, At(16, i, 1).times(1)))
        splits("ein", 16, 80, 0, 0)
        split(At(U0["dt"] + LEAD))
        summed(At(U0["dt"]))
        dve.wait_ge(cc, 3)
        for t in range(TH):
            last = nc.vector.scalar_tensor_tensor(out=dtz[:, 32 * t:32 * t + 32], in0=ps_y[:, 32 * t:32 * t + 32],
                                                  scalar=scal[:, t:t + 1], in1=rowb[:, 0:32],
                                                  op0=ALU.mult, op1=ALU.add)
        last.then_inc(dt_v, 1)
        dve.wait_ge(act_once, 7)
        nc.vector.scalar_tensor_tensor(out=dts[:, :], in0=dtz[:, :], scalar=0.0, in1=dts[:, :],
                                       op0=ALU.max, op1=ALU.add).then_inc(dt_v, 1)
        dve.wait_ge(dt_v, 2)
        for t in range(TH):
            last = nc.vector.scalar_tensor_tensor(out=d_a[:, 32 * t:32 * t + 32], in0=dts[:, 32 * t:32 * t + 32],
                                                  scalar=-1.0, in1=a_exp[:, :], op0=ALU.mult, op1=ALU.mult)
        last.then_inc(dt_v, 1)
        dve.wait_ge(pe_once, 4)
        nc.vector.tensor_copy(acum[:, :], ps_y[:, 64:128]).then_inc(dt_v, 1)
        dve.wait_ge(dt_v, 4)
        nc.vector.tensor_tensor(d_end[:, :], ps_y[:, 128:160], acum[:, 0:32], ALU.subtract).then_inc(dt_v, 1)
        dve.wait_ge(pe_once, 5)
        nc.vector.tensor_copy(ac_t[:, :], ps_s[0:64, 0:P]).then_inc(dt_v, 1)
        dve.wait_ge(act_once, 9)
        dve.wait_ge(mask_ready, 2)

        def per_head(a, n, width):
            return a.unsqueeze(2).to_broadcast([P, HG, width])

        def ssd(p, i):
            n = At(0, i, 1)
            if p in (0, 1, 2, 3):
                if p == 0:
                    dve.wait_ge(s_ut, n.times(1, 1))
                else:
                    dve.wait_ge(s_conv, n.times(4, p))
                for c in range(6):
                    bank = (turn[0], turn[1], ps_s)[c // 2]
                    u = bank[:, c % 2 * TOK:c % 2 * TOK + TOK - p]
                    ch = At(c, i, 4) if c < 4 else At(12 + 4 * (c - 4) + 4, i, 1)
                    w = col2[:, bass.ds(ch.times(1, 24 + 24 * (3 - p)), 1)]
                    if p == 0:
                        last = nc.vector.tensor_scalar(cv[:, c, :], u, w, col2[:, bass.ds(ch.times(1, 120), 1)],
                                                       ALU.mult, ALU.add)
                    else:
                        last = nc.vector.scalar_tensor_tensor(out=cv[:, c, p:], in0=u, scalar=w,
                                                              in1=cv[:, c, p:], op0=ALU.mult, op1=ALU.add)
                last.then_inc(s_conv, 1)
            if p == 4:
                dve.wait_ge(s_th, n.times(1, 1))
                c_ = cv[:, :, :].rearrange("p c t -> p (c t)")
                nc.vector.scalar_tensor_tensor(out=c_, in0=th[:, :], scalar=1.0, in1=c_,
                                               op0=ALU.add, op1=ALU.mult).then_inc(s_silu, 1)
            if p == 5:
                dve.wait_ge(s_ac, n.times(16, 16))
                for t in range(TH):
                    for h in range(HG):
                        d_ = dec[:, t, h * P:(h + 1) * P]
                        last = nc.vector.tensor_scalar(d_, d_, acum[:, bass.ds(At(32 * t + h, i, HG).times(1), 1)],
                                                       0.0, ALU.subtract, ALU.min)
                last.then_inc(s_min, 1)
            if p == 6:
                dve.wait_ge(s_zth, n.times(1, 1))
                nc.vector.scalar_tensor_tensor(out=zt[:, :, :], in0=zth[:, :, :], scalar=1.0, in1=zt[:, :, :],
                                               op0=ALU.add, op1=ALU.mult).then_inc(s_zs, 1)
            if p == 7:
                dve.wait_ge(s_cb, n.times(1, 1))
                nc.vector.tensor_copy(bm_t[:, :], ps_s[:, 0:P])
                for t in range(TH):
                    last = nc.vector.tensor_tensor(cbm[:, t, :], ps_s[:, (1 + t) * P:(2 + t) * P], tri[:, :],
                                                   ALU.mult)
                last.then_inc(s_cbm, 1)
            if p == 8:
                dve.wait_ge(s_xs, n.times(1, 1))
                for t in range(TH):
                    a = dts[:, bass.ds(At(32 * t, i, HG).times(1), HG)]
                    last = nc.vector.tensor_tensor(xdt[:, t, :].rearrange("p (h d) -> p h d", h=HG),
                                                   xs[:, t, :].rearrange("p (h d) -> p h d", h=HG),
                                                   per_head(a, i, SP_), ALU.mult)
                last.then_inc(s_xdt, 1)
                dve.wait_ge(s_xdt, n.times(1, 1))
                nc.vector.tensor_tensor(xde[:, :].rearrange("p (h d) -> p h d", h=HG),
                                        xdt[:, 0, :].rearrange("p (h d) -> p h d", h=HG),
                                        per_head(d_end[:, bass.ds(n.times(HG), HG)], i, SP_), ALU.mult)\
                    .then_inc(s_xde, 1)
            if p == 9:
                dve.wait_ge(s_dec, n.times(1, 1))
                for t in range(TH):
                    d_ = dec[:, t, :].rearrange("p (h q) -> p h q", h=HG)
                    last = nc.vector.tensor_tensor(d_, d_, cbm[:, t, :].unsqueeze(1).to_broadcast([P, HG, P]),
                                                   ALU.mult)
                last.then_inc(s_m, 1)
                for t in range(TH):
                    x_ = xs[:, t, :].rearrange("p (h d) -> p h d", h=HG)
                    last = nc.vector.tensor_tensor(x_, x_, per_head(rowb[:, bass.ds(n.times(HG, 64), HG)], i, SP_),
                                                   ALU.mult)
                last.then_inc(s_xd, 1)
            if p == 11:
                dve.wait_ge(s_y, n.times(1, 1))
                dve.wait_ge(s_xd, n.times(1, 1))
                for t in range(TH):
                    nc.vector.tensor_tensor(yb[:, t, :], turn[t][:, :], xs[:, t, :], ALU.add)
                nc.vector.tensor_tensor(xdt[:, 1, :].rearrange("p (h d) -> p h d", h=HG),
                                        ps_y[:, :].rearrange("p (h d) -> p h d", h=HG),
                                        per_head(e_ac[:, bass.ds(n.times(HG), HG)], i, SP_), ALU.mult)\
                    .then_inc(s_ya, 1)
                dve.wait_ge(s_ya, n.times(1, 1))
                nc.vector.tensor_tensor(yb[:, 1, :], yb[:, 1, :], xdt[:, 1, :], ALU.add).then_inc(s_yb, 1)
            if p == 12:
                dve.wait_ge(s_zs, n.times(1, 1))
                dve.wait_ge(s_yb, n.times(1, 1))
                nc.vector.scalar_tensor_tensor(out=yb[:, :, :], in0=yb[:, :, :], scalar=0.5, in1=zt[:, :, :],
                                               op0=ALU.mult, op1=ALU.mult).then_inc(s_yg, 1)
            if p == 13:
                dve.wait_ge(s_sq, n.times(1, 1))
                nc.vector.tensor_scalar(g_ms[:, :], g_ss[:, :], 1.0 / NBW, EPS, ALU.mult, ALU.add)\
                    .then_inc(s_gm, 1)
            if p == 14:
                dve.wait_ge(s_gr, n.times(1, 1))
                for t in range(TH):
                    last = nc.vector.tensor_scalar(yb[:, t, :], yb[:, t, :], g_r[:, t:t + 1], None, ALU.mult)
                last.then_inc(s_tile, 1)

        with dve.Fori(0, 4) as i:
            splits("sc", 16, 0, i, 16, lambda k: ssd(k, i))
            low(At(TURN["sy"], i, 1), z_t, At(0, i, 1), 96)

        def short(k, j):
            if k == 5 * j:
                dve.wait_ge(c_in, 32 * (j + 1))
                nc.vector.tensor_tensor(sc_in[:, :, 1, :], sc_in[:, :, 1, :], sc_in[:, :, 2, :], ALU.mult)\
                    .then_inc(c_u, 1)
            if k == 5 * j + 2:
                dve.wait_ge(c_th, j + 1)
                nc.vector.scalar_tensor_tensor(out=sc_in[:, :, 3, :], in0=sc_in[:, :, 2, :], scalar=1.0,
                                               in1=sc_in[:, :, 3, :], op0=ALU.add, op1=ALU.mult)\
                    .then_inc(c_zs, 1)
                dve.wait_ge(c_zs, j + 1)
                nc.vector.scalar_tensor_tensor(out=sc_in[:, :, 0, :], in0=sc_in[:, :, 3, :], scalar=0.5,
                                               in1=sc_in[:, :, 0, :], op0=ALU.mult, op1=ALU.mult)\
                    .then_inc(c_w, 1)
            if k == 5 * j + 4:
                dve.wait_ge(c_ut, 2 * j + 2)
                for tap in (2, 1, 0):
                    back = 2 - tap
                    if back:
                        dve.wait_ge(c_conv, 3 * j + back)
                    for c in range(4):
                        u = turn[c // 2][:, c % 2 * TOK:c % 2 * TOK + TOK - back]
                        w = col2[:, 8 * tap + 4 * j + c:8 * tap + 4 * j + c + 1]
                        if back == 0:
                            last = nc.vector.tensor_scalar(sc_cv[:, c, :], u, w, None, ALU.mult)
                        else:
                            last = nc.vector.scalar_tensor_tensor(
                                out=sc_cv[:, c, back:], in0=u, scalar=w, in1=sc_cv[:, c, back:],
                                op0=ALU.mult, op1=ALU.add)
                    last.then_inc(c_conv, 1)
                dve.wait_ge(c_wt, 2 * j + 2)
                dve.wait_ge(c_conv, 3 * j + 3)
                for h in range(2):
                    last = nc.vector.tensor_tensor(
                        sc_y[:, 2 * h * TOK:2 * (h + 1) * TOK], (ps_s, ps_y)[h][:, :],
                        sc_cv[:, 2 * h:2 * h + 2, :].rearrange("p c t -> p (c t)"), ALU.mult)
                last.then_inc(c_y, 1)
            if k == 5 * j + 5:
                dve.wait_ge(c_hi, j + 1)
                w = slice(20 + 4 * j, 24 + 4 * j)
                nc.vector.tensor_tensor(z_t[1][:, w, :].rearrange("p c t -> p (c t)"), sc_y[:, :],
                                        z_t[0][:, w, :].rearrange("p c t -> p (c t)").bitcast(F32),
                                        ALU.subtract).then_inc(c_lo, 1)

        for i in range(2):
            for b in range(2):
                for k in range(14):
                    if i == 0 and b == 0:
                        for j in range(2):
                            short(k, j)
                    if (b, k) == (1, 3):
                        low(At(TURN["x4"], i, 2), x_t, At(0, i, 2), 80)
                    split(At(U0["eout"] + 28 * i + 14 * b + k + LEAD))
                summed(At(U0["eout"] + 28 * i + 14 * b + 13))
                dve.wait_ge(xin_landed[b], 16 * (LOADED["eout"] + i + 1))
                dve.wait_ge(tile_moved[b], 16 * (STORED["eout"] + i + 1))
                bank = (B0["eout"] + b) % 2
                for t in range(TH):
                    last = nc.vector.scalar_tensor_tensor(out=tile[b][:, t, :], in0=xin[b][:, t, :],
                                                          scalar=rstd[:, 8 + t:9 + t], in1=acc[2 * bank + t][:, :],
                                                          op0=ALU.mult, op1=ALU.add)
                last.then_inc(sums_out, 1)
            low(At(TURN["x4"] + 1, i, 2), x_t, At(1, i, 2), 80)
        norm(6, 48, 28)

        def tables(k):
            if k == 0:
                nc.vector.tensor_copy(posf[:, :], posi[:, :]).then_inc(r_step, 1)
                dve.wait_ge(r_step, 1)
                for t in range(TH):
                    for h in range(2):
                        last = nc.vector.tensor_scalar(ang[:, t, 32 * h:32 * h + 32], inv[:, :],
                                                       posf[:, t:t + 1], None, ALU.mult)
                last.then_inc(r_step, 1)
            if k == 1:
                dve.wait_ge(r_step, 2)
                nc.vector.tensor_scalar(ang2[:, :, :], ang[:, :, :], 1.0 / (2.0 * PI), ROUND, ALU.mult, ALU.add)\
                    .then_inc(r_step, 1)
                dve.wait_ge(r_step, 3)
                nc.vector.tensor_scalar(ang2[:, :, :], ang2[:, :, :], ROUND, None, ALU.subtract)\
                    .then_inc(r_step, 1)
            if k == 2:
                for m, part_ in enumerate(TWO_PI):
                    dve.wait_ge(r_step, 4 + m)
                    nc.vector.scalar_tensor_tensor(out=ang[:, :, :], in0=ang2[:, :, :], scalar=-part_,
                                                   in1=ang[:, :, :], op0=ALU.mult, op1=ALU.add)\
                        .then_inc(r_step, 1)
            if k == 3:
                dve.wait_ge(r_step, 7)
                nc.vector.tensor_scalar(ang[:, :, :], ang[:, :, :], PI_IN, -PI_IN, ALU.min, ALU.max)\
                    .then_inc(r_step, 1)
                dve.wait_ge(r_step, 8)
                nc.vector.tensor_scalar(ang3[:, :, :], ang[:, :, :], PI / 2, -2.0 * PI, ALU.is_gt, ALU.mult)\
                    .then_inc(r_step, 1)
            if k == 4:
                dve.wait_ge(r_step, 9)
                nc.vector.scalar_tensor_tensor(out=ang3[:, :, :], in0=ang3[:, :, :], scalar=PI / 2,
                                               in1=ang[:, :, :], op0=ALU.add, op1=ALU.add).then_inc(r_step, 1)
                dve.wait_ge(r_step, 10)
                nc.vector.tensor_scalar(ang3[:, :, :], ang3[:, :, :], PI_IN, -PI_IN, ALU.min, ALU.max)\
                    .then_inc(r_step, 2)

        splits("olow", 24, 0, 0, 0, tables)
        dve.wait_ge(act_once, 10)
        dve.wait_ge(sums_out, B0["olow"] + 2 + 3)
        for h in range(2):
            last = nc.vector.tensor_tensor(ang2[:, :, 32 * h:32 * h + 32],
                                           lat[:, :, 1312 - 32 * h:1344 - 32 * h],
                                           sinn[:, :, 32 * h:32 * h + 32], ALU.mult)
        nc.vector.tensor_tensor(kr[:, :, :], lat[:, :, 1280:1344], cosn[:, :, :], ALU.mult).then_inc(r_step, 1)
        dve.wait_ge(r_step, 13)
        nc.vector.tensor_tensor(kr[:, :, :], kr[:, :, :], ang2[:, :, :], ALU.add).then_inc(r_kr, 1)
        nc.vector.tensor_scalar(scal[:, :], rstd[:, 12:14], 0.5, None, ALU.mult).then_inc(cc, 1)
        dve.wait_ge(act_once, 11)
        for m, width in enumerate((768, 512)):
            nc.vector.tensor_scalar(mean[:, 16 + 2 * m:18 + 2 * m], stat[:, 56 + 2 * m:58 + 2 * m],
                                    1.0 / width, EPS, ALU.mult, ALU.add).then_inc(lat_ms, 1)

        def omem_beside(p):
            if p in (2, 4, 6, 8, 10):
                h = p // 2 - 1
                dve.wait_ge(lat_hi, h + 1)
                for c in range(2):
                    last = nc.vector.scalar_tensor_tensor(
                        out=lat_t[1][:, 2 * h + c, :], in0=turn[h % 2][:, c * TOK:(c + 1) * TOK],
                        scalar=gain[:, 112 + 2 * h + c:113 + 2 * h + c],
                        in1=lat_t[0][:, 2 * h + c, :].bitcast(F32), op0=ALU.mult, op1=ALU.subtract)
                last.then_inc(lat_lo, 1)

        splits("omem", 16, 0, 0, 0, omem_beside)
        for p in range(18):
            for j in range(4):
                mem_job(1, At(4 + j), p - 7 * j - 5, o_t, 16 + j)
            split(At(U0["uq"] + p + LEAD))
        for p in range(16):
            for j in range(4):
                mem_job(1, At(4 + j), 18 + p - 7 * j - 5, o_t, 16 + j)
            split(At(U0["ukv"] + p + LEAD))

        def rotate(J):
            q_ = lq[J % 3]
            dve.wait_ge(at_loaded[J % 3], AT_LOADS + 32 * (J // 3 + 1))
            for h in range(2):
                last = nc.vector.tensor_tensor(rswap[:, :, 32 * h:32 * h + 32],
                                               q_[:, :, P + 32 * (1 - h):P + 32 * (2 - h)],
                                               sinn[:, :, 32 * h:32 * h + 32], ALU.mult)
            last.then_inc(l_rp, 1)
            dve.wait_ge(l_rp, 2 * J + 1)
            nc.vector.tensor_tensor(q_[:, :, P:192], q_[:, :, P:192], cosn[:, :, :], ALU.mult).then_inc(l_rp, 1)
            dve.wait_ge(l_rp, 2 * J + 2)
            nc.vector.tensor_tensor(q_[:, :, P:192], q_[:, :, P:192], rswap[:, :, :], ALU.add).then_inc(l_rot, 1)

        def latent_heads(p):
            for J in range(16):
                s, q = J % 2, p - 2 * J
                sums = lsm[:, 8 * s:8 * s + 8]
                if q == 1:
                    dve.wait_ge(l_scores, J + 1)
                    nc.vector.scalar_tensor_tensor(out=lz[s][:, :], in0=ps_s[:, 0:H3], scalar=L_SCALE,
                                                   in1=causal[:, :], op0=ALU.mult, op1=ALU.add).then_inc(l_z, 1)
                    dve.wait_ge(l_z, J + 2)
                    for x, w in enumerate((slice(0, P), slice(P, H3))):
                        last = nc.vector.tensor_reduce(sums[:, x:x + 1], lz[s][:, w], AX.X, ALU.max, negate=True)
                    last.then_inc(l_max, 1)
                if q == 2:
                    dve.wait_ge(l_exp, J + 1)
                    nc.vector.reciprocal(sums[:, 4:6], sums[:, 2:4]).then_inc(l_inv, 1)
                if q == 3:
                    dve.wait_ge(l_pt_ps, J + 1)
                    nc.vector.tensor_copy(lpt[s][:, :], turn[1][:, 0:H3]).then_inc(l_pt, 1)
                if q == 4:
                    dve.wait_ge(l_y_ps, J + 3)
                    dve.wait_ge(l_inv, J + 1)
                    for t in range(TH):
                        last = nc.vector.tensor_scalar(ybuf[:, t, J * P:(J + 1) * P],
                                                       ps_y[:, t * P:(t + 1) * P], sums[:, 4 + t:5 + t], None,
                                                       ALU.mult)
                    last.then_inc(l_y, 1)
            if p % 2 == 1 and (p + 1) // 2 < 16:
                rotate((p + 1) // 2)
            for n in range(4):
                if p == GATED + 8 * n - 2:
                    dve.wait_ge(l_y, 4 * n + 5)
                    dve.wait_ge(l_zs, n + 1)
                    y_ = ybuf[:, :, n * NBW:(n + 1) * NBW]
                    nc.vector.scalar_tensor_tensor(out=y_, in0=tile[n % 2][:, :, :], scalar=0.5, in1=y_,
                                                   op0=ALU.mult, op1=ALU.mult).then_inc(l_tile, 1)
                for h in range(2):
                    if p == GATED + 8 * n + 2 * h:
                        dve.wait_ge(turn_hi, 2 * (TURN["oy"] + n) + h + 1)
                        w = slice(4 * n + 2 * h, 4 * n + 2 * h + 2)
                        nc.vector.tensor_tensor(o_t[1][:, w, :].rearrange("p c t -> p (c t)"), turn[0][:, :],
                                                o_t[0][:, w, :].rearrange("p c t -> p (c t)").bitcast(F32),
                                                ALU.subtract).then_inc(turn_lo, 1)

        dve.wait_ge(mask_ready, 7)
        rotate(0)
        for n in range(4):
            splits("zc", 8, 8 * n, 0, 0, lambda k: latent_heads(8 * n + k))
            dve.wait_ge(sums_out, B0["zc"] + n + 3)
            nc.vector.scalar_tensor_tensor(out=tile[n % 2][:, :, :], in0=zgt[:, :, :], scalar=1.0,
                                           in1=tile[n % 2][:, :, :], op0=ALU.add, op1=ALU.mult).then_inc(l_zs, 1)
        for b in range(4):
            splits("oout", 10, 10 * b, 0, 0, lambda k: latent_heads(32 + k) if b == 0 else None)
            summed(At(U0["oout"] + 10 * b + 9))
            dve.wait_ge(xin_landed[b % 2], 16 * (LOADED["oout"] + b // 2 + 1))
            bank = (B0["oout"] + b) % 2
            for t in range(TH):
                last = nc.vector.tensor_tensor(res[:, b, t, :], acc[2 * bank + t][:, :], xin[b % 2][:, t, :],
                                               ALU.add)
            last.then_inc(sums_out, 1)
        norm(7, 0, 32)
        dve.wait_ge(rstd_ready, 8)
        dve.wait_ge(late_in, 48)
        for b in range(4):
            for t in range(TH):
                last = nc.vector.scalar_tensor_tensor(out=res[:, b, t, :], in0=res[:, b, t, :],
                                                      scalar=rstd[:, 14 + t:15 + t],
                                                      in1=fin[:, b * NBW:(b + 1) * NBW],
                                                      op0=ALU.mult, op1=ALU.mult)
            last.then_inc(fin_ready, 1)


def tiles_of(w, width=NBW):
    k, n = w.shape
    w = w.reshape(k // (UCH * P), UCH, P, n // width, width).transpose(3, 0, 2, 1, 4)
    return w.reshape(-1, P, UCH * width)


def kernel(**inputs):
    import numpy as np
    import concourse.bacc as bacc
    from concourse.bass_utils import run_bass_kernel_spmd as run
    a = {k: np.asarray(v) for k, v in inputs.items()}
    mem = np.concatenate([a[n] for n in ("mem_k0_2", "mem_v0_2", "mem_k1_2", "mem_v1_2")], axis=1)
    ffn = a["w_ffn_in"][0].reshape(D, 2, 11, NBW).transpose(0, 2, 1, 3).reshape(D, -1)
    sb, ca = (tiles_of(a[n][0]).reshape(4, 4, P, UW) for n in ("w_sb_out", "w_ca_out"))
    w0 = a["w_in0_2"]
    ein = np.concatenate([w0[:, 9248:EVW], w0[:, 6144:9216], w0[:, 4096:6144]], axis=1)
    dt = w0[:, 9216:9248].reshape(16, P, 32).transpose(1, 0, 2).reshape(1, P, -1)
    short = np.concatenate([w0[:, 1024 * m + NBW * j:1024 * m + NBW * (j + 1)]
                            for j in range(2) for m in range(4)], axis=1)
    out0 = np.concatenate([a["w_out0_2"][1024:], a["w_out0_2"][:1024]])
    w1 = a["w_in1_2"]
    out1 = np.concatenate([a["w_out1_2"][D:], a["w_out1_2"][:D]])
    units = [tiles_of(mem), tiles_of(a["w_in"][0]),
             np.stack([sb, ca], axis=1).reshape(-1, P, UW),
             tiles_of(a["w_mix_out"][0]), tiles_of(ffn), tiles_of(a["w_ffn_out"][0]),
             tiles_of(a["w_ple_in"][0]), tiles_of(a["w_ple_gate"][0]),
             tiles_of(ein), dt, tiles_of(short), tiles_of(out0),
             tiles_of(w1[:, :3 * OLW], OLW), tiles_of(w1[:, 3392:]), tiles_of(a["mla_w_uq_2"]),
             tiles_of(a["mla_w_ukv_2"]), tiles_of(w1[:, 3 * OLW:3392]), tiles_of(out1),
             np.zeros((LEAD, P, UW), np.float32)]
    stream = np.concatenate([np.pad(u, ((0, 0), (0, 0), (0, UW - u.shape[2]))) for u in units])
    gains = np.concatenate([a[n].reshape(-1, P) for n in (
        "mem_norm_w_2", "g_mix", "g_ffn", "g_ple", "norm0_w_2", "norm1_w_2", "ssd_norm_w_2",
        "mla_q_norm_w_2", "mla_kv_norm_w_2")])
    arrays = {
        "stream": stream, "gain_rows": gains, "x": a["x"][0], "mem": a["mem_2"][0], "p": a["p"][0, 0],
        "rel_bias": a["rel_bias"][0], "g_final": a["g_final"], "final_norm": a["final_norm_w_2"],
        "rows2": np.concatenate([a[n].reshape(-1, P) for n in ("sc_conv_w_2", "ssd_conv_w_2")]),
        "rows3": a["ssd_conv_b_2"].reshape(-1, P),
        "rowb": np.concatenate([a[n] for n in ("ssd_dt_bias_2", "ssd_a_log_2", "ssd_d_2")]),
        "inv": (10000.0 ** (-np.arange(32) / 32)).astype(np.float32), "positions": a["positions_2"].reshape(TH, P).T,
    }
    arrays = {k: np.ascontiguousarray(v) for k, v in arrays.items()}
    nc = bacc.Bacc("TRN2", target_bir_lowering=False, num_devices=1)
    io = {k: nc.dram_tensor(k, v.shape, I32 if k == "positions" else F32, kind="ExternalInput").ap()
          for k, v in arrays.items()}
    io["out"] = nc.dram_tensor("out", (TOK, D), F32, kind="ExternalOutput").ap()
    build(nc, io)
    r = run(nc, [arrays], core_ids=[0])
    return r.results[0]["out"].reshape(1, TOK, D)
```

```python
from contextlib import ExitStack

import numpy as np
import concourse.bass as bass
from concourse import mybir

F32 = mybir.dt.float32
F32R = mybir.dt.float32r
I32 = mybir.dt.int32
ALU = mybir.AluOpType
ACT = mybir.ActivationFunctionType
AX = mybir.AxisListType

P = 128
TOK = 256
TH = TOK // P
D = 2048
NBW = 512
UCH = 2
UW = UCH * NBW
RING = 4
LEAD = 3
D_FF = 5632
HD = 128
NEG = -1e30
EPS = 1e-6
SCALE = float(HD) ** -0.5
W_IN1 = 10240
EVW = 10272
REL_CLIP, CHUNK = 128, 64
N_REL = REL_CLIP + CHUNK
OLW = 448
L_SCALE = 192 ** -0.5
EOUT_ORDER = [(b, k) for ks in (range(10), range(10, 14)) for b in range(2) for k in ks]
TURN_AT = 3
GATED = 13
PI = float(np.pi)
PI_IN = 3.1415925
TWO_PI = (6.28125, 0.0019350051879882812, 3.019916050561733e-07)
ROUND = 12582912.0

STAGES = [
    ("mem", 4, 8), ("win", 20, 8), ("out", 8, 4), ("mix", 4, 8), ("ffn", 22, 8),
    ("ffo", 4, 22), ("ple", 4, 1), ("gate", 4, 8),
    ("ein", 10, 8), ("dt", 0, 1), ("ez", 2, 8), ("sc", 8, 8), ("eout", 4, 14),
    ("olow", 3, 8), ("omem", 2, 8), ("uq", 6, 3), ("ukv", 8, 2), ("zc", 4, 8), ("oout", 4, 10),
]
U0, B0 = {}, {}
_u = _b = 0
for _n, _nb, _ub in STAGES:
    U0[_n], B0[_n] = _u, _b
    _u += (_nb or 1) * _ub
    _b += _nb
N_UNITS = _u + LEAD


class At:

    def __init__(self, k, i=0, per=0):
        self.k, self.i, self.per = k, i, per

    def __add__(self, n):
        return At(self.k + n, self.i, self.per)

    def times(self, n, plus=0):
        if isinstance(self.i, int):
            return n * (self.k + self.i * self.per) + plus
        return self.i * (n * self.per) + (n * self.k + plus)

    @property
    def slot(self):
        return self.k % RING

    def landed(self):
        if isinstance(self.i, int):
            return 16 * ((self.k + self.i * self.per) // RING + 1)
        return self.i * (16 * self.per // RING) + 16 * (self.k // RING + 1)


def build(nc, io):
    ctx = ExitStack()
    with ctx:
        program(nc, io, ctx)


def program(nc, io, ctx):
    stream = io["stream"]
    base = (nc.sbuf_base + 63) // 64 * 64

    def place(name, shape, dt, at):
        return nc.alloc_sbuf_tensor_at(name, shape, dt, offset=base + at)

    def sem(name):
        return ctx.enter_context(nc.semaphore(name))

    def dram(name, shape):
        return nc.dram_tensor(name, shape, F32, kind="Internal").ap()

    K = 1024
    raw = place("raw", [P, RING, UW], F32, 0)
    w_hi = place("w_hi", [P, RING, UW], F32R, 16 * K)
    w_lo = place("w_lo", [P, RING, UW], F32R, 32 * K)
    AT, WD = 48 * K, 80 * K
    END = WD + 88 * K

    def pair(name, chunks, at):
        size = chunks * TOK * 4
        return (place(name + "_hi", [P, chunks, TOK], F32R, at),
                place(name + "_lo", [P, chunks, TOK], F32R, at + size))

    x_t = pair("x_t", 16, AT)
    mem_t = pair("mem_t", 16, WD)
    y_t = pair("y_t", 16, WD)
    m_t = pair("m_t", 16, WD + 32 * K)
    ff_t = pair("ff_t", 44, WD)
    ple_t = pair("ple_t", 2, END + 32 * K)
    x3_t = pair("x3_t", 16, WD)
    tile = [place(f"tile{s}", [P, TH, NBW], F32, END + 4 * K * s) for s in range(2)]
    xin = [place(f"xin{s}", [P, TH, NBW], F32, END + 8 * K + 4 * K * s) for s in range(2)]
    junk = place("junk", [P, TH * NBW], F32, END + 16 * K)
    ident = place("ident", [P, P], F32, END + 20 * K)
    gain = place("gain", [P, P], F32, END + 20 * K + 512)
    past = place("past", [P, 3 * P], F32, END + 21 * K)
    stat = place("stat", [P, 64], F32, END + 23 * K)
    rstd = place("rstd", [P, 64], F32, END + 23 * K + 256)
    expo = place("expo", [P, 2], F32, END + 23 * K + 512)
    total = place("total", [P, 32], F32, END + 23 * K + 576)
    mean = place("mean", [P, 32], F32, END + 23 * K + 704)
    T0 = WD + 32 * K
    qkv = [place(f"qkv{s}", [P, TH, 3, HD], F32, T0 + 3 * K * s if s < 2 else WD + 76 * K + 3 * K * (s - 2))
           for s in range(4)]
    qk_t = [place(f"qk_t{s}", [P, 2 * TOK], F32, T0 + 6 * K + 2 * K * s) for s in range(2)]
    H3 = 3 * P
    kinds = ("sb", "ca")
    z = {k: place(f"z_{k}", [P, H3], F32, T0 + 10 * K + 1536 * n) for n, k in enumerate(kinds)}
    prob = {k: place(f"prob_{k}", [P, H3], F32, T0 + 13 * K + 1536 * n) for n, k in enumerate(kinds)}
    keep = place("keep", [P, H3], F32, T0 + 16 * K)
    drop = place("drop", [P, H3], F32, T0 + 18 * K)
    left = place("left", [P, H3], F32, T0 + 20 * K)
    p_t = [place(f"p_t{s}", [P, H3], F32, T0 + 22 * K + 1536 * s) for s in range(2)]
    sm = place("sm", [P, 8], F32, T0 + 29 * K)
    e_rows = place("e_rows", [8, H3], F32, T0 + 30 * K)
    bias = place("bias", [P, 8, H3], F32, T0 + 32 * K)
    gates = [place(f"gates{s}", [P, 2, TH, NBW], F32, WD + 64 * K + 8 * K * s) for s in range(2)]
    part = place("part", [P, 2, TH, NBW], F32, WD + 80 * K)
    g_half = place("g_half", [P, TH, NBW], F32, END + 8 * K)
    g_sig = place("g_sig", [P, TH, NBW], F32, END + 12 * K)
    pl_row = place("pl_row", [P, TH, TOK], F32, END + 30 * K)
    pl_out = place("pl_out", [P, 4, TH, NBW], F32, WD + 40 * K)
    gf_row = place("gf_row", [P, D], F32, WD + 56 * K)
    pl_sig = place("pl_sig", [P, TH, NBW], F32, WD + 64 * K)
    x_raw = place("x_raw", [P, TH, NBW], F32, WD + 68 * K)

    z_t = pair("z_t", 28, WD + 32 * K)
    lat_t = pair("lat_t", 10, WD)
    o_t = pair("o_t", 20, WD + 20 * K)

    def row_of(at, *items):
        out = []
        for name, shape, dt in items:
            out.append(place(name, shape, dt, at))
            at += (int(np.prod(shape[1:])) * 4 + 31) // 32 * 32
        return out

    XT = END + 24 * K
    (col2, rowb, inv, posi, ones, tri, scal, posf, a_exp, dtz, dts, d_a, acum, e_ac, d_end, g_ss, g_ms, g_r,
     bm_t, cbm, zt, yb) = row_of(
        XT, ("col2", [P, 144], F32), ("rowb", [P, 96], F32), ("inv", [P, 32], F32), ("posi", [P, 2], I32),
        ("ones", [P, TOK], F32), ("tri", [P, P], F32), ("scal", [P, 2], F32), ("posf", [P, 2], F32), ("a_exp", [P, 32], F32),
        ("dtz", [P, 64], F32), ("dts", [P, 64], F32), ("d_a", [P, 64], F32), ("acum", [P, 64], F32),
        ("e_ac", [P, 32], F32), ("d_end", [P, 32], F32), ("g_ss", [P, 2], F32), ("g_ms", [P, 2], F32),
        ("g_r", [P, 2], F32), ("bm_t", [P, P], F32), ("cbm", [P, TH, P], F32),
        ("zt", [P, TH, NBW], F32), ("yb", [P, TH, NBW], F32))
    HG = 8
    SP_ = 64
    dec, u_in, cv, xs, xdt, xde, st = row_of(
        AT, ("dec", [P, TH, HG * P], F32), ("u_in", [P, TH, 768], F32), ("cv", [P, 6, TOK], F32),
        ("xs", [P, TH, NBW], F32), ("xdt", [P, TH, NBW], F32), ("xde", [P, NBW], F32), ("st", [P, NBW], F32))
    th = place("th", [P, 6 * TOK], F32, AT + 8 * K)
    zth = place("zth", [P, TH, NBW], F32, END + 16 * K)
    ac_t = place("ac_t", [64, P], F32, AT + 30 * K)
    mbuf = []
    for n, at in enumerate((AT, WD + 60 * K)):
        mbuf.append(row_of(at, *[(f"m{n}_{name}", shape, F32) for name, shape in (
            ("qkv", [P, 4, TH, HD]), ("qk_t", [P, 2 * TOK]), ("prob", [P, 2 * TOK]), ("p_t", [P, 2 * TOK]),
            ("y", [P, TH, HD]), ("th", [P, TH, HD]), ("sm", [P, 8]))]))
    mqkv = [[mbuf[0][0]], [mbuf[1][0], place("m1_qkv_b", [P, 4, TH, HD], F32, XT + 10 * K)]]
    sc_in, sc_cv, sc_y = row_of(AT, ("sc_in", [P, TH, 4, NBW], F32), ("sc_cv", [P, 4, TOK], F32),
                                ("sc_y", [P, 4 * TOK], F32))
    lat, = row_of(WD + 20 * K, ("lat", [P, TH, 1344], F32))
    ybuf, = row_of(WD, ("ybuf", [P, TH, D], F32))
    (kr, cosn, sinn, ang, ang2, ang3, lz0, lz1, lp0, lp1, lpt0, lpt1, kr_t) = row_of(
        WD + 73 * K, ("kr", [P, TH, 64], F32), ("cosn", [P, TH, 64], F32), ("sinn", [P, TH, 64], F32),
        ("ang", [P, TH, 64], F32), ("ang2", [P, TH, 64], F32), ("ang3", [P, TH, 64], F32),
        ("lz0", [P, H3], F32), ("lz1", [P, H3], F32), ("lp0", [P, H3], F32), ("lp1", [P, H3], F32),
        ("lpt0", [P, H3], F32), ("lpt1", [P, H3], F32), ("kr_t", [64, TOK], F32))
    lz, lp, lpt = (lz0, lz1), (lp0, lp1), (lpt0, lpt1)
    lq0, lq1, lkv0, lkv1, lqk0, lqk1 = row_of(
        XT + 3 * K, ("lq0", [P, TH, 192], F32), ("lq1", [P, TH, 192], F32),
        ("lkv0", [P, TH, 256], F32), ("lkv1", [P, TH, 256], F32),
        ("lqk0", [P, 2 * TOK], F32), ("lqk1", [P, 2 * TOK], F32))
    lq2 = place("lq2", [P, TH, 192], F32, XT + 14 * K)
    lkv2 = place("lkv2", [P, TH, 256], F32, WD + 86 * K)
    lq, lkv, lqk = (lq0, lq1, lq2), (lkv0, lkv1, lkv2), (lqk0, lqk1)
    lr0, lr1, lsm, rswap = row_of(
        WD + 60 * K, ("lr0", [64, TOK], F32), ("lr1", [64, TOK], F32),
        ("lsm", [P, 16], F32), ("rswap", [P, TH, 64], F32))
    lr = (lr0, lr1)
    causal = place("causal", [P, H3], F32, END + 21 * K)
    lat_junk = place("lat_junk", [P, 2560], F32, XT + 3 * K)
    zgt = place("zgt", [P, TH, NBW], F32, WD + 64 * K)
    res, fin = row_of(WD + 60 * K, ("res", [P, 4, TH, NBW], F32), ("fin", [P, D], F32))

    acc = [ctx.enter_context(nc.psum_tensor(f"acc{n}", [P, NBW], F32)) for n in range(4)]
    turn = [ctx.enter_context(nc.psum_tensor(f"turn{n}", [P, NBW], F32)) for n in range(2)]
    ps_s = ctx.enter_context(nc.psum_tensor("ps_s", [P, NBW], F32))
    ps_y = ctx.enter_context(nc.psum_tensor("ps_y", [P, NBW], F32))

    d_mem = dram("d_mem", (TOK, 4 * NBW))
    d_in = dram("d_in", (TOK, W_IN1))
    d_x = [dram(f"d_x{n}", (TOK, D)) for n in range(3)]
    d_e = dram("d_e", (8, 4 * P))
    d_skew = dram("d_skew", (P, 8, 4 * P))

    d_ev = dram("d_ev", (TOK, 10240))
    d_ac = dram("d_ac", (TH, 32 * P))
    d_x4 = dram("d_x4", (TOK, D))
    d_om = dram("d_om", (TOK, 2 * NBW))
    d_q = dram("d_q", (TOK, 3072))
    d_kv = dram("d_kv", (TOK, 4096))

    def halves(a):
        return a.rearrange("(t p) n -> p t n", p=P)

    raw_landed = [sem(f"raw_landed{s}") for s in range(RING)]
    hi_ready = sem("hi_ready")
    lo_ready = sem("lo_ready")
    unit_used = sem("unit_used")
    sums_out = sem("sums_out")
    tile_ready = sem("tile_ready")
    tile_moved = [sem(f"tile_moved{s}") for s in range(2)]
    xin_landed = [sem(f"xin_landed{s}") for s in range(2)]
    turned = sem("turned")
    turn_hi = sem("turn_hi")
    turn_lo = sem("turn_lo")
    squared = sem("squared")
    sum_ready = sem("sum_ready")
    mean_ready = sem("mean_ready")
    rstd_ready = sem("rstd_ready")
    zeroed = sem("zeroed")
    const_ready = sem("const_ready")
    mask_ready = sem("mask_ready")
    pe_once = sem("pe_once")
    act_once = sem("act_once")
    ones_ready = sem("ones_ready")
    e_built, e_out = sem("e_built"), sem("e_out")
    skewed = sem("skewed")
    bias_in, bias_ready = sem("bias_in"), sem("bias_ready")
    at_loaded = [sem(f"at_loaded{s}") for s in range(4)]
    AT_LOADS = 4 * 32
    at_qk_ps, at_qk = sem("at_qk_ps"), sem("at_qk")
    at_scores, at_z = sem("at_scores"), sem("at_z")
    at_abs, at_exp0, at_keep = sem("at_abs"), sem("at_exp0"), sem("at_keep")
    at_drop, at_scan, at_left = sem("at_drop"), sem("at_scan"), sem("at_left")
    at_max, at_exp, at_inv = sem("at_max"), sem("at_exp"), sem("at_inv")
    at_prob = {k: sem(f"at_prob_{k}") for k in ("sb", "ca")}
    at_pt_ps, at_pt = sem("at_pt_ps"), sem("at_pt")
    at_y_ps, at_y_hi, at_y_lo = sem("at_y_ps"), sem("at_y_hi"), sem("at_y_lo")
    gates_in = [sem(f"gates_in{s}") for s in range(2)]
    gates_sig = sem("gates_sig")
    ff_mul = sem("ff_mul")
    ff_half = sem("ff_half")
    ple_lo = sem("ple_lo")
    late_in = sem("late_in")
    pl_mul, pl_sum = sem("pl_mul"), sem("pl_sum")

    small_in = sem("small_in")
    cc = sem("cc")
    dt_v, dt_out = sem("dt_v"), sem("dt_out")
    m_loaded = [sem(f"m_loaded{s}") for s in range(2)]
    m_qk_ps, m_qk, m_scores, m_max, m_max2, m_exp, m_inv, m_pt_ps, m_pt = (
        sem(f"m_{n}") for n in ("qk_ps", "qk", "scores", "max", "max2", "exp", "inv", "pt_ps", "pt"))
    m_y_ps, m_zs, m_y, m_yt_ps, m_hi, m_lo = (
        sem(f"m_{n}") for n in ("y_ps", "zs", "y", "yt_ps", "hi", "lo"))
    s_tap = sem("s_tap")
    s_u, s_ac, s_z = sem("s_u"), sem("s_ac"), sem("s_z")
    s_ut, s_conv, s_th, s_silu, s_xt, s_cb = (sem(f"s_{n}") for n in ("ut", "conv", "th", "silu", "xt", "cb"))
    s_xs, s_cbm, s_xdt, s_xde, s_min = (sem(f"s_{n}") for n in ("xs", "cbm", "xdt", "xde", "min"))
    s_dec, s_st, s_state, s_m, s_xd, s_y = (sem(f"s_{n}") for n in ("dec", "st", "state", "m", "xd", "y"))
    s_ya, s_yb, s_zth, s_zs, s_yg, s_sq = (sem(f"s_{n}") for n in ("ya", "yb", "zth", "zs", "yg", "sq"))
    s_gm, s_gr, s_tile = (sem(f"s_{n}") for n in ("gm", "gr", "tile"))
    c_in, c_u, c_th, c_zs, c_w, c_ut, c_wt, c_conv, c_y, c_hi, c_lo = (
        sem(f"c_{n}") for n in ("in", "u", "th", "zs", "w", "ut", "wt", "conv", "y", "hi", "lo"))
    lat_ms, lat_r, lat_ps, lat_hi, lat_lo = (sem(f"lat_{n}") for n in ("ms", "r", "ps", "hi", "lo"))
    r_step, r_kr = sem("r_step"), sem("r_kr")
    l_rot, l_qk_ps, l_qr_ps, l_qk, l_qr, l_scores, l_z, l_max, l_exp, l_inv, l_pt_ps, l_pt, l_y_ps, l_y = (
        sem(f"l_{n}") for n in ("rot", "qk_ps", "qr_ps", "qk", "qr", "scores", "z", "max", "exp", "inv",
                                "pt_ps", "pt", "y_ps", "y"))
    l_rp = sem("l_rp")
    l_zs, l_tile = sem("l_zs"), sem("l_tile")
    fin_ready, fin_out = sem("fin_ready"), sem("fin_out")

    TURN = {"mem": 0, "x": 4, "mix": 8, "ffn": 12, "ffo": 16, "ple": 27, "x3": 31,
            "sy": 35, "x4": 39, "oy": 43}
    STORED = {"mem": 0, "win": 2, "mix": 12, "ffo": 14, "gate": 16, "l2": 18,
              "sc": 24, "eout": 28, "omem": 30, "uq": 31, "ukv": 34, "oout": 38}
    LOADED = {"mem": 0, "x": 2, "mix": 4, "ffo": 6, "gate": 8, "eout": 10, "oout": 12}

    def blk(stage, b, i=0, nb=2):
        return At(B0[stage] + b, i, nb)

    def written(b):
        return b.times(1, 3)

    block = ctx.enter_context(nc.Block())

    @block.sync
    def _(sp):
        def load(u):
            sp.wait_ge(lo_ready, u.times(1, 1))
            sp.dma_start(raw[:, u.slot, :], stream[bass.ds(u.times(1), 1), :, :].rearrange("a p n -> p (a n)"))\
              .then_inc(raw_landed[u.slot], 16)

        with sp.Fori(0, N_UNITS // RING) as i:
            for s in range(RING):
                load(At(s, i, RING))
        for u in range(N_UNITS // RING * RING, N_UNITS):
            load(At(u))

    @block.gpsimd
    def _(pool):
        def load_tile(src, b, slot, value):
            for s_, v_ in value:
                pool.wait_ge(s_, v_)
            pool.dma_start(xin[slot][:, :, :], src[:, :, bass.ds(b.times(NBW), NBW)])\
                .then_inc(xin_landed[slot], 16)

        def store_tile(dst, b, slot, s_, v_):
            pool.wait_ge(s_, v_)
            pool.dma_start(dst[:, :, bass.ds(b.times(NBW), NBW)], tile[slot][:, :, :])\
                .then_inc(tile_moved[slot], 16)

        def all_stored(count):
            for s in range(2):
                pool.wait_ge(tile_moved[s], 16 * (count + 1))

        pool.dma_start(tile[0][0:122, 0, 0:P], io["gain_rows"]).then_inc(tile_moved[0], 16)
        pool.dma_start(tile[1][0:8, 0, 0:N_REL], io["rel_bias"]).then_inc(tile_moved[1], 16)
        pool.dma_start(junk[0:120, 0:P], io["rows2"]).then_inc(small_in, 16)
        pool.dma_start(junk[0:24, P:2 * P], io["rows3"]).then_inc(small_in, 16)
        pool.dma_start(rowb[:, :], io["rowb"].partition_broadcast(P)).then_inc(small_in, 16)
        pool.dma_start(inv[:, :], io["inv"].partition_broadcast(P)).then_inc(small_in, 16)
        pool.dma_start(posi[:, :], io["positions"]).then_inc(small_in, 16)
        pool.dma_start(pl_row[:, :, :], halves(io["p"])).then_inc(late_in, 16)
        pool.memset(ident[:, :], 0.0).then_inc(zeroed, 1)
        pool.memset(past[:, :], 0.0).then_inc(zeroed, 1)
        pool.memset(expo[:, :], -0.5).then_inc(zeroed, 1)
        pool.wait_ge(zeroed, 1)
        pool.affine_select(out=ident[:, :], in_=ident[:, :], compare_op=ALU.not_equal, fill=1.0, base=0,
                           pattern=[[-1, P]], channel_multiplier=1).then_inc(const_ready, 1)
        mem_v, x_v, dx_v = halves(io["mem"]), halves(io["x"]), [halves(a) for a in d_x]
        for b in range(4):
            free = [(turned, 2 * b - 2), (squared, b - 1)] if b >= 2 else []
            load_tile(mem_v, At(b), b % 2, free)
        pool.memset(tri[:, :], 1.0).then_inc(mask_ready, 1)
        pool.wait_ge(mask_ready, 1)
        pool.affine_select(out=tri[:, :], in_=tri[:, :], compare_op=ALU.is_ge, fill=0.0, base=0,
                           pattern=[[1, P]], channel_multiplier=-1).then_inc(mask_ready, 1)
        pool.wait_ge(zeroed, 3)
        for at in (0, TOK):
            m = past[:, at:at + P]
            pool.affine_select(out=m, in_=m, compare_op=ALU.is_ge, fill=NEG, base=-1,
                               pattern=[[-1, P]], channel_multiplier=1).then_inc(mask_ready, 1)

        def norm(r):
            pool.wait_ge(mean_ready, r + 1)
            pool.tensor_tensor(rstd[:, 2 * r:2 * r + 2], mean[:, 2 * r:2 * r + 2], expo[:, :], ALU.pow)\
                .then_inc(rstd_ready, 1)

        norm(0)
        for b in range(2):
            load_tile(x_v, At(b), b, [(turned, 2 * b + 6), (squared, b + 3)])
        pool.wait_ge(e_built, 3)
        pool.dma_start(d_e[:, 0:H3], e_rows[:, :]).then_inc(e_out, 16)
        pool.wait_ge(e_out, 16)
        pool.dma_start(bass.AP(d_skew.tensor, 0, [[8 * 4 * P + 1, P], [4 * P, 8], [1, H3]]),
                       bass.AP(d_e.tensor, 0, [[0, P], [4 * P, 8], [1, H3]])).then_inc(skewed, 16)
        pool.wait_ge(skewed, 16)
        pool.dma_start(bias[:, :, 0:P], d_skew[:, :, TOK - 1:H3 - 1]).then_inc(bias_in, 16)
        pool.dma_start(bias[:, :, P:H3], d_skew[:, :, P - 1:H3 - 1]).then_inc(bias_in, 16)
        pool.wait_ge(bias_in, 32)
        pool.memset(bias[0:CHUNK, :, CHUNK:P], NEG).then_inc(bias_ready, 1)
        pool.memset(bias[0:CHUNK, :, H3 - CHUNK:H3], NEG).then_inc(bias_ready, 1)
        for b in range(4):
            store_tile(halves(d_mem), At(b), b % 2, sums_out, B0["mem"] + b + 3)
            if b < 2:
                load_tile(x_v, At(b + 2), b, [(turned, 2 * b + 10), (squared, b + 5)])
        norm(1)
        din_v = halves(d_in)
        with pool.Fori(0, 5) as i:
            for b in range(2):
                store_tile(din_v, At(b, i, 2), b, sums_out, written(blk("win", b, i)))
        heads = [halves(d_in[:, 3072 * k:3072 * (k + 1)]).rearrange("p t (m h d) -> p t m h d", m=3, h=8)
                 for k in range(2)]

        def load_head(j, J, m):
            if J is not None:
                pool.wait_ge(at_y_ps, J)
            for t in range(TH):
                src = heads[j % 2][:, t, :, bass.ds(m, 1), :].rearrange("p m h d -> p m (h d)")
                pool.dma_start(qkv[j][:, t, :, :], src).then_inc(at_loaded[j], 16)

        store_tile(din_v, At(10), 0, sums_out, written(blk("win", 10)))
        pool.wait_ge(tile_moved[1], 16 * (STORED["win"] + 5 + 1))
        pool.wait_ge(tile_moved[0], 16 * (STORED["win"] + 6 + 1))
        for j in range(4):
            load_head(j, None, j // 2)
        store_tile(din_v, At(11), 1, sums_out, written(blk("win", 11)))
        pool.wait_ge(tile_moved[1], 16 * (STORED["win"] + 6 + 1))

        def gate_pair(i, last):
            for j in range(4):
                if not last:
                    load_head(j, At(j, i, 4).times(1, 3), At(2 + j // 2, i, 2).times(1))
                if j == 0:
                    store_tile(din_v, At(12, i, 2), 0, sums_out, written(blk("win", 12, i)))
            if last:
                pool.wait_ge(at_z, 17)
                pool.wait_ge(tile_moved[0], 16 * (STORED["win"] + 9 + 1))
                load_gates(0, 0, None)
            store_tile(din_v, At(13, i, 2), 1, sums_out, written(blk("win", 13, i)))

        gate_v = d_in[:, 6144:].rearrange("(t p) (g n) -> p t g n", p=P, g=2)

        def load_gates(s, b, n):
            if n is not None:
                pool.wait_ge(tile_ready, n)
            for g in range(2):
                pool.dma_start(gates[s][:, g, :, :], gate_v[:, :, g, bass.ds(b, NBW)])\
                    .then_inc(gates_in[s], 16)

        with pool.Fori(0, 3) as i:
            gate_pair(i, False)
        gate_pair(3, True)
        pool.wait_ge(at_y_lo, 17)
        pool.wait_ge(tile_moved[1], 16 * (STORED["win"] + 9 + 1))
        load_gates(1, NBW, None)
        all_stored(STORED["mix"])
        for n in (2, 3):
            load_gates(n % 2, n * NBW, n + 1)

        def residual(stage, old, new, ready, base):
            for b in range(2):
                load_tile(old, At(b), b, [])
            for b in range(4):
                s_, v_ = ready(b)
                store_tile(new, At(b), b % 2, s_, v_)
                if b < 2:
                    load_tile(old, At(b + 2), b % 2, [])

        residual("mix", x_v, dx_v[0], lambda b: (sums_out, B0["mix"] + b + 3), 0)
        norm(2)
        all_stored(STORED["ffo"])
        pool.wait_ge(turned, 2 * (TURN["ffo"] + 10) + 1)
        residual("ffo", dx_v[0], dx_v[1], lambda b: (sums_out, B0["ffo"] + b + 3), 0)
        all_stored(STORED["gate"])
        pool.wait_ge(sums_out, B0["ffo"] + 3 + 3)
        pool.dma_start(gf_row[:, :], io["g_final"].partition_broadcast(P)).then_inc(late_in, 16)
        norm(3)
        residual("gate", dx_v[1], dx_v[2], lambda b: (tile_ready, 4 + b + 1 + 2), 0)
        norm(4)
        all_stored(STORED["l2"])
        norm(5)
        ev_v = halves(d_ev)
        mem_heads = [d_mem[:, 1024 * n:1024 * (n + 1)].rearrange("(t p) (m h d) -> p m t h d", p=P, m=2, h=4)
                     for n in range(2)]

        def load_mem(n, h, J, src):
            buf, landed = mqkv[n][J % len(mqkv[n])], m_loaded[J % len(mqkv[n])]
            for m in range(2):
                q = src[:, m * NBW:(m + 1) * NBW].rearrange("(t p) (h d) -> p t h d", p=P, h=4)
                pool.dma_start(buf[:, 3 * m, :, :], q[:, :, bass.ds(h, 1), :].rearrange("p t h d -> p t (h d)"))\
                    .then_inc(landed, 16)
                kv = mem_heads[n][:, m, :, bass.ds(h, 1), :].rearrange("p t h d -> p t (h d)")
                pool.dma_start(buf[:, 1 + m, :, :], kv).then_inc(landed, 16)

        def store_block(dst, stage, b, i, col, slot):
            store_tile(dst, col, slot, sums_out, written(blk(stage, b, i)))

        for b in range(2):
            store_block(ev_v, "ein", b, 0, At(b), b)
        all_stored(STORED["l2"] + 1)
        load_mem(0, 0, 0, d_ev)

        def ein_pair(i, last):
            store_block(ev_v, "ein", 2, i, At(2, i, 2), 0)
            if not last:
                pool.wait_ge(m_yt_ps, At(1, i, 1).times(1))
                load_mem(0, At(1, i, 1).times(1), 0, d_ev)
            store_block(ev_v, "ein", 3, i, At(3, i, 2), 1)

        with pool.Fori(0, 3) as i:
            ein_pair(i, False)
        ein_pair(3, True)
        pool.wait_ge(m_lo, 5)
        pool.wait_ge(dt_v, 6)
        pool.dma_start(d_ac.rearrange("t (h q) -> (t h) q", q=P), ac_t[:, :]).then_inc(dt_out, 16)
        pool.wait_ge(dt_out, 16)

        def load_u(g):
            pool.dma_start(u_in[:, :, 0:512], ev_v[:, :, bass.ds(g.times(512, 1024), 512)]).then_inc(s_u, 16)
            for m in range(2):
                pool.dma_start(u_in[:, :, 512 + m * P:640 + m * P],
                               ev_v[:, :, bass.ds(g.times(P, 3072 + 512 * m), P)]).then_inc(s_u, 16)

        def load_ac(g):
            pool.dma_start(dec[:, :, :], d_ac[:, bass.ds(g.times(HG * P), HG * P)].partition_broadcast(P))\
                .then_inc(s_ac, 16)

        def load_z(g):
            pool.dma_start(zt[:, :, :], ev_v[:, :, bass.ds(g.times(512, 4096), 512)]).then_inc(s_z, 16)

        load_ac(At(0))
        all_stored(STORED["l2"] + 5)
        load_u(At(0))
        load_z(At(0))
        for b in range(2):
            store_block(ev_v, "ez", b, 0, At(10 + b), b)
        all_stored(STORED["l2"] + 6)

        def sc_pair(i, last):
            g = At(1, i, 1)
            if not last:
                pool.wait_ge(s_silu, g.times(1))
                load_u(g)
            store_block(ev_v, "sc", 0, i, At(12, i, 2), 0)
            if not last:
                pool.wait_ge(s_y, g.times(1))
                load_ac(g)
                pool.wait_ge(s_yg, g.times(1))
                load_z(g)
            pool.wait_ge(s_gm, g.times(1))
            pool.tensor_tensor(g_r[:, :], g_ms[:, :], expo[:, :], ALU.pow).then_inc(s_gr, 1)
            store_block(ev_v, "sc", 1, i, At(13, i, 2), 1)

        with pool.Fori(0, 3) as i:
            sc_pair(i, False)
        sc_pair(3, True)
        all_stored(STORED["eout"])
        for j in range(2):
            if j:
                pool.wait_ge(c_ut, 2 * j)
                pool.wait_ge(c_wt, 2 * j)
            else:
                pool.wait_ge(turn_lo, 2 * TURN["x4"] + 2)
            for t in range(TH):
                pool.dma_start(sc_in[:, t, :, :].rearrange("p a n -> p (a n)"),
                               ev_v[:, t, 6144 + 2048 * j:6144 + 2048 * (j + 1)]).then_inc(c_in, 16)
        residual("eout", dx_v[2], halves(d_x4), lambda b: (sums_out, B0["eout"] + b + 3), 0)
        pool.memset(causal[:, :], 0.0).then_inc(mask_ready, 1)
        pool.wait_ge(mask_ready, 5)
        for at in (0, TOK):
            pool.affine_select(out=causal[:, at:at + P], in_=causal[:, at:at + P], compare_op=ALU.is_ge, fill=NEG,
                               base=0, pattern=[[-1, P]], channel_multiplier=1).then_inc(mask_ready, 1)
        norm(6)
        om_v = halves(d_om)
        for b in range(2):
            store_block(om_v, "omem", b, 0, At(b), b)
        pool.wait_ge(lat_ms, 2)
        for m in range(2):
            pool.tensor_tensor(rstd[:, 16 + 2 * m:18 + 2 * m], mean[:, 16 + 2 * m:18 + 2 * m], expo[:, :],
                               ALU.pow).then_inc(lat_r, 1)
        all_stored(STORED["uq"])
        load_mem(1, 0, 4, d_om)
        load_mem(1, 1, 5, d_om)
        q_v, kv_v = halves(d_q), halves(d_kv)

        def load_latent(J):
            s = J % 3
            if J >= 3:
                pool.wait_ge(l_y_ps, J)
            pool.dma_start(lq[s][:, :, :], q_v[:, :, 192 * J:192 * (J + 1)]).then_inc(at_loaded[s], 16)
            pool.dma_start(lkv[s][:, :, :], kv_v[:, :, 256 * J:256 * (J + 1)]).then_inc(at_loaded[s], 16)

        for b in range(6):
            if b == 4:
                pool.wait_ge(m_yt_ps, 5)
                load_mem(1, 2, 6, d_om)
            store_block(q_v, "uq", b, 0, At(b), b % 2)
        for b in range(8):
            if b == 1:
                pool.wait_ge(m_yt_ps, 6)
                load_mem(1, 3, 7, d_om)
            store_block(kv_v, "ukv", b, 0, At(b), b % 2)
            if b == 3:
                for s in range(2):
                    pool.wait_ge(tile_moved[s], 16 * (STORED["ukv"] + 1 + 1))
                for J in range(3):
                    load_latent(J)
        all_stored(STORED["oout"])
        for J in range(3, 16):
            load_latent(J)

        pool.wait_ge(l_tile, 4)
        pool.dma_start(fin[:, :], io["final_norm"].partition_broadcast(P)).then_inc(late_in, 16)
        for b in range(4):
            free = [] if b < 2 else [(sums_out, B0["oout"] + b + 1)]
            load_tile(halves(d_x4), At(b), b % 2, free)
        norm(7)
        out_v = halves(io["out"])
        for b in range(4):
            pool.wait_ge(fin_ready, b + 1)
            pool.dma_start(out_v[:, :, b * NBW:(b + 1) * NBW], res[:, b, :, :]).then_inc(fin_out, 16)
        pool.wait_ge(fin_out, 64)

    @block.tensor
    def _(pe):
        def unit(u, src, chunk, bank, first, last, width=NBW):
            pe.wait_ge(lo_ready, u.times(1, 1 + RING))
            s = u.slot
            for c in range(UCH):
                w = slice(c * width, (c + 1) * width)
                for t in range(TH):
                    a_hi = src[0][:, chunk + c, t * P:(t + 1) * P]
                    a_lo = src[1][:, chunk + c, t * P:(t + 1) * P]
                    out = acc[2 * bank + t][:, 0:width]
                    nc.tensor.matmul(out, a_hi, w_hi[:, s, w], start=first and c == 0, stop=False)
                    nc.tensor.matmul(out, a_hi, w_lo[:, s, w], start=False, stop=False)
                    mm = nc.tensor.matmul(out, a_lo, w_hi[:, s, w], start=False,
                                          stop=last and c == UCH - 1)
            mm.then_inc(unit_used, 1)

        def turn_tile(n, src, ready, value):
            pe.wait_ge(ready, value)
            for h in range(2):
                pe.wait_ge(turn_lo, n.times(2, h + 1))
                for c in range(2):
                    for t in range(TH):
                        at = (2 * h + c) * P
                        mm = nc.tensor.transpose(turn[h][:, (c * TH + t) * P:(c * TH + t + 1) * P],
                                                 src[:, t, at:at + P], ident[:, :])
                mm.then_inc(turned, 1)

        def source(turns, k):
            if k % 2 == 0:
                pe.wait_ge(turn_lo, 2 * (turns + k // 2) + 4)

        pe.sem_inc(unit_used, RING)
        pe.sem_inc(at_scores, 2)
        pe.sem_inc(at_y_ps, 2)
        pe.sem_inc(l_y_ps, 2)
        pe.wait_ge(const_ready, 1)
        pe.wait_ge(tile_moved[0], 16)
        nc.tensor.transpose(ps_s[:, 0:122], tile[0][0:122, 0, 0:P], ident[0:122, 0:122]).then_inc(pe_once, 1)
        pe.wait_ge(small_in, 80)
        nc.tensor.transpose(ps_y[:, 0:120], junk[0:120, 0:P], ident[0:120, 0:120])
        nc.tensor.transpose(ps_y[:, 120:144], junk[0:24, P:2 * P], ident[0:24, 0:24]).then_inc(pe_once, 1)
        for b in range(4):
            turn_tile(At(TURN["mem"] + b), xin[b % 2], xin_landed[b % 2], 16 * (b // 2 + 1))

        with pe.Fori(0, 2) as i:
            for b in range(2):
                pe.wait_ge(sums_out, blk("mem", b, i).times(1, 1))
                for k in range(8):
                    source(TURN["mem"], k)
                    unit(At(U0["mem"] + 8 * b + k, i, 16), mem_t, UCH * k, b, k == 0, k == 7)
                turn_tile(At(TURN["x"] + b, i, 2), xin[b], xin_landed[b], At(LOADED["x"], i, 1).times(16, 16))

        with pe.Fori(0, 6) as i:
            for b in range(2):
                pe.wait_ge(sums_out, blk("win", b, i).times(1, 1))
                for k in range(8):
                    source(TURN["x"], k)
                    unit(At(U0["win"] + 8 * b + k, i, 16), x_t, UCH * k, b, k == 0, k == 7)

        def attend(p, i):
            for j in range(4):
                J, m, s, kind = At(j, i, 4), At(j // 2, i, 2), j % 2, ("sb", "ca")[j % 2]
                if p == 3 * j:
                    pe.wait_ge(at_loaded[j], At(0, i, 1).times(32, 32))
                    pe.wait_ge(at_qk, J.times(1, 1))
                    for x in range(2):
                        for t in range(TH):
                            mm = nc.tensor.transpose(turn[0][:, (2 * x + t) * P:(2 * x + t + 1) * P],
                                                     qkv[j][:, t, x, :], ident[:, :])
                    mm.then_inc(at_qk_ps, 1)
                if p == 3 * j + 1:
                    pe.wait_ge(at_qk, J.times(1, 2))
                    pe.wait_ge(at_z, J.times(1, 1))
                    q, k = qk_t[s][:, 0:TOK], qk_t[s][:, TOK:2 * TOK]
                    nc.tensor.matmul(ps_s[:, 0:P], q[:, 0:P], k[:, 0:P], start=True, stop=True)
                    nc.tensor.matmul(ps_s[:, P:H3], q[:, P:TOK], k, start=True, stop=True)\
                        .then_inc(at_scores, 1)
                if p == 3 * j + 5:
                    pe.wait_ge(at_prob[kind], m.times(1, 1))
                    pe.wait_ge(at_pt, J.times(1, 1))
                    for c in range(3):
                        mm = nc.tensor.transpose(turn[1][:, c * P:(c + 1) * P],
                                                 prob[kind][:, c * P:(c + 1) * P], ident[:, :])
                    mm.then_inc(at_pt_ps, 1)
                if p == 3 * j + 6:
                    pe.wait_ge(at_pt, J.times(1, 2))
                    pe.wait_ge(at_y_lo, J.times(1, 1))
                    nc.tensor.matmul(ps_y[:, 0:TOK], qkv[j][:, 0, 2, :], p_t[s][:, 0:TOK],
                                     start=True, stop=False)
                    nc.tensor.matmul(ps_y[:, P:TOK], qkv[j][:, 1, 2, :], p_t[s][:, TOK:H3],
                                     start=False, stop=True).then_inc(at_y_ps, 1)

        with pe.Fori(0, 4) as i:
            for b in range(2):
                pe.wait_ge(sums_out, blk("win", 12 + b, i).times(1, 1))
                for k in range(8):
                    attend(8 * b + k, i)
                    unit(At(U0["win"] + 96 + 8 * b + k, i, 16), x_t, UCH * k, b, k == 0, k == 7)

        pe.wait_ge(at_y_lo, 17)
        for n in range(4):
            for b in range(2):
                pe.wait_ge(sums_out, B0["out"] + 2 * n + b + 1)
                for k in range(4):
                    if n and (b, k) == (0, 2):
                        turn_tile(At(TURN["mix"] + n - 1), tile[0], tile_ready, n + 2)
                    unit(At(U0["out"] + 8 * n + 4 * b + k), y_t, 8 * b + UCH * k, b, k == 0, k == 3)

        pe.wait_ge(late_in, 16)
        for c in range(2):
            for t in range(TH):
                mm = nc.tensor.transpose(ps_s[:, (2 * c + t) * P:(2 * c + t + 1) * P],
                                         pl_row[:, t, c * P:(c + 1) * P], ident[:, :])
        mm.then_inc(pe_once, 1)

        def residual(stage, src, units, src_turns, turns, ready, before):
            for b in range(4):
                pe.wait_ge(sums_out, B0[stage] + b + 1)
                for k in range(units):
                    if k == TURN_AT:
                        if b == 0:
                            before()
                        else:
                            turn_tile(At(turns + b - 1), tile[(b - 1) % 2], *ready(b - 1))
                    source(src_turns, k)
                    unit(At(U0[stage] + b * units + k), src, UCH * k, b % 2, k == 0, k == units - 1)
            return lambda: turn_tile(At(turns + 3), tile[1], *ready(3))

        def from_sums(stage):
            return lambda b: (sums_out, B0[stage] + b + 3)

        before = residual("mix", m_t, 8, TURN["mix"], TURN["ffn"], from_sums("mix"),
                          lambda: turn_tile(At(TURN["mix"] + 3), tile[0], tile_ready, 6))

        def ffn_pair(n, i, before):
            for b in range(2):
                pe.wait_ge(sums_out, blk("ffn", 2 * n + b, i).times(1, 1))
                for k in range(8):
                    if (b, k) == (0, TURN_AT):
                        before()
                    source(TURN["ffn"], k)
                    unit(At(U0["ffn"] + 16 * n + 8 * b + k, i, 16), x_t, UCH * k, b, k == 0, k == 7)

        ffn_pair(0, 0, before)
        with pe.Fori(0, 10) as i:
            ffn_pair(1, i, lambda: turn_tile(At(TURN["ffo"], i, 1), tile[0], sums_out, written(blk("ffn", 1, i))))
        before = residual("ffo", ff_t, 22, TURN["ffo"], TURN["ple"], from_sums("ffo"),
                          lambda: turn_tile(At(TURN["ffo"] + 10), tile[0], sums_out, B0["ffn"] + 21 + 3))

        pe.wait_ge(ple_lo, 1)
        for b in range(4):
            pe.wait_ge(sums_out, B0["ple"] + b + 1)
            unit(At(U0["ple"] + b), ple_t, 0, b % 2, True, True)
        before = residual("gate", x_t, 8, TURN["ple"], TURN["x3"], lambda b: (tile_ready, 4 + b + 3), before)

        def mem_job(n, J, p):
            _, qk_, pr_, pt_, y_, th_, sm_ = mbuf[n]
            qkv_ = mqkv[n][J.k % len(mqkv[n])]
            if p == 0:
                if n == 0:
                    pe.wait_ge(m_loaded[0], J.times(64, 64))
                else:
                    pe.wait_ge(m_loaded[J.k % 2], 64 * ((4 if J.k % 2 == 0 else 0) + (J.k - 4) // 2 + 1))
                pe.wait_ge(m_qk, J.times(1, 1))
                for x in range(2):
                    for t in range(TH):
                        mm = nc.tensor.transpose(turn[0][:, (2 * x + t) * P:(2 * x + t + 1) * P],
                                                 qkv_[:, x, t, :], ident[:, :])
                mm.then_inc(m_qk_ps, 1)
            if p == 1:
                pe.wait_ge(m_qk, J.times(1, 2))
                for t in range(TH):
                    mm = nc.tensor.matmul(ps_s[:, t * TOK:(t + 1) * TOK], qk_[:, t * P:(t + 1) * P],
                                          qk_[:, TOK:2 * TOK], start=True, stop=True)
                mm.then_inc(m_scores, 1)
            if p == 4:
                pe.wait_ge(m_exp, J.times(1, 1))
                for k in range(2):
                    for t in range(TH):
                        mm = nc.tensor.transpose(turn[1][:, (2 * k + t) * P:(2 * k + t + 1) * P],
                                                 pr_[:, t * TOK + k * P:t * TOK + (k + 1) * P], ident[:, :])
                mm.then_inc(m_pt_ps, 1)
            if p == 5:
                pe.wait_ge(m_pt, J.times(1, 1))
                pe.wait_ge(m_lo, J.times(1, 1))
                for t in range(TH):
                    for k in range(2):
                        mm = nc.tensor.matmul(ps_y[:, t * P:(t + 1) * P], pt_[:, (2 * k + t) * P:(2 * k + t + 1) * P],
                                              qkv_[:, 2, k, :], start=k == 0, stop=k == 1)
                mm.then_inc(m_y_ps, 1)
            if p == 7:
                pe.wait_ge(m_y, J.times(1, 1))
                for t in range(TH):
                    mm = nc.tensor.transpose(ps_y[:, TOK + t * P:TOK + (t + 1) * P], y_[:, t, :], ident[:, :])
                mm.then_inc(m_yt_ps, 1)

        def pair_of(stage, b0, i, per, units, src, chunk, beside=None, turns=None, before=None):
            for b in range(2):
                n = blk(stage, b0 + b, i)
                pe.wait_ge(sums_out, n.times(1, 1))
                for k in range(units):
                    if before and (b, k) == (0, TURN_AT):
                        before()
                    if turns is not None:
                        source(turns, k)
                    if beside:
                        beside(units * b + k)
                    unit(At(U0[stage] + units * (b0 + b) + k, i, 2 * units), src, chunk + UCH * k, n.k % 2,
                         k == 0, k == units - 1)

        pair_of("ein", 0, 0, 0, 8, x3_t, 0, None, TURN["x3"], before)
        with pe.Fori(0, 4) as i:
            pair_of("ein", 2, i, 1, 8, x3_t, 0, lambda p: mem_job(0, At(0, i, 1), p - 4))
        u = At(U0["dt"])
        pe.wait_ge(lo_ready, u.times(1, 1 + RING))
        pe.wait_ge(m_lo, 5)
        for t in range(TH):
            for c in range(16):
                w = slice(32 * c, 32 * c + 32)
                a_hi, a_lo = (x3_t[x][:, c, t * P:(t + 1) * P] for x in range(2))
                out = ps_y[:, 32 * t:32 * t + 32]
                nc.tensor.matmul(out, a_hi, w_hi[:, u.slot, w], start=c == 0, stop=False)
                nc.tensor.matmul(out, a_hi, w_lo[:, u.slot, w], start=False, stop=False)
                mm = nc.tensor.matmul(out, a_lo, w_hi[:, u.slot, w], start=False, stop=c == 15)
        mm.then_inc(unit_used, 1)

        def time_steps(p):
            if p == 3:
                pe.wait_ge(dt_v, 3)
                pe.wait_ge(mask_ready, 2)
                nc.tensor.matmul(ps_y[:, 64:128], tri[:, :], d_a[:, :], start=True, stop=True)
                nc.tensor.matmul(ps_y[:, 128:192], ones[:, 0:P], d_a[:, :], start=True, stop=True)\
                    .then_inc(pe_once, 1)
            if p == 5:
                pe.wait_ge(dt_v, 4)
                nc.tensor.transpose(ps_s[0:64, 0:P], acum[:, :], ident[:, :]).then_inc(pe_once, 1)

        pair_of("ez", 0, 0, 0, 8, x3_t, 0, time_steps)

        def ssd(p, i):
            n = At(0, i, 1)
            if p == 0:
                pe.wait_ge(s_u, n.times(48, 48))
                pe.wait_ge(dt_v, 6)
                pe.wait_ge(turn_lo, At(TURN["sy"], i, 1).times(2, 2))
                for c in range(6):
                    bank = (turn[0], turn[1], ps_s)[c // 2]
                    for t in range(TH):
                        mm = nc.tensor.transpose(bank[:, (c % 2 * TH + t) * P:(c % 2 * TH + t + 1) * P],
                                                 u_in[:, t, c * P:(c + 1) * P], ident[:, :])
                mm.then_inc(s_ut, 1)
            if p == 7:
                pe.wait_ge(s_silu, n.times(1, 1))
                for t in range(TH):
                    for c in range(4):
                        mm = nc.tensor.transpose(turn[t][:, c * P:(c + 1) * P], cv[:, c, t * P:(t + 1) * P],
                                                 ident[:, :])
                mm.then_inc(s_xt, 1)
                nc.tensor.transpose(ps_s[:, 0:P], cv[:, 4, 0:P], ident[:, :])
                for t in range(TH):
                    w = slice(t * P, (t + 1) * P)
                    mm = nc.tensor.matmul(ps_s[:, (1 + t) * P:(2 + t) * P], cv[:, 4, w], cv[:, 5, w],
                                          start=True, stop=True)
                mm.then_inc(s_cb, 1)
            if p == 9:
                pe.wait_ge(s_xde, n.times(1, 1))
                nc.tensor.matmul(ps_s[:, :], bm_t[:, :], xde[:, :], start=True, stop=True).then_inc(s_st, 1)
            if p == 11:
                pe.wait_ge(s_m, n.times(1, 1))
                pe.wait_ge(s_xd, n.times(1, 1))
                pe.wait_ge(s_state, n.times(1, 1))
                for t in range(TH):
                    for h in range(HG):
                        w = slice(h * SP_, (h + 1) * SP_)
                        nc.tensor.matmul(turn[t][:, w], dec[:, t, h * P:(h + 1) * P], xdt[:, t, w],
                                         start=True, stop=True)
                nc.tensor.matmul(ps_y[:, :], cv[:, 5, P:TOK], st[:, :], start=True, stop=True).then_inc(s_y, 1)
            if p == 15:
                turn_tile(At(TURN["sy"], i, 1), yb, s_tile, n.times(1, 1))

        with pe.Fori(0, 4) as i:
            pair_of("sc", 0, i, 1, 8, x3_t, 0, lambda p: ssd(p, i))

        def short(p, j):
            if p == 6 + 7 * j:
                if j:
                    pe.wait_ge(c_y, j)
                else:
                    pe.wait_ge(turn_lo, 2 * TURN["x4"] + 2)
                pe.wait_ge(c_u, j + 1)
                pe.wait_ge(c_w, j + 1)
                for src, banks, s_ in ((sc_in[:, :, 1, :], turn, c_ut), (sc_in[:, :, 0, :], (ps_s, ps_y), c_wt)):
                    for h in range(2):
                        for c in range(2):
                            for t in range(TH):
                                mm = nc.tensor.transpose(
                                    banks[h][:, (c * TH + t) * P:(c * TH + t + 1) * P],
                                    src[:, t, (2 * h + c) * P:(2 * h + c + 1) * P], ident[:, :])
                        mm.then_inc(s_, 1)

        def turn_x4(b):
            turn_tile(At(TURN["x4"] + b), tile[b % 2], sums_out, B0["eout"] + b + 3)

        for q, (b, k) in enumerate(EOUT_ORDER):
            if k == 0:
                pe.wait_ge(sums_out, B0["eout"] + b + 1)
            for j in range(2):
                short(q, j)
            if q == 6:
                pe.wait_ge(turn_lo, 2 * TURN["x4"] + 2)
                pe.wait_ge(m_lo, 5)
            if q == 20:
                pe.wait_ge(c_lo, 2)
            if q == 27:
                turn_x4(0)
            unit(At(U0["eout"] + q), z_t, UCH * k, (B0["eout"] + b) % 2, k == 0, k == 13)
        for b in range(2, 4):
            pe.wait_ge(sums_out, B0["eout"] + b + 1)
            for k in range(14):
                if k == TURN_AT:
                    turn_x4(b - 1)
                unit(At(U0["eout"] + 14 * b + k), z_t, UCH * k, (B0["eout"] + b) % 2, k == 0, k == 13)

        for b in range(3):
            n = B0["olow"] + b
            pe.wait_ge(sums_out, n + 1)
            for k in range(8):
                if (b, k) == (0, TURN_AT):
                    turn_x4(3)
                source(TURN["x4"], k)
                unit(At(U0["olow"] + 8 * b + k), x_t, UCH * k, n % 2, k == 0, k == 7, 448)

        def latents(h):
            if h == 0:
                pe.wait_ge(sums_out, B0["olow"] + 2 + 3)
            pe.wait_ge(lat_lo, h + 1)
            for c in range(2):
                for t in range(TH):
                    at = (2 * h + c) * P
                    mm = nc.tensor.transpose(turn[h % 2][:, (c * TH + t) * P:(c * TH + t + 1) * P],
                                             lat[:, t, at:at + P], ident[:, :])
            mm.then_inc(lat_ps, 1)

        def omem_beside(p):
            if p in (2, 4, 6, 8, 10):
                latents(p // 2 - 1)
            if p == 14:
                pe.wait_ge(r_kr, 1)
                for t in range(TH):
                    mm = nc.tensor.transpose(ps_s[0:64, t * P:(t + 1) * P], kr[:, t, :], ident[:, :])
                mm.then_inc(pe_once, 1)

        pair_of("omem", 0, 0, 0, 8, x_t, 0, omem_beside)
        pe.wait_ge(lat_lo, 7)
        pe.wait_ge(act_once, 12)
        for b in range(6):
            n = B0["uq"] + b
            pe.wait_ge(sums_out, n + 1)
            for k in range(3):
                p = 3 * b + k
                for j in range(4):
                    mem_job(1, At(4 + j), p - 7 * j - 5)
                unit(At(U0["uq"] + p), lat_t, UCH * k, n % 2, k == 0, k == 2)
        for b in range(8):
            n = B0["ukv"] + b
            pe.wait_ge(sums_out, n + 1)
            for k in range(2):
                p = 2 * b + k
                for j in range(4):
                    mem_job(1, At(4 + j), 18 + p - 7 * j - 5)
                unit(At(U0["ukv"] + p), lat_t, 6 + UCH * k, n % 2, k == 0, k == 1)

        def latent_heads(p):
            for J in range(16):
                s, q = J % 2, p - 2 * J
                if q == 0:
                    pe.wait_ge(at_loaded[J % 3], AT_LOADS + 32 * (J // 3 + 1))
                    pe.wait_ge(l_rot, J + 1)
                    pe.wait_ge(l_pt, J + 1)
                    pe.wait_ge(turn_lo, 2 * TURN["oy"] + sum(p > GATED + 8 * n + 2 * h for n in range(4)
                                                             for h in range(2)) + 2)
                    for x, src in enumerate((lq[J % 3], lkv[J % 3])):
                        for t in range(TH):
                            mm = nc.tensor.transpose(turn[0][:, (2 * x + t) * P:(2 * x + t + 1) * P],
                                                     src[:, t, 0:P], ident[:, :])
                    mm.then_inc(l_qk_ps, 1)
                    for t in range(TH):
                        mm = nc.tensor.transpose(turn[1][0:64, t * P:(t + 1) * P], lq[J % 3][:, t, P:192],
                                                 ident[:, :])
                    mm.then_inc(l_qr_ps, 1)
                if q == 1:
                    pe.wait_ge(l_qk, J + 1)
                    pe.wait_ge(l_qr, J + 1)
                    pe.wait_ge(l_z, J + 1)
                    q_n, k_n, q_r = lqk[s][:, 0:TOK], lqk[s][:, TOK:2 * TOK], lr[s]
                    for out, qw, kw in ((ps_s[:, 0:P], slice(0, P), slice(0, P)),
                                        (ps_s[:, P:H3], slice(P, TOK), slice(0, TOK))):
                        nc.tensor.matmul(out, q_n[:, qw], k_n[:, kw], start=True, stop=False)
                        mm = nc.tensor.matmul(out, q_r[:, qw], kr_t[:, kw], start=False, stop=True)
                    mm.then_inc(l_scores, 1)
                if q == 3:
                    pe.wait_ge(l_exp, J + 1)
                    pe.wait_ge(l_qr, min(J + 2, 16))
                    for c in range(3):
                        mm = nc.tensor.transpose(turn[1][:, c * P:(c + 1) * P], lp[s][:, c * P:(c + 1) * P],
                                                 ident[:, :])
                    mm.then_inc(l_pt_ps, 1)
                if q == 4:
                    pe.wait_ge(l_pt, J + 3)
                    pe.wait_ge(l_y, J + 1)
                    v = lkv[J % 3]
                    nc.tensor.matmul(ps_y[:, 0:P], lpt[s][:, 0:P], v[:, 0, P:TOK], start=True, stop=True)
                    nc.tensor.matmul(ps_y[:, P:TOK], lpt[s][:, P:TOK], v[:, 0, P:TOK],
                                     start=True, stop=False)
                    nc.tensor.matmul(ps_y[:, P:TOK], lpt[s][:, TOK:H3], v[:, 1, P:TOK],
                                     start=False, stop=True).then_inc(l_y_ps, 1)
            for n in range(4):
                for h in range(2):
                    if p == GATED + 8 * n + 2 * h:
                        pe.wait_ge(l_tile, n + 1)
                        pe.wait_ge(turn_lo, 2 * (TURN["oy"] + n) + h + 2)
                        pe.wait_ge(l_qk, min(p // 2 + 1, 16))
                        for c in range(2):
                            for t in range(TH):
                                at = n * NBW + (2 * h + c) * P
                                mm = nc.tensor.transpose(turn[0][:, (c * TH + t) * P:(c * TH + t + 1) * P],
                                                         ybuf[:, t, at:at + P], ident[:, :])
                        mm.then_inc(turned, 1)

        for b in range(4):
            n = B0["zc"] + b
            pe.wait_ge(sums_out, n + 1)
            for k in range(8):
                latent_heads(8 * b + k)
                unit(At(U0["zc"] + 8 * b + k), x_t, UCH * k, n % 2, k == 0, k == 7)
        pe.wait_ge(m_lo, 9)
        for b in range(4):
            n = B0["oout"] + b
            pe.wait_ge(sums_out, n + 1)
            for k in range(10):
                if b == 0:
                    latent_heads(32 + k)
                    if k >= 2:
                        pe.wait_ge(turn_lo, 2 * TURN["oy"] + k - 1 + 2)
                unit(At(U0["oout"] + 10 * b + k), o_t, (16 + UCH * k) % 20, n % 2, k == 0, k == 9)

    @block.scalar
    def _(act):
        def split(u):
            act.wait_ge(raw_landed[u.slot], u.landed())
            act.wait_ge(unit_used, u.times(1, 1))
            nc.scalar.activation(w_hi[:, u.slot, :], raw[:, u.slot, :], ACT.Copy).then_inc(hi_ready, 1)

        def splits(stage, units, first, i, per, hook=None):
            for k in range(units):
                if hook:
                    hook(k)
                split(At(U0[stage] + first + k + LEAD, i, per))

        def summed(u):
            act.wait_ge(unit_used, u.times(1, 1 + RING))

        def high(n, dst, b, g=None):
            for h in range(2):
                act.wait_ge(turned, n.times(2, h + 1))
                if g is None:
                    at = dst[0][:, bass.ds(b.times(4, 2 * h), 2), :].rearrange("p c t -> p (c t)")
                    last = nc.scalar.activation(at, turn[h][:, :], ACT.Copy)
                else:
                    for c in range(2):
                        at = dst[0][:, bass.ds(b.times(4, 2 * h + c), 1), :].rearrange("p c t -> p (c t)")
                        last = nc.scalar.activation(at, turn[h][:, c * TOK:(c + 1) * TOK], ACT.Copy,
                                                    scale=gain[:, bass.ds(b.times(4, 2 * h + c + g), 1)])
                last.then_inc(turn_hi, 1)

        def square(src, col, b, count):
            if count is not None:
                act.wait_ge(squared, count)
            for t in range(TH):
                last = nc.scalar.activation(junk[:, t * NBW:(t + 1) * NBW], src[:, t, :], ACT.Square,
                                            accum_out=stat[:, bass.ds(b.times(1, col + 4 * t), 1)])
            last.then_inc(squared, 1)

        def scale_out(u, s, stored, r):
            summed(u)
            act.wait_ge(tile_moved[s], stored)
            for t in range(TH):
                last = nc.scalar.activation(tile[s][:, t, :], acc[2 * s + t][:, :], ACT.Copy,
                                            scale=rstd[:, 2 * r + t:2 * r + t + 1])
            last.then_inc(sums_out, 1)

        act.sem_inc(at_qk, 1)
        act.sem_inc(m_qk, 1)
        act.wait_ge(pe_once, 1)
        nc.scalar.activation(gain[:, 0:122], ps_s[:, 0:122], ACT.Copy).then_inc(act_once, 1)
        act.wait_ge(pe_once, 2)
        nc.scalar.activation(col2[:, 0:24], ps_y[:, 0:24], ACT.Copy)
        nc.scalar.activation(col2[:, 24:144], ps_y[:, 24:144], ACT.Copy, scale=0.5).then_inc(act_once, 1)
        act.wait_ge(act_once, 2)
        for u in range(LEAD):
            split(At(u))
        for b in range(4):
            act.wait_ge(xin_landed[b % 2], 16 * (b // 2 + 1))
            square(xin[b % 2], 0, At(b), b or None)
            high(At(TURN["mem"] + b), mem_t, At(b), 0)
        with act.Fori(0, 2) as i:
            for b in range(2):
                splits("mem", 8, 8 * b, i, 16)
                act.wait_ge(rstd_ready, 1)
                act.wait_ge(e_built, 3)
                scale_out(At(8 * b + 7, i, 16), b, At(STORED["mem"], i, 1).times(16, 16), 0)
                act.wait_ge(xin_landed[b], At(LOADED["x"], i, 1).times(16, 16))
                square(xin[b], 8, At(b, i, 2), At(4 + b, i, 2).times(1))
                high(At(TURN["x"] + b, i, 2), x_t, At(b, i, 2), 16)
        act.wait_ge(rstd_ready, 2)
        with act.Fori(0, 6) as i:
            for b in range(2):
                splits("win", 8, 8 * b, i, 16)
                scale_out(At(U0["win"] + 8 * b + 7, i, 16), b, At(STORED["win"], i, 1).times(16, 16), 1)

        def attend(p, i):
            for j in range(4):
                J, m, s, kind = At(j, i, 4), At(j // 2, i, 2), j % 2, ("sb", "ca")[j % 2]
                if p == 3 * j:
                    act.wait_ge(at_qk_ps, J.times(1, 1))
                    act.wait_ge(at_scores, J.times(1, 1))
                    nc.scalar.activation(qk_t[s][:, :], turn[0][:, :], ACT.Copy).then_inc(at_qk, 1)
                if p == 3 * j + 1 and kind == "sb":
                    act.wait_ge(at_z, J.times(1, 2))
                    nc.scalar.activation(keep[:, :], z["sb"][:, :], ACT.Abs).then_inc(at_abs, 1)
                    act.wait_ge(at_abs, m.times(1, 1))
                    nc.scalar.activation(keep[:, :], keep[:, :], ACT.Exp, scale=-1.0).then_inc(at_exp0, 1)
                    act.wait_ge(at_exp0, m.times(1, 1))
                    nc.scalar.activation(keep[:, :], keep[:, :], ACT.Ln, bias=1.0).then_inc(at_keep, 1)
                if p == 3 * j + 2 and kind == "ca":
                    act.wait_ge(at_max, m.times(1, 1))
                    for x, w in enumerate((slice(0, P), slice(P, H3))):
                        last = nc.scalar.activation(prob["ca"][:, w], z["ca"][:, w], ACT.Exp,
                                                    bias=sm[:, x:x + 1], accum_out=sm[:, 2 + x:3 + x])
                    last.then_inc(at_exp, 1)
                if p == 3 * j + 3 and kind == "sb":
                    act.wait_ge(at_left, m.times(1, 1))
                    nc.scalar.activation(prob["sb"][:, :], left[:, :], ACT.Exp).then_inc(at_prob["sb"], 1)
                if p == 3 * j + 6:
                    act.wait_ge(at_y_ps, J.times(1, 3))
                    head = At(j // 2 + 8 * s, i, 2)
                    nc.scalar.activation(y_t[0][:, bass.ds(head.times(1), 1), :].rearrange("p c t -> p (c t)"),
                                         ps_y[:, 0:TOK], ACT.Copy).then_inc(at_y_hi, 1)

        with act.Fori(0, 4) as i:
            for b in range(2):
                splits("win", 8, 96 + 8 * b, i, 16, lambda k: attend(8 * b + k, i))
                scale_out(At(U0["win"] + 96 + 8 * b + 7, i, 16), b,
                          At(STORED["win"] + 6, i, 1).times(16, 16), 1)

        def open_gates(s, i):
            act.wait_ge(gates_in[s], At(0, i, 1).times(32, 32))
            g = gates[s][:, :, :, :].rearrange("p g t n -> p (g t n)")
            nc.scalar.activation(g, g, ACT.Sigmoid).then_inc(gates_sig, 1)

        for n in range(4):
            def beside_out(k):
                if k == 1:
                    open_gates(n % 2, n // 2)
                if n and k == 2:
                    high(At(TURN["mix"] + n - 1), m_t, At(n - 1))
            splits("out", 8, 8 * n, 0, 0, beside_out)

        act.wait_ge(pe_once, 3)
        nc.scalar.activation(ple_t[0][:, :, :].rearrange("p c t -> p (c t)"), ps_s[:, :], ACT.Copy)\
            .then_inc(act_once, 1)

        def residual(stage, units, turns, dst, g, col, count, ready, before, gate=None):
            def tile_out(b):
                act.wait_ge(*ready(b))
                square(tile[b % 2], col, At(b), count + b if gate is None else count + 2 * b + 1)
                high(At(turns + b), dst, At(b), g)
            for b in range(4):
                splits(stage, units, b * units, 0, 0,
                       lambda k: (tile_out(b - 1) if b else before()) if k == TURN_AT else None)
                if gate:
                    gate(b)
            return lambda: tile_out(3)

        def from_sums(stage):
            return lambda b: (sums_out, B0[stage] + b + 3)

        before = residual("mix", 8, TURN["ffn"], x_t, 32, 16, 8, from_sums("mix"),
                          lambda: high(At(TURN["mix"] + 3), m_t, At(3)))

        def ffn_pair(n, i, before):
            for b in range(2):
                splits("ffn", 8, 16 * n + 8 * b, i, 16, lambda k: before() if (b, k) == (0, TURN_AT) else None)
                if b == 0:
                    summed(At(U0["ffn"] + 16 * n + 7, i, 16))
                    act.wait_ge(rstd_ready, 3)
                    act.wait_ge(ff_half, At(n, i, 1).times(1, 1))
                    for t in range(TH):
                        r = rstd[:, 4 + t:5 + t]
                        nc.scalar.activation(g_half[:, t, :], acc[t][:, :], ACT.Copy, scale=r)
                        last = nc.scalar.activation(g_sig[:, t, :], acc[t][:, :], ACT.Sigmoid, scale=r)
                    last.then_inc(sums_out, 1)

        ffn_pair(0, 0, before)
        with act.Fori(0, 10) as i:
            ffn_pair(1, i, lambda: high(At(TURN["ffo"], i, 1), ff_t, At(0, i, 1)))
        before = residual("ffo", 22, TURN["ple"], x_t, 48, 24, 12, from_sums("ffo"),
                          lambda: high(At(TURN["ffo"] + 10), ff_t, At(10)))
        for b in range(4):
            split(At(U0["ple"] + b + LEAD))
            summed(At(U0["ple"] + b))
            if b == 0:
                act.wait_ge(sums_out, B0["ple"] + 2)
            for t in range(TH):
                last = nc.scalar.activation(pl_out[:, b, t, :], acc[2 * (b % 2) + t][:, :], ACT.Copy)
            last.then_inc(sums_out, 1)

        def ple_gate(b):
            summed(At(U0["gate"] + 8 * b + 7))
            act.wait_ge(rstd_ready, 4)
            act.wait_ge(pl_mul, b + 1)
            for t in range(TH):
                last = nc.scalar.activation(pl_sig[:, t, :], acc[2 * (b % 2) + t][:, :], ACT.Sigmoid,
                                            scale=rstd[:, 6 + t:7 + t])
            last.then_inc(sums_out, 1)
            act.wait_ge(pl_sum, b + 1)
            square(x_raw, 32, At(b), 16 + 2 * b)

        before = residual("gate", 8, TURN["x3"], x3_t, 64, 40, 16, lambda b: (tile_ready, 4 + b + 3),
                          before, ple_gate)

        def scaled(u, bank, slot, stored, scale):
            summed(u)
            act.wait_ge(tile_moved[slot], stored)
            for t in range(TH):
                last = nc.scalar.activation(tile[slot][:, t, :], acc[2 * bank + t][:, :], ACT.Copy,
                                            scale=scale[:, t:t + 1])
            last.then_inc(sums_out, 1)

        def mem_job(n, J, p, dst, chunk):
            _, qk_, pr_, pt_, y_, th_, sm_ = mbuf[n]
            qkv_ = mqkv[n][J.k % len(mqkv[n])]
            if p == 0:
                act.wait_ge(m_qk_ps, J.times(1, 1))
                nc.scalar.activation(qk_[:, :], turn[0][:, :], ACT.Copy).then_inc(m_qk, 1)
                nc.scalar.activation(th_[:, :, :], qkv_[:, 3, :, :], ACT.Tanh, scale=0.5)
            if p == 2:
                act.wait_ge(m_max2, J.times(1, 1))
                for t in range(TH):
                    last = nc.scalar.activation(pr_[:, t * TOK:(t + 1) * TOK], ps_s[:, t * TOK:(t + 1) * TOK],
                                                ACT.Exp, scale=SCALE, bias=sm_[:, t:t + 1],
                                                accum_out=sm_[:, 2 + t:3 + t])
                last.then_inc(m_exp, 1)
            if p == 7:
                act.wait_ge(m_yt_ps, J.times(1, 1))
                nc.scalar.activation(dst[0][:, bass.ds(chunk, 1), :].rearrange("p c t -> p (c t)"),
                                     ps_y[:, TOK:2 * TOK], ACT.Copy, scale=0.5).then_inc(m_hi, 1)

        act.wait_ge(small_in, 80)
        nc.scalar.activation(a_exp[:, :], rowb[:, 32:64], ACT.Exp).then_inc(act_once, 1)
        for b in range(2):
            splits("ein", 8, 8 * b, 0, 0, lambda k: before() if (b, k) == (0, TURN_AT) else None)
            act.wait_ge(cc, 3)
            scaled(At(U0["ein"] + 8 * b + 7), b, b, 16 * (STORED["l2"] + 1), scal)
        with act.Fori(0, 4) as i:
            for b in range(2):
                splits("ein", 8, 16 + 8 * b, i, 16,
                       lambda k: mem_job(0, At(0, i, 1), 8 * b + k - 4, z_t, At(16, i, 1).times(1)))
                scaled(At(U0["ein"] + 16 + 8 * b + 7, i, 16), b, b, At(STORED["l2"] + 1, i, 1).times(16, 16), scal)
        split(At(U0["dt"] + LEAD))

        def time_steps(p):
            if p == 1:
                act.wait_ge(dt_v, 1)
                nc.scalar.activation(dts[:, :], dtz[:, :], ACT.Abs).then_inc(act_once, 1)
                act.wait_ge(act_once, 5)
                nc.scalar.activation(dts[:, :], dts[:, :], ACT.Exp, scale=-1.0).then_inc(act_once, 1)
                act.wait_ge(act_once, 6)
                nc.scalar.activation(dts[:, :], dts[:, :], ACT.Ln, bias=1.0).then_inc(act_once, 1)
            if p == 4:
                act.wait_ge(dt_v, 5)
                nc.scalar.activation(d_end[:, :], d_end[:, :], ACT.Exp).then_inc(act_once, 1)
                nc.scalar.activation(e_ac[:, :], acum[:, 32:64], ACT.Exp).then_inc(act_once, 1)
            if p == 14:
                open_decays(At(0))

        def open_decays(n):
            act.wait_ge(s_min, n.times(1, 1))
            nc.scalar.activation(dec[:, :, :], dec[:, :, :], ACT.Exp).then_inc(s_dec, 1)

        for b in range(2):
            splits("ez", 8, 8 * b, 0, 0, lambda k: time_steps(8 * b + k))
            scaled(At(U0["ez"] + 8 * b + 7), b, b, 16 * (STORED["l2"] + 6), scal)

        def ssd(p, i, last_group):
            n = At(0, i, 1)
            if p == 0:
                act.wait_ge(s_ut, n.times(1, 1))
                for c in range(6):
                    bank = (turn[0], turn[1], ps_s)[c // 2]
                    ch = At(c, i, 4) if c < 4 else At(12 + 4 * (c - 3), i, 1)
                    last = nc.scalar.activation(cv[:, c, :], bank[:, c % 2 * TOK:(c % 2 + 1) * TOK], ACT.Identity,
                                                scale=col2[:, bass.ds(ch.times(1, 96), 1)],
                                                bias=col2[:, bass.ds(ch.times(1, 120), 1)])
                last.then_inc(s_tap, 1)
            if p == 3:
                act.wait_ge(s_conv, n.times(3, 3))
                nc.scalar.activation(th[:, :], cv[:, :, :].rearrange("p c t -> p (c t)"), ACT.Tanh)\
                    .then_inc(s_th, 1)
            if p == 5:
                act.wait_ge(s_z, n.times(16, 16))
                nc.scalar.activation(zth[:, :, :], zt[:, :, :], ACT.Tanh, scale=0.5).then_inc(s_zth, 1)
            if p == 7:
                act.wait_ge(s_xt, n.times(1, 1))
                for t in range(TH):
                    last = nc.scalar.activation(xs[:, t, :], turn[t][:, :], ACT.Copy)
                last.then_inc(s_xs, 1)
            if p == 9:
                act.wait_ge(s_st, n.times(1, 1))
                nc.scalar.activation(st[:, :], ps_s[:, :], ACT.Copy).then_inc(s_state, 1)
            if p == 12:
                act.wait_ge(s_yg, n.times(1, 1))
                for t in range(TH):
                    last = nc.scalar.activation(zth[:, t, :], yb[:, t, :], ACT.Square,
                                                accum_out=g_ss[:, t:t + 1])
                last.then_inc(s_sq, 1)
            if p == 14 and not last_group:
                open_decays(n + 1)

        def sc_pair(i, last_group):
            for b in range(2):
                splits("sc", 8, 8 * b, i, 16, lambda k: ssd(8 * b + k, i, last_group))
                if b == 1:
                    high(At(TURN["sy"], i, 1), z_t, At(0, i, 1), 96)
                scaled(At(U0["sc"] + 8 * b + 7, i, 16), b, b, At(STORED["sc"], i, 1).times(16, 16), scal)

        with act.Fori(0, 3) as i:
            sc_pair(i, False)
        sc_pair(3, True)

        def short(k, j):
            if k == 7 * j + 4:
                act.wait_ge(c_u, j + 1)
                nc.scalar.activation(sc_in[:, :, 2, :], sc_in[:, :, 3, :], ACT.Tanh, scale=0.5).then_inc(c_th, 1)
            if k == 7 * j + 8:
                act.wait_ge(c_y, j + 1)
                nc.scalar.activation(z_t[0][:, 20 + 4 * j:24 + 4 * j, :].rearrange("p c t -> p (c t)"),
                                     sc_y[:, :], ACT.Copy).then_inc(c_hi, 1)

        def eout_tile(b):
            act.wait_ge(sums_out, B0["eout"] + b + 3)
            square(tile[b % 2], 48, At(b), 24 + b)
            high(At(TURN["x4"] + b), x_t, At(b), 80)

        for q in range(28):
            for j in range(2):
                short(q, j)
            if q == 27:
                eout_tile(0)
            split(At(U0["eout"] + q + LEAD))
        for b in range(2, 4):
            splits("eout", 14, 14 * b, 0, 0, lambda k: eout_tile(b - 1) if k == TURN_AT else None)

        c4 = rstd[:, 12:14]
        for b in range(3):
            splits("olow", 8, 8 * b, 0, 0, lambda k: eout_tile(3) if (b, k) == (0, TURN_AT) else None)
            act.wait_ge(rstd_ready, 7)
            summed(At(U0["olow"] + 8 * b + 7))
            bank = (B0["olow"] + b) % 2
            for t in range(TH):
                last = nc.scalar.activation(lat[:, t, 448 * b:448 * (b + 1)], acc[2 * bank + t][:, 0:448],
                                            ACT.Copy, scale=c4[:, t:t + 1])
            last.then_inc(sums_out, 1)
            if b == 1:
                act.wait_ge(r_step, 8)
                nc.scalar.activation(sinn[:, :, 0:32], ang[:, :, 0:32], ACT.Sin, scale=-1.0)
                nc.scalar.activation(sinn[:, :, 32:64], ang[:, :, 32:64], ACT.Sin)
                act.wait_ge(r_step, 12)
                nc.scalar.activation(cosn[:, :, :], ang3[:, :, :], ACT.Sin).then_inc(act_once, 1)
        act.wait_ge(sums_out, B0["olow"] + 2 + 3)
        for m, w in enumerate((slice(0, 768), slice(768, 1280))):
            for t in range(TH):
                at = (0, 768, 1536, 2048)[2 * m + t]
                last = nc.scalar.activation(lat_junk[:, at:at + w.stop - w.start], lat[:, t, w], ACT.Square,
                                            accum_out=stat[:, 56 + 2 * m + t:57 + 2 * m + t])
        last.then_inc(act_once, 1)

        def omem_beside(p):
            if p in (2, 4, 6, 8, 10):
                h = p // 2 - 1
                act.wait_ge(lat_ps, h + 1)
                for c in range(2):
                    last = nc.scalar.activation(lat_t[0][:, 2 * h + c, :], turn[h % 2][:, c * TOK:(c + 1) * TOK],
                                                ACT.Copy, scale=gain[:, 112 + 2 * h + c:113 + 2 * h + c])
                last.then_inc(lat_hi, 1)
            if p == 14:
                act.wait_ge(pe_once, 6)
                nc.scalar.activation(kr_t[:, :], ps_s[0:64, 0:TOK], ACT.Copy).then_inc(act_once, 1)

        for b in range(2):
            splits("omem", 8, 8 * b, 0, 0, lambda k: omem_beside(8 * b + k))
            scaled(At(U0["omem"] + 8 * b + 7), (B0["omem"] + b) % 2, b, 16 * (STORED["omem"] + 1), c4)
        act.wait_ge(lat_r, 2)
        for b in range(6):
            for k in range(3):
                p = 3 * b + k
                for j in range(4):
                    mem_job(1, At(4 + j), p - 7 * j - 5, o_t, 16 + j)
                split(At(U0["uq"] + p + LEAD))
            scaled(At(U0["uq"] + 3 * b + 2), (B0["uq"] + b) % 2, b % 2, 16 * (STORED["uq"] + b // 2 + 1),
                   rstd[:, 16:18])
        for b in range(8):
            for k in range(2):
                p = 2 * b + k
                for j in range(4):
                    mem_job(1, At(4 + j), 18 + p - 7 * j - 5, o_t, 16 + j)
                split(At(U0["ukv"] + p + LEAD))
            scaled(At(U0["ukv"] + 2 * b + 1), (B0["ukv"] + b) % 2, b % 2, 16 * (STORED["ukv"] + b // 2 + 1),
                   rstd[:, 18:20])

        def latent_heads(p):
            for J in range(16):
                s, q = J % 2, p - 2 * J
                if q == 0:
                    act.wait_ge(l_qk_ps, J + 1)
                    nc.scalar.activation(lqk[s][:, :], turn[0][:, :], ACT.Copy).then_inc(l_qk, 1)
                    act.wait_ge(l_qr_ps, J + 1)
                    nc.scalar.activation(lr[s][:, :], turn[1][0:64, 0:TOK], ACT.Copy).then_inc(l_qr, 1)
                if q == 1:
                    act.wait_ge(l_max, J + 1)
                    for x, w in enumerate((slice(0, P), slice(P, H3))):
                        last = nc.scalar.activation(lp[s][:, w], lz[s][:, w], ACT.Exp,
                                                    bias=lsm[:, 8 * s + x:8 * s + x + 1],
                                                    accum_out=lsm[:, 8 * s + 2 + x:8 * s + 3 + x])
                    last.then_inc(l_exp, 1)
            for n in range(4):
                for h in range(2):
                    if p == GATED + 8 * n + 2 * h:
                        act.wait_ge(turned, 2 * (TURN["oy"] + n) + h + 1)
                        w = slice(4 * n + 2 * h, 4 * n + 2 * h + 2)
                        nc.scalar.activation(o_t[0][:, w, :].rearrange("p c t -> p (c t)"), turn[0][:, :],
                                             ACT.Copy).then_inc(turn_hi, 1)

        act.wait_ge(cc, 4)
        for n in range(4):
            b = n % 2
            splits("zc", 8, 8 * n, 0, 0, lambda k: latent_heads(8 * n + k))
            summed(At(U0["zc"] + 8 * n + 7))
            act.wait_ge(tile_moved[b], 16 * (STORED["oout"] + 1))
            if n:
                act.wait_ge(l_zs, n)
            if n >= 2:
                act.wait_ge(l_tile, n - 1)
            bank = (B0["zc"] + n) % 2
            for t in range(TH):
                nc.scalar.activation(tile[b][:, t, :], acc[2 * bank + t][:, :], ACT.Copy, scale=c4[:, t:t + 1])
                last = nc.scalar.activation(zgt[:, t, :], acc[2 * bank + t][:, :], ACT.Tanh,
                                            scale=scal[:, t:t + 1])
            last.then_inc(sums_out, 1)
        for b in range(4):
            splits("oout", 10, 10 * b, 0, 0, lambda k: latent_heads(32 + k) if b == 0 else None)
            act.wait_ge(sums_out, B0["oout"] + b + 3)
            square(res[:, b, :, :], 0, At(b), 28 + b)

    @block.vector
    def _(dve):
        def split(u):
            dve.wait_ge(hi_ready, u.times(1, 1))
            s = u.slot
            nc.vector.tensor_tensor(w_lo[:, s, :], raw[:, s, :], w_hi[:, s, :].bitcast(F32),
                                    ALU.subtract).then_inc(lo_ready, 1)

        def splits(stage, units, first, i, per, hook=None):
            for k in range(units):
                if hook:
                    hook(k)
                split(At(U0[stage] + first + k + LEAD, i, per))

        def summed(u):
            dve.wait_ge(unit_used, u.times(1, 1 + RING))

        def low(n, dst, b, g=None):
            for h in range(2):
                dve.wait_ge(turn_hi, n.times(2, h + 1))
                if g is None:
                    w = bass.ds(b.times(4, 2 * h), 2)
                    last = nc.vector.tensor_tensor(
                        dst[1][:, w, :].rearrange("p c t -> p (c t)"), turn[h][:, :],
                        dst[0][:, w, :].rearrange("p c t -> p (c t)").bitcast(F32), ALU.subtract)
                else:
                    for c in range(2):
                        w = bass.ds(b.times(4, 2 * h + c), 1)
                        last = nc.vector.scalar_tensor_tensor(
                            out=dst[1][:, w, :].rearrange("p c t -> p (c t)"),
                            in0=turn[h][:, c * TOK:(c + 1) * TOK],
                            scalar=gain[:, bass.ds(b.times(4, 2 * h + c + g), 1)],
                            in1=dst[0][:, w, :].rearrange("p c t -> p (c t)").bitcast(F32),
                            op0=ALU.mult, op1=ALU.subtract)
                last.then_inc(turn_lo, 1)

        def mean_squares(r, col, count):
            dve.wait_ge(squared, count)
            nc.vector.tensor_reduce(total[:, 2 * r:2 * r + 2],
                                    stat[:, col:col + 8].rearrange("p (t b) -> p t b", t=TH),
                                    AX.X, ALU.add).then_inc(sum_ready, 1)
            dve.wait_ge(sum_ready, r + 1)

        def norm(r, col, count):
            mean_squares(r, col, count)
            nc.vector.tensor_scalar(mean[:, 2 * r:2 * r + 2], total[:, 2 * r:2 * r + 2], 1.0 / D, EPS,
                                    ALU.mult, ALU.add).then_inc(mean_ready, 1)

        dve.sem_inc(lo_ready, RING)
        dve.sem_inc(sums_out, 2)
        dve.sem_inc(tile_ready, 2)
        dve.sem_inc(turn_lo, 2)
        dve.sem_inc(at_z, 1)
        dve.sem_inc(at_pt, 1)
        dve.sem_inc(at_y_lo, 1)
        dve.sem_inc(ff_half, 1)
        dve.sem_inc(pl_mul, 1)
        dve.sem_inc(m_lo, 1)
        dve.sem_inc(lat_lo, 2)
        dve.sem_inc(l_z, 1)
        dve.sem_inc(l_pt, 2)
        dve.sem_inc(l_y, 1)
        nc.vector.memset(ones[:, :], 1.0).then_inc(ones_ready, 1)
        dve.wait_ge(act_once, 2)
        for u in range(LEAD):
            split(At(u))
        for b in range(4):
            low(At(TURN["mem"] + b), mem_t, At(b), 0)
        norm(0, 0, 4)
        dve.wait_ge(ones_ready, 1)
        rel = tile[1][0:8, 0, 0:N_REL]
        dve.wait_ge(tile_moved[1], 16)
        nc.vector.tensor_copy(e_rows[:, P - 1:P - 1 + N_REL], rel).then_inc(e_built, 1)
        nc.vector.tensor_scalar(e_rows[:, 0:P - 1], ones[0:8, 0:P - 1], rel[:, 0:1], None, ALU.mult)\
            .then_inc(e_built, 1)
        nc.vector.tensor_scalar(e_rows[:, P - 1 + N_REL:H3], ones[0:8, 0:H3 - N_REL - P + 1],
                                rel[:, N_REL - 1:N_REL], None, ALU.mult).then_inc(e_built, 1)
        with dve.Fori(0, 2) as i:
            for b in range(2):
                splits("mem", 8, 8 * b, i, 16)
                low(At(TURN["x"] + b, i, 2), x_t, At(b, i, 2), 16)
        norm(1, 8, 8)
        with dve.Fori(0, 6) as i:
            for b in range(2):
                splits("win", 8, 8 * b, i, 16)

        def attend(p, i):
            for j in range(4):
                J, m, s, kind = At(j, i, 4), At(j // 2, i, 2), j % 2, ("sb", "ca")[j % 2]
                if p == 3 * j + 1:
                    dve.wait_ge(at_scores, J.times(1, 3))
                    if kind == "sb":
                        more = past[:, :]
                    else:
                        more = bias[:, bass.ds(m.times(1), 1), :].rearrange("p h n -> p (h n)")
                    nc.vector.scalar_tensor_tensor(out=z[kind][:, :], in0=ps_s[:, 0:H3], scalar=SCALE,
                                                   in1=more, op0=ALU.mult, op1=ALU.add).then_inc(at_z, 1)
                    if kind == "ca":
                        dve.wait_ge(at_z, J.times(1, 2))
                        for x, w in enumerate((slice(0, P), slice(P, H3))):
                            last = nc.vector.tensor_reduce(sm[:, x:x + 1], z["ca"][:, w], AX.X, ALU.max,
                                                           negate=True)
                        last.then_inc(at_max, 1)
                if p == 3 * j + 2 and kind == "sb":
                    dve.wait_ge(at_keep, m.times(1, 1))
                    nc.vector.scalar_tensor_tensor(out=drop[:, :], in0=z["sb"][:, :], scalar=0.0,
                                                   in1=keep[:, :], op0=ALU.max, op1=ALU.add)\
                        .then_inc(at_drop, 1)
                    dve.wait_ge(at_drop, m.times(1, 1))
                    nc.vector.tensor_tensor_scan(left[:, P - 1::-1], ones[:, 0:P], drop[:, P - 1::-1], 0.0,
                                                 ALU.mult, ALU.add)
                    nc.vector.tensor_tensor_scan(left[:, H3 - 1:P - 1:-1], ones[:, :],
                                                 drop[:, H3 - 1:P - 1:-1], 0.0,
                                                 ALU.mult, ALU.add).then_inc(at_scan, 1)
                    dve.wait_ge(at_scan, m.times(1, 1))
                    nc.vector.tensor_tensor(left[:, :], z["sb"][:, :], left[:, :], ALU.subtract)\
                        .then_inc(at_left, 1)
                if p == 3 * j + 3 and kind == "ca":
                    dve.wait_ge(at_exp, m.times(1, 1))
                    nc.vector.reciprocal(sm[:, 4:6], sm[:, 2:4]).then_inc(at_inv, 1)
                    dve.wait_ge(at_inv, m.times(1, 1))
                    for x, w in enumerate((slice(0, P), slice(P, H3))):
                        last = nc.vector.tensor_scalar(prob["ca"][:, w], prob["ca"][:, w],
                                                       sm[:, 4 + x:5 + x], None, ALU.mult)
                    last.then_inc(at_prob["ca"], 1)
                if p == 3 * j + 5:
                    dve.wait_ge(at_pt_ps, J.times(1, 1))
                    nc.vector.tensor_copy(p_t[s][:, :], turn[1][:, 0:H3]).then_inc(at_pt, 1)
                if p == 3 * j + 6:
                    dve.wait_ge(at_y_hi, J.times(1, 1))
                    w = bass.ds(At(j // 2 + 8 * s, i, 2).times(1), 1)
                    nc.vector.tensor_tensor(
                        y_t[1][:, w, :].rearrange("p c t -> p (c t)"), ps_y[:, 0:TOK],
                        y_t[0][:, w, :].rearrange("p c t -> p (c t)").bitcast(F32),
                        ALU.subtract).then_inc(at_y_lo, 1)

        dve.wait_ge(mask_ready, 4)
        dve.wait_ge(bias_ready, 2)
        with dve.Fori(0, 4) as i:
            for b in range(2):
                splits("win", 8, 96 + 8 * b, i, 16, lambda k: attend(8 * b + k, i))

        for s in range(2):
            dve.wait_ge(tile_moved[s], 16 * (STORED["mix"] + 1))
        for n in range(4):
            for b in range(2):
                splits("out", 4, 8 * n + 4 * b, 0, 0,
                       lambda k: low(At(TURN["mix"] + n - 1), m_t, At(n - 1)) if n and (b, k) == (0, 2) else None)
                if b == 0:
                    dve.wait_ge(gates_sig, n + 1)
                summed(At(U0["out"] + 8 * n + 4 * b + 3))
                for t in range(TH):
                    last = nc.vector.tensor_tensor(part[:, b, t, :], acc[2 * b + t][:, :],
                                                   gates[n % 2][:, b, t, :], ALU.mult)
                last.then_inc(sums_out, 1)
            dve.wait_ge(sums_out, B0["out"] + 2 * n + 1 + 3)
            dve.wait_ge(turned, 2 * (TURN["mix"] + n))
            nc.vector.tensor_tensor(tile[0][:, :, :], part[:, 0, :, :], part[:, 1, :, :], ALU.add)\
                .then_inc(tile_ready, 1)

        dve.wait_ge(act_once, 3)
        nc.vector.tensor_tensor(ple_t[1][:, :, :].rearrange("p c t -> p (c t)"), ps_s[:, :],
                                ple_t[0][:, :, :].rearrange("p c t -> p (c t)").bitcast(F32),
                                ALU.subtract).then_inc(ple_lo, 1)

        def residual(stage, units, turns, dst, g, add, before, norm_of=None):
            for b in range(4):
                def beside(k):
                    if k == TURN_AT:
                        if b == 0:
                            before()
                        else:
                            low(At(turns + b - 1), dst, At(b - 1), g)
                    if norm_of and (b, k) == (0, TURN_AT + 1):
                        norm(*norm_of)
                splits(stage, units, b * units, 0, 0, beside)
                add(b)
            return lambda: low(At(turns + 3), dst, At(3), g)

        def add_to(stage, units):
            def add(b):
                summed(At(U0[stage] + b * units + units - 1))
                dve.wait_ge(xin_landed[b % 2], 16 * (LOADED[stage] + b // 2 + 1))
                dve.wait_ge(tile_moved[b % 2], 16 * (STORED[stage] + b // 2 + 1))
                for t in range(TH):
                    last = nc.vector.tensor_tensor(tile[b % 2][:, t, :], acc[2 * (b % 2) + t][:, :],
                                                   xin[b % 2][:, t, :], ALU.add)
                last.then_inc(sums_out, 1)
            return add

        before = residual("mix", 8, TURN["ffn"], x_t, 32, add_to("mix", 8),
                          lambda: low(At(TURN["mix"] + 3), m_t, At(3)))

        def ffn_pair(n, i, before):
            for b in range(2):
                splits("ffn", 8, 16 * n + 8 * b, i, 16,
                       lambda k: before(k) if b == 0 and k in (TURN_AT, TURN_AT + 1) else None)
                if b == 0:
                    dve.wait_ge(sums_out, written(blk("ffn", 2 * n, i)))
                    nc.vector.tensor_tensor(g_half[:, :, :], g_half[:, :, :], g_sig[:, :, :], ALU.mult)\
                        .then_inc(ff_mul, 1)
            summed(At(U0["ffn"] + 16 * n + 15, i, 16))
            dve.wait_ge(ff_mul, At(n, i, 1).times(1, 1))
            dve.wait_ge(turned, At(TURN["ffo"] + n, i, 1).times(2))
            for t in range(TH):
                last = nc.vector.scalar_tensor_tensor(out=tile[0][:, t, :], in0=acc[2 + t][:, :],
                                                      scalar=rstd[:, 4 + t:5 + t], in1=g_half[:, t, :],
                                                      op0=ALU.mult, op1=ALU.mult)
            last.then_inc(sums_out, 1)

        def first_ffn(k):
            before() if k == TURN_AT else norm(2, 16, 12)

        def next_ffn(n, i):
            low(At(TURN["ffo"] + n, i, 1), ff_t, At(n, i, 1))
            nc.vector.sem_inc(ff_half, 1)

        dve.wait_ge(tile_moved[0], 16 * (STORED["ffo"] + 1))
        ffn_pair(0, 0, first_ffn)
        with dve.Fori(0, 10) as i:
            ffn_pair(1, i, lambda k: next_ffn(0, i) if k == TURN_AT else None)
        before = residual("ffo", 22, TURN["ple"], x_t, 48, add_to("ffo", 22), lambda: next_ffn(10, 0))
        for b in range(4):
            split(At(U0["ple"] + b + LEAD))

        def ple_add(b):
            dve.wait_ge(sums_out, B0["gate"] + b + 3)
            dve.wait_ge(squared, 16 + 2 * b)
            nc.vector.tensor_tensor(x_raw[:, :, :], pl_sig[:, :, :], pl_out[:, b, :, :], ALU.mult)\
                .then_inc(pl_mul, 1)
            if b == 0:
                dve.wait_ge(late_in, 32)
            dve.wait_ge(pl_mul, b + 2)
            dve.wait_ge(xin_landed[b % 2], 16 * (LOADED["gate"] + b // 2 + 1))
            nc.vector.tensor_tensor(x_raw[:, :, :], x_raw[:, :, :], xin[b % 2][:, :, :], ALU.add)\
                .then_inc(pl_sum, 1)
            dve.wait_ge(pl_sum, b + 1)
            dve.wait_ge(tile_moved[b % 2], 16 * (STORED["gate"] + b // 2 + 1))
            for t in range(TH):
                last = nc.vector.tensor_tensor(tile[b % 2][:, t, :], x_raw[:, t, :],
                                               gf_row[:, b * NBW:(b + 1) * NBW], ALU.mult)
            last.then_inc(tile_ready, 1)

        before = residual("gate", 8, TURN["x3"], x3_t, 64, ple_add, before, (3, 24, 16))

        def mem_job(n, J, p, dst, chunk):
            _, qk_, pr_, pt_, y_, th_, sm_ = mbuf[n]
            qkv_ = mqkv[n][J.k % len(mqkv[n])]
            if p == 1:
                dve.wait_ge(m_scores, J.times(1, 1))
                nc.vector.tensor_reduce(sm_[:, 0:2], ps_s[:, :].rearrange("p (t n) -> p t n", t=TH), AX.X,
                                        ALU.max, negate=True).then_inc(m_max, 1)
                dve.wait_ge(m_max, J.times(1, 1))
                nc.vector.tensor_scalar(sm_[:, 0:2], sm_[:, 0:2], SCALE, None, ALU.mult).then_inc(m_max2, 1)
            if p == 3:
                dve.wait_ge(m_exp, J.times(1, 1))
                nc.vector.reciprocal(sm_[:, 4:6], sm_[:, 2:4]).then_inc(m_inv, 1)
                nc.vector.scalar_tensor_tensor(out=qkv_[:, 3, :, :], in0=th_[:, :, :], scalar=1.0,
                                               in1=qkv_[:, 3, :, :], op0=ALU.add, op1=ALU.mult)\
                    .then_inc(m_zs, 1)
            if p == 4:
                dve.wait_ge(m_pt_ps, J.times(1, 1))
                nc.vector.tensor_copy(pt_[:, :], turn[1][:, :]).then_inc(m_pt, 1)
            if p == 5:
                dve.wait_ge(m_y_ps, J.times(1, 1))
                dve.wait_ge(m_inv, J.times(1, 1))
                dve.wait_ge(m_zs, J.times(1, 1))
                for t in range(TH):
                    last = nc.vector.scalar_tensor_tensor(out=y_[:, t, :], in0=ps_y[:, t * P:(t + 1) * P],
                                                          scalar=sm_[:, 4 + t:5 + t], in1=qkv_[:, 3, t, :],
                                                          op0=ALU.mult, op1=ALU.mult)
                last.then_inc(m_y, 1)
            if p == 7:
                dve.wait_ge(m_hi, J.times(1, 1))
                nc.vector.scalar_tensor_tensor(
                    out=dst[1][:, bass.ds(chunk, 1), :].rearrange("p c t -> p (c t)"),
                    in0=ps_y[:, TOK:2 * TOK], scalar=0.5,
                    in1=dst[0][:, bass.ds(chunk, 1), :].rearrange("p c t -> p (c t)").bitcast(F32),
                    op0=ALU.mult, op1=ALU.subtract).then_inc(m_lo, 1)

        r3 = rstd[:, 8:10]

        def first_norm(k):
            if k == TURN_AT:
                before()
            if k == TURN_AT + 1:
                norm(4, 32, 24)
                mean_squares(5, 40, 24)
            if k == TURN_AT + 2:
                dve.wait_ge(rstd_ready, 5)
                nc.vector.tensor_tensor(mean[:, 10:12], total[:, 10:12], r3, ALU.mult).then_inc(cc, 1)
                dve.wait_ge(cc, 1)
                nc.vector.tensor_tensor(mean[:, 10:12], mean[:, 10:12], r3, ALU.mult).then_inc(cc, 1)
                dve.wait_ge(cc, 2)
                nc.vector.tensor_scalar(mean[:, 10:12], mean[:, 10:12], 1.0 / D, EPS, ALU.mult, ALU.add)\
                    .then_inc(mean_ready, 1)
            if k == TURN_AT + 4:
                dve.wait_ge(rstd_ready, 6)
                nc.vector.tensor_tensor(scal[:, :], rstd[:, 10:12], r3, ALU.mult).then_inc(cc, 1)

        dve.wait_ge(small_in, 80)
        splits("ein", 16, 0, 0, 0, first_norm)
        with dve.Fori(0, 4) as i:
            splits("ein", 16, 16, i, 16, lambda k: mem_job(0, At(0, i, 1), k - 4, z_t, At(16, i, 1).times(1)))
        split(At(U0["dt"] + LEAD))

        def time_steps(p):
            if p == 0:
                summed(At(U0["dt"]))
                dve.wait_ge(cc, 3)
                for t in range(TH):
                    w = slice(32 * t, 32 * t + 32)
                    last = nc.vector.scalar_tensor_tensor(out=dtz[:, w], in0=ps_y[:, w], scalar=scal[:, t:t + 1],
                                                          in1=rowb[:, 0:32], op0=ALU.mult, op1=ALU.add)
                last.then_inc(dt_v, 1)
            if p == 2:
                dve.wait_ge(act_once, 7)
                nc.vector.scalar_tensor_tensor(out=dts[:, :], in0=dtz[:, :], scalar=0.0, in1=dts[:, :],
                                               op0=ALU.max, op1=ALU.add).then_inc(dt_v, 1)
                dve.wait_ge(dt_v, 2)
                for t in range(TH):
                    w = slice(32 * t, 32 * t + 32)
                    last = nc.vector.scalar_tensor_tensor(out=d_a[:, w], in0=dts[:, w], scalar=-1.0,
                                                          in1=a_exp[:, :], op0=ALU.mult, op1=ALU.mult)
                last.then_inc(dt_v, 1)
            if p == 3:
                dve.wait_ge(pe_once, 4)
                nc.vector.tensor_copy(acum[:, :], ps_y[:, 64:128]).then_inc(dt_v, 1)
                dve.wait_ge(dt_v, 4)
                nc.vector.tensor_tensor(d_end[:, :], ps_y[:, 128:160], acum[:, 0:32], ALU.subtract)\
                    .then_inc(dt_v, 1)
            if p == 5:
                dve.wait_ge(pe_once, 5)
                nc.vector.tensor_copy(ac_t[:, :], ps_s[0:64, 0:P]).then_inc(dt_v, 1)
                dve.wait_ge(act_once, 9)
            if p == 14:
                decays(At(0))

        def decays(n):
            dve.wait_ge(s_ac, n.times(16, 16))
            for t in range(TH):
                for h in range(HG):
                    d_ = dec[:, t, h * P:(h + 1) * P]
                    last = nc.vector.tensor_scalar(d_, d_, acum[:, bass.ds(n.times(HG, 32 * t + h), 1)],
                                                   0.0, ALU.subtract, ALU.min)
            last.then_inc(s_min, 1)

        splits("ez", 16, 0, 0, 0, time_steps)
        dve.wait_ge(mask_ready, 2)

        def per_head(a, n, width):
            return a.unsqueeze(2).to_broadcast([P, HG, width])

        def ssd(p, i, last_group):
            n = At(0, i, 1)
            if p in (0, 1, 2):
                back = p + 1
                if p == 0:
                    dve.wait_ge(s_tap, n.times(1, 1))
                else:
                    dve.wait_ge(s_conv, n.times(3, p))
                for c in range(6):
                    bank = (turn[0], turn[1], ps_s)[c // 2]
                    u = bank[:, c % 2 * TOK:(c % 2 + 1) * TOK - back]
                    ch = At(c, i, 4) if c < 4 else At(12 + 4 * (c - 3), i, 1)
                    w = col2[:, bass.ds(ch.times(1, 24 + 24 * (3 - back)), 1)]
                    last = nc.vector.scalar_tensor_tensor(out=cv[:, c, back:], in0=u, scalar=w,
                                                          in1=cv[:, c, back:], op0=ALU.mult, op1=ALU.add)
                last.then_inc(s_conv, 1)
            if p == 4:
                dve.wait_ge(s_th, n.times(1, 1))
                c_ = cv[:, :, :].rearrange("p c t -> p (c t)")
                nc.vector.scalar_tensor_tensor(out=c_, in0=th[:, :], scalar=1.0, in1=c_,
                                               op0=ALU.add, op1=ALU.mult).then_inc(s_silu, 1)
            if p == 6:
                dve.wait_ge(s_zth, n.times(1, 1))
                nc.vector.scalar_tensor_tensor(out=zt[:, :, :], in0=zth[:, :, :], scalar=1.0, in1=zt[:, :, :],
                                               op0=ALU.add, op1=ALU.mult).then_inc(s_zs, 1)
            if p == 7:
                dve.wait_ge(s_cb, n.times(1, 1))
                nc.vector.tensor_copy(bm_t[:, :], ps_s[:, 0:P])
                for t in range(TH):
                    last = nc.vector.tensor_tensor(cbm[:, t, :], ps_s[:, (1 + t) * P:(2 + t) * P], tri[:, :],
                                                   ALU.mult)
                last.then_inc(s_cbm, 1)
            if p == 8:
                dve.wait_ge(s_xs, n.times(1, 1))
                for t in range(TH):
                    a = dts[:, bass.ds(At(32 * t, i, HG).times(1), HG)]
                    last = nc.vector.tensor_tensor(xdt[:, t, :].rearrange("p (h d) -> p h d", h=HG),
                                                   xs[:, t, :].rearrange("p (h d) -> p h d", h=HG),
                                                   per_head(a, i, SP_), ALU.mult)
                last.then_inc(s_xdt, 1)
                dve.wait_ge(s_xdt, n.times(1, 1))
                nc.vector.tensor_tensor(xde[:, :].rearrange("p (h d) -> p h d", h=HG),
                                        xdt[:, 0, :].rearrange("p (h d) -> p h d", h=HG),
                                        per_head(d_end[:, bass.ds(n.times(HG), HG)], i, SP_), ALU.mult)\
                    .then_inc(s_xde, 1)
            if p == 9:
                dve.wait_ge(s_dec, n.times(1, 1))
                for t in range(TH):
                    d_ = dec[:, t, :].rearrange("p (h q) -> p h q", h=HG)
                    last = nc.vector.tensor_tensor(d_, d_, cbm[:, t, :].unsqueeze(1).to_broadcast([P, HG, P]),
                                                   ALU.mult)
                last.then_inc(s_m, 1)
                for t in range(TH):
                    x_ = xs[:, t, :].rearrange("p (h d) -> p h d", h=HG)
                    last = nc.vector.tensor_tensor(x_, x_, per_head(rowb[:, bass.ds(n.times(HG, 64), HG)], i, SP_),
                                                   ALU.mult)
                last.then_inc(s_xd, 1)
            if p == 11:
                dve.wait_ge(s_y, n.times(1, 1))
                dve.wait_ge(s_xd, n.times(1, 1))
                for t in range(TH):
                    nc.vector.tensor_tensor(yb[:, t, :], turn[t][:, :], xs[:, t, :], ALU.add)
                nc.vector.tensor_tensor(xdt[:, 1, :].rearrange("p (h d) -> p h d", h=HG),
                                        ps_y[:, :].rearrange("p (h d) -> p h d", h=HG),
                                        per_head(e_ac[:, bass.ds(n.times(HG), HG)], i, SP_), ALU.mult)\
                    .then_inc(s_ya, 1)
                dve.wait_ge(s_ya, n.times(1, 1))
                nc.vector.tensor_tensor(yb[:, 1, :], yb[:, 1, :], xdt[:, 1, :], ALU.add).then_inc(s_yb, 1)
            if p == 12:
                dve.wait_ge(s_zs, n.times(1, 1))
                dve.wait_ge(s_yb, n.times(1, 1))
                nc.vector.scalar_tensor_tensor(out=yb[:, :, :], in0=yb[:, :, :], scalar=0.5, in1=zt[:, :, :],
                                               op0=ALU.mult, op1=ALU.mult).then_inc(s_yg, 1)
            if p == 13:
                dve.wait_ge(s_sq, n.times(1, 1))
                nc.vector.tensor_scalar(g_ms[:, :], g_ss[:, :], 1.0 / NBW, EPS, ALU.mult, ALU.add)\
                    .then_inc(s_gm, 1)
                if not last_group:
                    decays(n + 1)
            if p == 14:
                dve.wait_ge(s_gr, n.times(1, 1))
                for t in range(TH):
                    last = nc.vector.tensor_scalar(yb[:, t, :], yb[:, t, :], g_r[:, t:t + 1], None, ALU.mult)
                last.then_inc(s_tile, 1)

        def sc_pair(i, last_group):
            splits("sc", 16, 0, i, 16, lambda k: ssd(k, i, last_group))
            low(At(TURN["sy"], i, 1), z_t, At(0, i, 1), 96)

        with dve.Fori(0, 3) as i:
            sc_pair(i, False)
        sc_pair(3, True)

        def short(k, j):
            if k == 7 * j + 3:
                dve.wait_ge(c_in, 32 * (j + 1))
                nc.vector.tensor_tensor(sc_in[:, :, 1, :], sc_in[:, :, 1, :], sc_in[:, :, 2, :], ALU.mult)\
                    .then_inc(c_u, 1)
            if k == 7 * j + 5:
                dve.wait_ge(c_th, j + 1)
                nc.vector.scalar_tensor_tensor(out=sc_in[:, :, 3, :], in0=sc_in[:, :, 2, :], scalar=1.0,
                                               in1=sc_in[:, :, 3, :], op0=ALU.add, op1=ALU.mult)\
                    .then_inc(c_zs, 1)
                dve.wait_ge(c_zs, j + 1)
                nc.vector.scalar_tensor_tensor(out=sc_in[:, :, 0, :], in0=sc_in[:, :, 3, :], scalar=0.5,
                                               in1=sc_in[:, :, 0, :], op0=ALU.mult, op1=ALU.mult)\
                    .then_inc(c_w, 1)
            if k == 7 * j + 7:
                dve.wait_ge(c_ut, 2 * j + 2)
                for tap in (2, 1, 0):
                    back = 2 - tap
                    if back:
                        dve.wait_ge(c_conv, 3 * j + back)
                    for c in range(4):
                        u = turn[c // 2][:, c % 2 * TOK:c % 2 * TOK + TOK - back]
                        w = col2[:, 8 * tap + 4 * j + c:8 * tap + 4 * j + c + 1]
                        if back == 0:
                            last = nc.vector.tensor_scalar(sc_cv[:, c, :], u, w, None, ALU.mult)
                        else:
                            last = nc.vector.scalar_tensor_tensor(
                                out=sc_cv[:, c, back:], in0=u, scalar=w, in1=sc_cv[:, c, back:],
                                op0=ALU.mult, op1=ALU.add)
                    last.then_inc(c_conv, 1)
                dve.wait_ge(c_wt, 2 * j + 2)
                dve.wait_ge(c_conv, 3 * j + 3)
                for h in range(2):
                    last = nc.vector.tensor_tensor(
                        sc_y[:, 2 * h * TOK:2 * (h + 1) * TOK], (ps_s, ps_y)[h][:, :],
                        sc_cv[:, 2 * h:2 * h + 2, :].rearrange("p c t -> p (c t)"), ALU.mult)
                last.then_inc(c_y, 1)
            if k == 7 * j + 8:
                dve.wait_ge(c_hi, j + 1)
                w = slice(20 + 4 * j, 24 + 4 * j)
                nc.vector.tensor_tensor(z_t[1][:, w, :].rearrange("p c t -> p (c t)"), sc_y[:, :],
                                        z_t[0][:, w, :].rearrange("p c t -> p (c t)").bitcast(F32),
                                        ALU.subtract).then_inc(c_lo, 1)

        def eout_add(b):
            dve.wait_ge(xin_landed[b % 2], 16 * (LOADED["eout"] + b // 2 + 1))
            dve.wait_ge(tile_moved[b % 2], 16 * (STORED["eout"] + b // 2 + 1))
            bank = (B0["eout"] + b) % 2
            for t in range(TH):
                last = nc.vector.scalar_tensor_tensor(out=tile[b % 2][:, t, :], in0=xin[b % 2][:, t, :],
                                                      scalar=rstd[:, 8 + t:9 + t], in1=acc[2 * bank + t][:, :],
                                                      op0=ALU.mult, op1=ALU.add)
            last.then_inc(sums_out, 1)

        def eout_low(b):
            low(At(TURN["x4"] + b), x_t, At(b), 80)

        for q, (b, k) in enumerate(EOUT_ORDER):
            for j in range(2):
                short(q, j)
            if q == 27:
                eout_low(0)
            split(At(U0["eout"] + q + LEAD))
            if k == 13:
                summed(At(U0["eout"] + q))
                eout_add(b)
        for b in range(2, 4):
            splits("eout", 14, 14 * b, 0, 0, lambda k: eout_low(b - 1) if k == TURN_AT else None)
            summed(At(U0["eout"] + 14 * b + 13))
            eout_add(b)

        def tables(k):
            if k == TURN_AT:
                eout_low(3)
            if k == 5:
                norm(6, 48, 28)
            if k == 0:
                nc.vector.tensor_copy(posf[:, :], posi[:, :]).then_inc(r_step, 1)
                dve.wait_ge(r_step, 1)
                for t in range(TH):
                    for h in range(2):
                        last = nc.vector.tensor_scalar(ang[:, t, 32 * h:32 * h + 32], inv[:, :],
                                                       posf[:, t:t + 1], None, ALU.mult)
                last.then_inc(r_step, 1)
            if k == 1:
                dve.wait_ge(r_step, 2)
                nc.vector.tensor_scalar(ang2[:, :, :], ang[:, :, :], 1.0 / (2.0 * PI), ROUND, ALU.mult, ALU.add)\
                    .then_inc(r_step, 1)
                dve.wait_ge(r_step, 3)
                nc.vector.tensor_scalar(ang2[:, :, :], ang2[:, :, :], ROUND, None, ALU.subtract)\
                    .then_inc(r_step, 1)
            if k == 2:
                for m, part_ in enumerate(TWO_PI):
                    dve.wait_ge(r_step, 4 + m)
                    nc.vector.scalar_tensor_tensor(out=ang[:, :, :], in0=ang2[:, :, :], scalar=-part_,
                                                   in1=ang[:, :, :], op0=ALU.mult, op1=ALU.add)\
                        .then_inc(r_step, 1)
            if k == 3:
                dve.wait_ge(r_step, 7)
                nc.vector.tensor_scalar(ang[:, :, :], ang[:, :, :], PI_IN, -PI_IN, ALU.min, ALU.max)\
                    .then_inc(r_step, 1)
                dve.wait_ge(r_step, 8)
                nc.vector.tensor_scalar(ang3[:, :, :], ang[:, :, :], PI / 2, -2.0 * PI, ALU.is_gt, ALU.mult)\
                    .then_inc(r_step, 1)
            if k == 4:
                dve.wait_ge(r_step, 9)
                nc.vector.scalar_tensor_tensor(out=ang3[:, :, :], in0=ang3[:, :, :], scalar=PI / 2,
                                               in1=ang[:, :, :], op0=ALU.add, op1=ALU.add).then_inc(r_step, 1)
                dve.wait_ge(r_step, 10)
                nc.vector.tensor_scalar(ang3[:, :, :], ang3[:, :, :], PI_IN, -PI_IN, ALU.min, ALU.max)\
                    .then_inc(r_step, 2)

        splits("olow", 24, 0, 0, 0, tables)
        dve.wait_ge(act_once, 10)
        dve.wait_ge(sums_out, B0["olow"] + 2 + 3)
        for h in range(2):
            last = nc.vector.tensor_tensor(ang2[:, :, 32 * h:32 * h + 32],
                                           lat[:, :, 1312 - 32 * h:1344 - 32 * h],
                                           sinn[:, :, 32 * h:32 * h + 32], ALU.mult)
        nc.vector.tensor_tensor(kr[:, :, :], lat[:, :, 1280:1344], cosn[:, :, :], ALU.mult).then_inc(r_step, 1)
        dve.wait_ge(r_step, 13)
        nc.vector.tensor_tensor(kr[:, :, :], kr[:, :, :], ang2[:, :, :], ALU.add).then_inc(r_kr, 1)
        nc.vector.tensor_scalar(scal[:, :], rstd[:, 12:14], 0.5, None, ALU.mult).then_inc(cc, 1)
        dve.wait_ge(act_once, 11)
        for m, width in enumerate((768, 512)):
            nc.vector.tensor_scalar(mean[:, 16 + 2 * m:18 + 2 * m], stat[:, 56 + 2 * m:58 + 2 * m],
                                    1.0 / width, EPS, ALU.mult, ALU.add).then_inc(lat_ms, 1)

        def omem_beside(p):
            if p in (2, 4, 6, 8, 10):
                h = p // 2 - 1
                dve.wait_ge(lat_hi, h + 1)
                for c in range(2):
                    last = nc.vector.scalar_tensor_tensor(
                        out=lat_t[1][:, 2 * h + c, :], in0=turn[h % 2][:, c * TOK:(c + 1) * TOK],
                        scalar=gain[:, 112 + 2 * h + c:113 + 2 * h + c],
                        in1=lat_t[0][:, 2 * h + c, :].bitcast(F32), op0=ALU.mult, op1=ALU.subtract)
                last.then_inc(lat_lo, 1)

        splits("omem", 16, 0, 0, 0, omem_beside)
        for p in range(18):
            for j in range(4):
                mem_job(1, At(4 + j), p - 7 * j - 5, o_t, 16 + j)
            split(At(U0["uq"] + p + LEAD))
        for p in range(16):
            for j in range(4):
                mem_job(1, At(4 + j), 18 + p - 7 * j - 5, o_t, 16 + j)
            split(At(U0["ukv"] + p + LEAD))

        def rotate(J):
            q_ = lq[J % 3]
            dve.wait_ge(at_loaded[J % 3], AT_LOADS + 32 * (J // 3 + 1))
            for h in range(2):
                last = nc.vector.tensor_tensor(rswap[:, :, 32 * h:32 * h + 32],
                                               q_[:, :, P + 32 * (1 - h):P + 32 * (2 - h)],
                                               sinn[:, :, 32 * h:32 * h + 32], ALU.mult)
            last.then_inc(l_rp, 1)
            dve.wait_ge(l_rp, 2 * J + 1)
            nc.vector.tensor_tensor(q_[:, :, P:192], q_[:, :, P:192], cosn[:, :, :], ALU.mult).then_inc(l_rp, 1)
            dve.wait_ge(l_rp, 2 * J + 2)
            nc.vector.tensor_tensor(q_[:, :, P:192], q_[:, :, P:192], rswap[:, :, :], ALU.add).then_inc(l_rot, 1)

        def latent_heads(p):
            for J in range(16):
                s, q = J % 2, p - 2 * J
                sums = lsm[:, 8 * s:8 * s + 8]
                if q == 1:
                    dve.wait_ge(l_scores, J + 1)
                    nc.vector.scalar_tensor_tensor(out=lz[s][:, :], in0=ps_s[:, 0:H3], scalar=L_SCALE,
                                                   in1=causal[:, :], op0=ALU.mult, op1=ALU.add).then_inc(l_z, 1)
                    dve.wait_ge(l_z, J + 2)
                    for x, w in enumerate((slice(0, P), slice(P, H3))):
                        last = nc.vector.tensor_reduce(sums[:, x:x + 1], lz[s][:, w], AX.X, ALU.max, negate=True)
                    last.then_inc(l_max, 1)
                if q == 2:
                    dve.wait_ge(l_exp, J + 1)
                    nc.vector.reciprocal(sums[:, 4:6], sums[:, 2:4]).then_inc(l_inv, 1)
                if q == 3:
                    dve.wait_ge(l_pt_ps, J + 1)
                    nc.vector.tensor_copy(lpt[s][:, :], turn[1][:, 0:H3]).then_inc(l_pt, 1)
                if q == 4:
                    dve.wait_ge(l_y_ps, J + 3)
                    dve.wait_ge(l_inv, J + 1)
                    for t in range(TH):
                        last = nc.vector.tensor_scalar(ybuf[:, t, J * P:(J + 1) * P],
                                                       ps_y[:, t * P:(t + 1) * P], sums[:, 4 + t:5 + t], None,
                                                       ALU.mult)
                    last.then_inc(l_y, 1)
            if p % 2 == 1 and (p + 1) // 2 < 16:
                rotate((p + 1) // 2)
            for n in range(4):
                if p == GATED + 8 * n - 2:
                    dve.wait_ge(l_y, 4 * n + 5)
                    dve.wait_ge(l_zs, n + 1)
                    y_ = ybuf[:, :, n * NBW:(n + 1) * NBW]
                    nc.vector.scalar_tensor_tensor(out=y_, in0=tile[n % 2][:, :, :], scalar=0.5, in1=y_,
                                                   op0=ALU.mult, op1=ALU.mult).then_inc(l_tile, 1)
                for h in range(2):
                    if p == GATED + 8 * n + 2 * h:
                        dve.wait_ge(turn_hi, 2 * (TURN["oy"] + n) + h + 1)
                        w = slice(4 * n + 2 * h, 4 * n + 2 * h + 2)
                        nc.vector.tensor_tensor(o_t[1][:, w, :].rearrange("p c t -> p (c t)"), turn[0][:, :],
                                                o_t[0][:, w, :].rearrange("p c t -> p (c t)").bitcast(F32),
                                                ALU.subtract).then_inc(turn_lo, 1)

        dve.wait_ge(mask_ready, 7)
        rotate(0)
        for n in range(4):
            splits("zc", 8, 8 * n, 0, 0, lambda k: latent_heads(8 * n + k))
            dve.wait_ge(sums_out, B0["zc"] + n + 3)
            nc.vector.scalar_tensor_tensor(out=tile[n % 2][:, :, :], in0=zgt[:, :, :], scalar=1.0,
                                           in1=tile[n % 2][:, :, :], op0=ALU.add, op1=ALU.mult).then_inc(l_zs, 1)
        for b in range(4):
            splits("oout", 10, 10 * b, 0, 0, lambda k: latent_heads(32 + k) if b == 0 else None)
            summed(At(U0["oout"] + 10 * b + 9))
            dve.wait_ge(xin_landed[b % 2], 16 * (LOADED["oout"] + b // 2 + 1))
            bank = (B0["oout"] + b) % 2
            for t in range(TH):
                last = nc.vector.tensor_tensor(res[:, b, t, :], acc[2 * bank + t][:, :], xin[b % 2][:, t, :],
                                               ALU.add)
            last.then_inc(sums_out, 1)
        norm(7, 0, 32)
        dve.wait_ge(rstd_ready, 8)
        dve.wait_ge(late_in, 48)
        for b in range(4):
            for t in range(TH):
                last = nc.vector.scalar_tensor_tensor(out=res[:, b, t, :], in0=res[:, b, t, :],
                                                      scalar=rstd[:, 14 + t:15 + t],
                                                      in1=fin[:, b * NBW:(b + 1) * NBW],
                                                      op0=ALU.mult, op1=ALU.mult)
            last.then_inc(fin_ready, 1)


def tiles_of(w, width=NBW):
    k, n = w.shape
    w = w.reshape(k // (UCH * P), UCH, P, n // width, width).transpose(3, 0, 2, 1, 4)
    return w.reshape(-1, P, UCH * width)


def kernel(**inputs):
    import numpy as np
    import concourse.bacc as bacc
    from concourse.bass_utils import run_bass_kernel_spmd as run
    a = {k: np.asarray(v) for k, v in inputs.items()}
    mem = np.concatenate([a[n] for n in ("mem_k0_2", "mem_v0_2", "mem_k1_2", "mem_v1_2")], axis=1)
    ffn = a["w_ffn_in"][0].reshape(D, 2, 11, NBW).transpose(0, 2, 1, 3).reshape(D, -1)
    sb, ca = (tiles_of(a[n][0]).reshape(4, 4, P, UW) for n in ("w_sb_out", "w_ca_out"))
    w0 = a["w_in0_2"]
    ein = np.concatenate([w0[:, 9248:EVW], w0[:, 6144:9216], w0[:, 4096:6144]], axis=1)
    dt = w0[:, 9216:9248].reshape(16, P, 32).transpose(1, 0, 2).reshape(1, P, -1)
    short = np.concatenate([w0[:, 1024 * m + NBW * j:1024 * m + NBW * (j + 1)]
                            for j in range(2) for m in range(4)], axis=1)
    out0 = tiles_of(np.concatenate([a["w_out0_2"][1024:], a["w_out0_2"][:1024]]))
    first = [14 * b + k for b, k in EOUT_ORDER]
    w1 = a["w_in1_2"]
    out1 = np.concatenate([a["w_out1_2"][D:], a["w_out1_2"][:D]])
    units = [tiles_of(mem), tiles_of(a["w_in"][0]),
             np.stack([sb, ca], axis=1).reshape(-1, P, UW),
             tiles_of(a["w_mix_out"][0]), tiles_of(ffn), tiles_of(a["w_ffn_out"][0]),
             tiles_of(a["w_ple_in"][0]), tiles_of(a["w_ple_gate"][0]),
             tiles_of(ein[:, :10 * NBW]), dt, tiles_of(ein[:, 10 * NBW:]), tiles_of(short), out0[first], out0[28:],
             tiles_of(w1[:, :3 * OLW], OLW), tiles_of(w1[:, 3392:]), tiles_of(a["mla_w_uq_2"]),
             tiles_of(a["mla_w_ukv_2"]), tiles_of(w1[:, 3 * OLW:3392]), tiles_of(out1),
             np.zeros((LEAD, P, UW), np.float32)]
    stream = np.concatenate([np.pad(u, ((0, 0), (0, 0), (0, UW - u.shape[2]))) for u in units])
    gains = np.concatenate([a[n].reshape(-1, P) for n in (
        "mem_norm_w_2", "g_mix", "g_ffn", "g_ple", "norm0_w_2", "norm1_w_2", "ssd_norm_w_2",
        "mla_q_norm_w_2", "mla_kv_norm_w_2")])
    arrays = {
        "stream": stream, "gain_rows": gains, "x": a["x"][0], "mem": a["mem_2"][0], "p": a["p"][0, 0],
        "rel_bias": a["rel_bias"][0], "g_final": a["g_final"], "final_norm": a["final_norm_w_2"],
        "rows2": np.concatenate([a[n].reshape(-1, P) for n in ("sc_conv_w_2", "ssd_conv_w_2")]),
        "rows3": a["ssd_conv_b_2"].reshape(-1, P),
        "rowb": np.concatenate([a[n] for n in ("ssd_dt_bias_2", "ssd_a_log_2", "ssd_d_2")]),
        "inv": (10000.0 ** (-np.arange(32) / 32)).astype(np.float32), "positions": a["positions_2"].reshape(TH, P).T,
    }
    arrays = {k: np.ascontiguousarray(v) for k, v in arrays.items()}
    nc = bacc.Bacc("TRN2", target_bir_lowering=False, num_devices=1)
    io = {k: nc.dram_tensor(k, v.shape, I32 if k == "positions" else F32, kind="ExternalInput").ap()
          for k, v in arrays.items()}
    io["out"] = nc.dram_tensor("out", (TOK, D), F32, kind="ExternalOutput").ap()
    build(nc, io)
    r = run(nc, [arrays], core_ids=[0])
    return r.results[0]["out"].reshape(1, TOK, D)
```
